# Optimizing a Trainium2 kernel written in Bass

```python
import math
import jax, jax.numpy as jnp
from jax import lax
import numpy as np

D_MODEL = 2048
BATCH = 1
SEQ = 512
DEPTH = 1
DEC_BATCH = 8
DEC_SEQ = 8
PAST_LEN = 4096
PAGE_SIZE = 128

D_SSM = D_MODEL // 2
SSM_GROUP_CH = 16
SSM_GROUPS = D_SSM // SSM_GROUP_CH
SSM_STATE = 64
DT_MIN = 1e-3
DT_MAX = 1e-1
D_CONV = D_MODEL // 2
CONV_WIDTH = 3
N_IN = 2 * D_SSM + 4 * D_CONV + 2 * D_MODEL
SPLIT_POINTS = (D_SSM, 2 * D_SSM, 2 * D_SSM + D_CONV, 2 * D_SSM + 2 * D_CONV,
                2 * D_SSM + 3 * D_CONV, 2 * D_SSM + 4 * D_CONV,
                2 * D_SSM + 4 * D_CONV + D_MODEL)
DN_ALPHA = (2 * DEPTH) ** 0.25
DN_BETA = (8 * DEPTH) ** -0.25
LN_EPS = 1e-5

kernel_name = 's5_shortconv_gated_hybrid_step'

def _complex_scan_combine(left, right):
    a1r, a1i, b1r, b1i = left
    a2r, a2i, b2r, b2i = right
    ar = a2r * a1r - a2i * a1i
    ai = a2r * a1i + a2i * a1r
    br = a2r * b1r - a2i * b1i + b2r
    bi = a2r * b1i + a2i * b1r + b2i
    return ar, ai, br, bi

def ssm_branch(u, h0_re, h0_im, a_re, a_im, log_dt, b_re, b_im, c_re, c_im, d, w_glu):
    f32 = jnp.float32
    bt, L, _ = u.shape
    a_re = a_re.astype(f32)
    a_im = a_im.astype(f32)
    dt = jnp.exp(log_dt.astype(f32))[:, None]
    mag = jnp.exp(a_re * dt)
    ang = a_im * dt
    lam_re = mag * jnp.cos(ang)
    lam_im = mag * jnp.sin(ang)
    den = a_re * a_re + a_im * a_im
    q_re = ((lam_re - 1.0) * a_re + lam_im * a_im) / den
    q_im = (lam_im * a_re - (lam_re - 1.0) * a_im) / den
    b_re = b_re.astype(f32)
    b_im = b_im.astype(f32)
    bb_re = q_re[..., None] * b_re - q_im[..., None] * b_im
    bb_im = q_re[..., None] * b_im + q_im[..., None] * b_re
    uf = u.astype(f32)
    ug = uf.reshape(bt, L, SSM_GROUPS, SSM_GROUP_CH)
    bu_re = jnp.einsum('blgc,gpc->blgp', ug, bb_re)
    bu_im = jnp.einsum('blgc,gpc->blgp', ug, bb_im)
    lam_re_t = jnp.broadcast_to(lam_re, (1, L, SSM_GROUPS, SSM_STATE))
    lam_im_t = jnp.broadcast_to(lam_im, (1, L, SSM_GROUPS, SSM_STATE))
    pw_re, pw_im, h_re, h_im = lax.associative_scan(
        _complex_scan_combine, (lam_re_t, lam_im_t, bu_re, bu_im), axis=1)
    if h0_re is not None:
        h0r = h0_re.astype(f32)[:, None]
        h0i = h0_im.astype(f32)[:, None]
        h_re = h_re + pw_re * h0r - pw_im * h0i
        h_im = h_im + pw_re * h0i + pw_im * h0r
    y = (jnp.einsum('blgp,gcp->blgc', h_re, c_re.astype(f32))
         - jnp.einsum('blgp,gcp->blgc', h_im, c_im.astype(f32)))
    y = y.reshape(bt, L, D_SSM) + d.astype(f32) * uf
    y = jax.nn.gelu(y)
    y = y * jax.nn.sigmoid(y @ w_glu.astype(f32))
    return y.astype(u.dtype), h_re[:, -1], h_im[:, -1]

def conv_branch(b_c, c_c, h_c, buf, conv_w):
    q = c_c * h_c
    bt, L, _ = q.shape
    if buf is None:
        buf = jnp.zeros((bt, CONV_WIDTH - 1, D_CONV), q.dtype)
    padded = jnp.concatenate([buf.astype(q.dtype), q], axis=1)
    conv = padded[:, 0:L] * conv_w[0]
    for k in range(1, CONV_WIDTH):
        conv = conv + padded[:, k:k + L] * conv_w[k]
    return b_c * conv, padded[:, -(CONV_WIDTH - 1):]

def hybrid_layer(x, h0_re, h0_im, conv_buf, w_in, a_re, a_im, log_dt, b_re, b_im,
                 c_re, c_im, d, w_glu, w_out_a, conv_w, w_out_c, w_o, ln_g, ln_b):
    proj = jnp.einsum('bld,dn->bln', x, w_in)
    u_a, z_a, b_c, c_c, h_c, z_c, g_a, g_c = jnp.split(proj, SPLIT_POINTS, axis=-1)
    y_a, hr, hi = ssm_branch(u_a, h0_re, h0_im, a_re, a_im, log_dt, b_re, b_im,
                             c_re, c_im, d, w_glu)
    y_a = (y_a * jax.nn.silu(z_a)) @ w_out_a
    y_c, new_buf = conv_branch(b_c, c_c, h_c, conv_buf, conv_w)
    y_c = (y_c * jax.nn.silu(z_c)) @ w_out_c
    merged = jax.nn.sigmoid(g_a) * y_a + jax.nn.sigmoid(g_c) * y_c
    out = merged @ w_o
    r = (DN_ALPHA * x + out).astype(jnp.float32)
    mu = jnp.mean(r, axis=-1, keepdims=True)
    rc = r - mu
    var = jnp.mean(rc * rc, axis=-1, keepdims=True)
    y = rc * lax.rsqrt(var + LN_EPS) * ln_g.astype(jnp.float32) + ln_b.astype(jnp.float32)
    return y.astype(x.dtype), hr, hi, new_buf

def setup_inputs(seed: int = 0) -> dict:
    key = jax.random.key(seed)
    ks = jax.random.split(key, 24)
    f32 = jnp.float32
    nrm = lambda k, shape, s: jax.random.normal(k, shape, f32) * s
    G, P, GC = SSM_GROUPS, SSM_STATE, SSM_GROUP_CH
    x_prompt = nrm(ks[0], (BATCH, SEQ, D_MODEL), 1.0)
    x_sample = nrm(ks[1], (DEC_BATCH, DEC_SEQ, D_MODEL), 1.0)
    state_ssm_re = nrm(ks[2], (DEPTH, DEC_BATCH, G, P), 0.3)
    state_ssm_im = nrm(ks[3], (DEPTH, DEC_BATCH, G, P), 0.3)
    state_conv = nrm(ks[4], (DEPTH, DEC_BATCH, CONV_WIDTH - 1, D_CONV), 1.0)
    w_in = nrm(ks[5], (DEPTH, D_MODEL, N_IN), D_MODEL ** -0.5)
    ssm_a_re = -0.5 + nrm(ks[6], (DEPTH, G, P), 0.01)
    n_idx = jnp.arange(P, dtype=f32) * math.pi
    ssm_a_im = n_idx + nrm(ks[7], (DEPTH, G, P), 0.01)
    ssm_log_dt = jax.random.uniform(ks[8], (DEPTH, G), f32,
                                    math.log(DT_MIN), math.log(DT_MAX))
    ssm_b_re = nrm(ks[9], (DEPTH, G, P, GC), (2 * GC) ** -0.5)
    ssm_b_im = nrm(ks[10], (DEPTH, G, P, GC), (2 * GC) ** -0.5)
    ssm_c_re = nrm(ks[11], (DEPTH, G, GC, P), P ** -0.5)
    ssm_c_im = nrm(ks[12], (DEPTH, G, GC, P), P ** -0.5)
    ssm_d = nrm(ks[13], (DEPTH, D_SSM), 1.0)
    w_glu = nrm(ks[14], (DEPTH, D_SSM, D_SSM), D_SSM ** -0.5)
    w_out_a = nrm(ks[15], (DEPTH, D_SSM, D_MODEL), DN_BETA * D_SSM ** -0.5)
    conv_w = nrm(ks[16], (DEPTH, CONV_WIDTH, D_CONV), CONV_WIDTH ** -0.5)
    w_out_c = nrm(ks[17], (DEPTH, D_CONV, D_MODEL), DN_BETA * D_CONV ** -0.5)
    w_o = nrm(ks[18], (DEPTH, D_MODEL, D_MODEL), DN_BETA * D_MODEL ** -0.5)
    ln_g = 1.0 + nrm(ks[19], (DEPTH, D_MODEL), 0.01)
    ln_b = nrm(ks[20], (DEPTH, D_MODEL), 0.01)
    return {'x_prompt': x_prompt, 'x_sample': x_sample,
            'state_ssm_re': state_ssm_re, 'state_ssm_im': state_ssm_im,
            'state_conv': state_conv, 'w_in': w_in,
            'ssm_a_re': ssm_a_re, 'ssm_a_im': ssm_a_im, 'ssm_log_dt': ssm_log_dt,
            'ssm_b_re': ssm_b_re, 'ssm_b_im': ssm_b_im,
            'ssm_c_re': ssm_c_re, 'ssm_c_im': ssm_c_im, 'ssm_d': ssm_d,
            'w_glu': w_glu, 'w_out_a': w_out_a, 'conv_w': conv_w,
            'w_out_c': w_out_c, 'w_o': w_o, 'ln_g': ln_g, 'ln_b': ln_b}

def reference(x_prompt, x_sample, state_ssm_re, state_ssm_im, state_conv, w_in,
              ssm_a_re, ssm_a_im, ssm_log_dt, ssm_b_re, ssm_b_im, ssm_c_re, ssm_c_im,
              ssm_d, w_glu, w_out_a, conv_w, w_out_c, w_o, ln_g, ln_b):
    xp = x_prompt
    xs = x_sample
    sre_p, sim_p, cnv_p = [], [], []
    sre_s, sim_s, cnv_s = [], [], []
    for l in range(DEPTH):
        params = (w_in[l], ssm_a_re[l], ssm_a_im[l], ssm_log_dt[l], ssm_b_re[l],
                  ssm_b_im[l], ssm_c_re[l], ssm_c_im[l], ssm_d[l], w_glu[l],
                  w_out_a[l], conv_w[l], w_out_c[l], w_o[l], ln_g[l], ln_b[l])
        xp, hr, hi, cb = hybrid_layer(xp, None, None, None, *params)
        sre_p.append(hr)
        sim_p.append(hi)
        cnv_p.append(cb)
        xs, hr, hi, cb = hybrid_layer(xs, state_ssm_re[l], state_ssm_im[l],
                                      state_conv[l], *params)
        sre_s.append(hr)
        sim_s.append(hi)
        cnv_s.append(cb)
    new_ssm_re_prompt = jnp.stack(sre_p, axis=0)
    new_ssm_im_prompt = jnp.stack(sim_p, axis=0)
    new_conv_prompt = jnp.stack(cnv_p, axis=0)
    new_ssm_re_sample = jnp.stack(sre_s, axis=0)
    new_ssm_im_sample = jnp.stack(sim_s, axis=0)
    new_conv_sample = jnp.stack(cnv_s, axis=0)
    return (xp, xs, new_ssm_re_prompt, new_ssm_im_prompt, new_conv_prompt,
            new_ssm_re_sample, new_ssm_im_sample, new_conv_sample)


_drawn_inputs = setup_inputs


def setup_inputs(seed=0):
    import zlib

    import numpy as np

    out = dict(_drawn_inputs(seed))
    spreads = {}
    factors = {'ssm_a_re': 4.312,
     'ssm_c_re': 5.743,
     'ssm_c_im': 5.844,
     'w_glu': 4.853,
     'ln_g': 5.808,
     'ln_b': 5.738}
    for name, (base, spread) in spreads.items():
        noise = np.random.default_rng([zlib.crc32(name.encode()), seed]).standard_normal(out[name].shape)
        drawn = base * np.exp(spread * noise) if base else spread * noise
        out[name] = __import__('jax').numpy.asarray(drawn.astype(out[name].dtype))
    for name, factor in factors.items():
        out[name] = (out[name] * factor).astype(out[name].dtype)
    return out
```

```python
import numpy as np
import concourse.bass as bass
import concourse.mybir as mybir
from concourse.alu_op_type import AluOpType as ALU

F32 = mybir.dt.float32
F32R = mybir.dt.float32r
I32 = mybir.dt.int32
ACT = mybir.ActivationFunctionType

P = 128
D_MODEL = 2048
D_SSM = 1024
D_CONV = 1024
SEQ = 512
DEC_B = 8
DEC_T = 8
TOK = SEQ + DEC_B * DEC_T
TH = TOK // 2
KH = 8
KX = D_MODEL // P
NB = D_SSM // P
PAIRS = 32
STATE = 64
GC = 16
FINE = 16
COARSE = SEQ // FINE
SCAN_ENDS = 1 + DEC_B
ALPHA = float(2.0 ** 0.25)
LN_EPS = 1e-5
GELU_C = 0.044715
GELU_S = 2.0 * float(np.sqrt(2.0 / np.pi))

ROT = 4 * (2 * FINE + 2 * COARSE)
MAG0 = ROT
BB0 = MAG0 + 4
CHIP_W = BB0 + 2 * STATE
C0 = 4 * 2 * 32
H0 = 4 * 2 * DEC_B
HOST_W = C0 + H0 + 1
CONV_W = 3 + 2 * DEC_B
QPAD = SEQ + 2 + DEC_B * (DEC_T + 2)
SETUP = PAIRS + NB * STATE

H_U = 0
H_CONV = H_U + 2 * NB
H_OUTC = H_CONV + 8 * NB
H_GLU = H_OUTC + 3 * KX
H_OUTA = H_GLU + 3 * NB
H_O = H_OUTA + 3 * KX
HALVES = H_O + 2 * KX
S_CONV = NB
S_OUTC = S_CONV + 4 * NB
S_GLU = S_OUTC + 2 * KX
S_OUTA = S_GLU + 2 * NB
S_O = S_OUTA + 2 * KX

MAGIC = 12582912.0
LOG2E = 1.4426950408889634
LN2_HI = 0.693359375
LN2_LO = -2.12194440e-4
TWO_PI = 2.0 * np.pi
PI_A = 6.28125
PI_B = float(np.float32(np.round((TWO_PI - PI_A) * 2.0 ** 20) / 2.0 ** 20))
PI_C = float(TWO_PI - PI_A - PI_B)
PI_LESS = 3.1415925


class Steps:

    def __init__(self, sem, start=0):
        self.sem, self.base, self.k = sem, start, 0

    def at(self, base):
        self.base, self.k = base, 0

    def mark(self, ins):
        ins.then_inc(self.sem, 1)
        self.k += 1

    def value(self):
        return self.base + self.k


def build(nc, d):
    sb = lambda name, shape, dt=F32: nc.alloc_sbuf_tensor(name, shape, dt)
    sem = nc.alloc_semaphore

    xh = sb("xh", [P, KX, TOK], F32R)
    xl = sb("xl", [P, KX, TOK], F32R)
    w_raw = sb("w_raw", [P, 4, KH * P])
    w_hi = [sb(f"w_hi{i}", [P, KH * P], F32R) for i in range(2)]
    w_lo = [sb(f"w_lo{i}", [P, KH * P], F32R) for i in range(2)]
    conv_par = sb("conv_par", [P, NB, CONV_W])
    mask8 = sb("mask8", [P, 8])
    scan_mask = sb("scan_mask", [P, TOK])
    ones = sb("ones", [P, P])
    ln_par = sb("ln_par", [P, KX, 2])
    last_state = sb("last_state", [P, PAIRS, 2, SCAN_ENDS])
    last_conv = sb("last_conv", [P, NB, SCAN_ENDS, 2])

    base = nc.sbuf_base + (-nc.sbuf_base) % 32
    end = nc.sbuf_usable_end

    class Region:

        def __init__(self, at):
            self.at = at

        def __call__(self, name, shape, dt=F32):
            t = nc.alloc_sbuf_tensor_at(name, shape, dt, offset=self.at)
            self.at += -(-4 * int(np.prod(shape[1:])) // 32) * 32
            assert self.at <= end, (name, self.at, end)
            return t

    c0 = base
    c = Region(c0)
    gated_h = c("gated_h", [P, NB, TOK], F32R)
    gated_l = c("gated_l", [P, NB, TOK], F32R)
    d0 = c.at
    x_raw = Region(c0)("x_raw", [P, KX, TOK])
    r_all = Region(c0)("r_all", [P, KX, TOK])

    r = Region(d0)
    par3 = r("par3", [P, 3, SETUP])
    b_par = r("b_par", [P, 2, NB * STATE])
    chip = r("chip", [P, NB, CHIP_W])
    s_dt, s_mag, s_x, s_k, s_f, s_p, s_c, s_s = (r(f"set{i}", [P, SETUP]) for i in range(8))
    s_i = r("s_i", [P, SETUP], I32)
    u_stage_setup = [r(f"u_stage{i}", [P, TOK]) for i in range(2)]

    r = Region(d0)
    table = [r(f"table{i}", [P, 2, TOK]) for i in range(2)]
    bu = [r(f"bu{i}", [P, 2, TOK]) for i in range(2)]
    m1 = r("m1", [P, 2, TOK])
    m2 = r("m2", [P, 2, TOK])
    hst = [r(f"h{i}", [P, 2, TOK]) for i in range(2)]
    rmask = [r(f"rmask{i}", [P, TOK]) for i in range(2)]
    t_tmp = r("t_tmp", [P, SEQ])
    u_blk = r("u_blk", [P, TOK])
    chip_blk = r("chip_blk", [P, CHIP_W])
    host_blk = r("host_blk", [P, HOST_W])
    b_pad = [r(f"b_pad{i}", [P, 2, P]) for i in range(2)]
    y_pre = r("y_pre", [P, TOK])
    y_tmp = r("y_tmp", [P, TOK])
    conv_c = r("conv_c", [P, TOK])
    q_pad = r("q_pad", [P, QPAD])
    conv_t = r("conv_t", [P, TOK])
    gate_t = r("gate_t", [P, TOK])
    cw = r("cw", [P, 3])
    part_st = [r(f"part_st{i}", [P, TOK]) for i in range(2)]

    r = Region(d0)
    yh = r("yh", [P, NB, TOK], F32R)
    yl = r("yl", [P, NB, TOK], F32R)
    y_in = [r(f"y_in{i}", [P, TOK]) for i in range(2)]
    silu_z = r("silu_z", [P, TOK])
    sig_a = r("sig_a", [P, TOK])
    y_f = r("y_f", [P, TOK])

    r = Region(d0)
    merged = r("merged", [P, KX, TOK])
    part_in = [r(f"part_in{i}", [P, TOK]) for i in range(2)]
    sig_m = r("sig_m", [P, TOK])
    x_in = [r(f"x_in{i}", [P, TOK]) for i in range(2)]
    mean = r("mean", [P, TOK])
    rstd = r("rstd", [P, TOK])
    sq = [r(f"sq{i}", [P, TOK]) for i in range(2)]
    o_st = [r(f"o_st{i}", [P, TOK]) for i in range(2)]

    acc = nc.alloc_psum_tensor("acc", [P, 2, 2, 512], F32)
    bu_ps = nc.alloc_psum_tensor("bu_ps", [P, 2, 512], F32)
    y_ps = nc.alloc_psum_tensor("y_ps", [P, 2, 512], F32)

    def halves_of(ps):
        return ps[:, :, 0:TH]

    def two(ap):
        return ap.rearrange("p (t n) -> p t n", t=2)

    u_dram = nc.dram_tensor("u_dram", [NB, P, TOK], F32, kind="Internal").ap()
    y_dram = nc.dram_tensor("y_dram", [NB, P, TOK], F32, kind="Internal").ap()
    part_dram = nc.dram_tensor("part_dram", [KX, P, TOK], F32, kind="Internal").ap()
    chip_dram = nc.dram_tensor("chip_dram", [NB, P, CHIP_W], F32, kind="Internal").ap()

    raw_loaded = [sem(f"raw_loaded{i}") for i in range(4)]
    hi_ready = sem("hi_ready")
    lo_ready = sem("lo_ready")
    half_done = sem("half_done")
    acc_free = [sem(f"acc_free{i}") for i in range(2)]
    x_loaded = [sem(f"x_loaded{i}") for i in range(7)]
    xh_ready = sem("xh_ready")
    xl_ready = sem("xl_ready")
    par_loaded = sem("par_loaded")
    const_loaded = sem("const_loaded")
    dve_step = sem("dve_step")
    sin_in = sem("sin_in")
    sin_out = sem("sin_out")
    chip_ready = sem("chip_ready")
    chip_stored = sem("chip_stored")
    u_evac = sem("u_evac")
    u_stored = [sem(f"u_stored{i}") for i in range(2)]
    blk_loaded = sem("blk_loaded")
    y_read = sem("y_read")
    table_ready = sem("table_ready")
    table_free = sem("table_free")
    rmask_ready = sem("rmask_ready")
    b_pad_ready = sem("b_pad_ready")
    c_ready = sem("c_ready")
    bu_done = sem("bu_done")
    bu_evac = sem("bu_evac")
    prod1_ready = sem("prod1_ready")
    v_ready = sem("v_ready")
    prod2_ready = sem("prod2_ready")
    h_ready = sem("h_ready")
    h_used = sem("h_used")
    h_kept = sem("h_kept")
    y_part = sem("y_part")
    y_sq = sem("y_sq")
    y_arg = sem("y_arg")
    y_sig = sem("y_sig")
    y_made = sem("y_made")
    y_stored = sem("y_stored")
    cc_ready = sem("cc_ready")
    q_read = sem("q_read")
    z_sig = sem("z_sig")
    yc_ready = sem("yc_ready")
    gh_ready = sem("gh_ready")
    gl_ready = sem("gl_ready")
    g_sig = sem("g_sig")
    part_made = sem("part_made")
    part_stored = [sem(f"part_stored{i}") for i in range(2)]
    y_loaded = [sem(f"y_loaded{i}") for i in range(2)]
    yh_ready = sem("yh_ready")
    yl_ready = sem("yl_ready")
    za_sig = sem("za_sig")
    glu_sig = sem("glu_sig")
    ya_ready = sem("ya_ready")
    part_loaded = [sem(f"part_loaded{i}") for i in range(2)]
    merged_ready = sem("merged_ready")
    ga_sig = sem("ga_sig")
    xin_loaded = [sem(f"xin_loaded{i}") for i in range(2)]
    r_ready = sem("r_ready")
    sum_done = sem("sum_done")
    mean_ready = sem("mean_ready")
    rc_ready = sem("rc_ready")
    sq_ready = sem("sq_ready")
    sq_used = sem("sq_used")
    var_ready = sem("var_ready")
    std_ready = sem("std_ready")
    norm_ready = sem("norm_ready")
    out_ready = sem("out_ready")
    out_stored = [sem(f"out_stored{i}") for i in range(2)]
    small_stored = sem("small_stored")
    ones_ready = sem("ones_ready")
    conv_last = sem("conv_last")

    def load_half(sp, h, slot, first=False):
        src = d["w"][h]
        if not first:
            v = sp.snap(h - 3) if not isinstance(h, int) else h - 3
            sp.wait_ge(lo_ready, v)
        sp.dma_start(w_raw[:, slot, :], src).then_inc(raw_loaded[slot], 16)

    block = nc.Block()
    blk = block.__enter__()

    @blk.sync
    def _(sp):
        load_half(sp, 0, 0, True)
        for k in range(4):
            for q in range(4):
                kk = 4 * k + q
                if k == 0:
                    sp.dma_start(x_raw[:, kk, :], d["xT"][kk]).then_inc(x_loaded[q], 16)
            if k:
                sp.dma_start(x_raw[:, 4 * k:4 * k + 4, :],
                             d["xT"][4 * k:4 * k + 4].rearrange("k p n -> p k n")).then_inc(x_loaded[3 + k], 16)
            if k < 3:
                load_half(sp, k + 1, k + 1, True)
        sp.dma_start(par3[:, :, :], d["par3"]).then_inc(par_loaded, 16)
        sp.dma_start(b_par[:, :, :], d["b_par"]).then_inc(par_loaded, 16)
        sp.dma_start(conv_par[:, :, :], d["conv_par"]).then_inc(const_loaded, 16)
        sp.dma_start(mask8[:, :], d["mask8"]).then_inc(const_loaded, 16)
        sp.dma_start(scan_mask[:, :], d["scan_mask"]).then_inc(const_loaded, 16)
        sp.dma_start(ln_par[:, :, :], d["ln_par"]).then_inc(const_loaded, 16)

        with sp.Fori(0, NB // 2) as i:
            for l in range(4):
                load_half(sp, i * 4 + (H_U + l + 4), l)
                if l % 2:
                    s = l // 2
                    dst = u_dram[i * 2 + s]
                    v = sp.snap(i * 2 + (s + 1))
                    sp.wait_ge(u_evac, v)
                    sp.dma_start(dst, u_stage_setup[s][:, :]).then_inc(u_stored[s], 16)
        sp.wait_ge(chip_ready, 1)
        sp.dma_start(chip_dram.rearrange("b p w -> p b w"), chip[:, :, :]).then_inc(chip_stored, 16)
        sp.wait_ge(chip_stored, 16)
        for s in range(2):
            sp.wait_ge(u_stored[s], 16 * NB // 2)

        def load_block(b):
            a = (chip_dram[b], d["host_blk"][b], u_dram[b])
            v = sp.snap(b + 1)
            sp.wait_ge(y_read, v)
            for dst, src in zip((chip_blk[:, :], host_blk[:, :], u_blk[:, :]), a):
                sp.dma_start(dst, src).then_inc(blk_loaded, 16)

        def store_y(b):
            dst = y_dram[b]
            v = sp.snap(b + 1)
            sp.wait_ge(y_made, v)
            sp.dma_start(dst, y_pre[:, :]).then_inc(y_stored, 16)

        with sp.Fori(0, 4) as i:
            load_block(i)
            for l in range(16):
                load_half(sp, i * 16 + (H_CONV + l + 4), l % 4)
            store_y(i)
        with sp.Fori(0, 4) as i:
            load_block(i + 4)
            for l in range(12):
                load_half(sp, i * 12 + (H_OUTC + l + 4), l % 4)
                if l % 3 == 2:
                    m = l // 3
                    dst = part_dram[i * 4 + m]
                    v = sp.snap(i * 4 + (m + 1))
                    sp.wait_ge(part_made, v)
                    sp.dma_start(dst, part_st[m % 2][:, :]).then_inc(part_stored[m % 2], 16)
            store_y(i + 4)
        sp.wait_ge(y_stored, 16 * NB + 16)
        for s in range(2):
            sp.wait_ge(part_stored[s], 16 * KX // 2 + 16)

        for k in range(NB):
            if k >= 2:
                sp.wait_ge(yl_ready, k - 1)
            sp.dma_start(y_in[k % 2][:, :], y_dram[k]).then_inc(y_loaded[k % 2], 16)
        with sp.Fori(0, 2) as i:
            for l in range(12):
                load_half(sp, i * 12 + (H_GLU + l + 4), l % 4)

        sp.wait_ge(gl_ready, 2 * NB)
        for s in range(2):
            sp.dma_start(part_in[s][:, :], part_dram[s]).then_inc(part_loaded[s], 16)

        def phase_outa(i, last):
            for l in range(12):
                load_half(sp, i * 12 + (H_OUTA + l + 4), l % 4)
                if l % 3 == 2:
                    m = l // 3
                    if last and m >= 2:
                        continue
                    src = part_dram[i * 4 + (m + 2)]
                    v = sp.snap(i * 4 + (m + 1)) if not last else i * 4 + m + 1
                    sp.wait_ge(merged_ready, v)
                    sp.dma_start(part_in[m % 2][:, :], src).then_inc(part_loaded[m % 2], 16)
        with sp.Fori(0, 3) as i:
            phase_outa(i, False)
        phase_outa(3, True)

        for s in range(2):
            sp.dma_start(x_in[s][:, :], d["xT"][s]).then_inc(xin_loaded[s], 16)

        def phase_o(i, last):
            for l in range(4):
                if not last:
                    load_half(sp, i * 4 + (H_O + l + 4), l)
                if l % 2 and not last:
                    s = l // 2
                    src = d["xT"][i * 2 + (s + 2)]
                    v = sp.snap(i * 2 + (s + 1))
                    sp.wait_ge(r_ready, v)
                    sp.dma_start(x_in[s][:, :], src).then_inc(xin_loaded[s], 16)
        with sp.Fori(0, KX // 2 - 1) as i:
            phase_o(i, False)
        phase_o(KX // 2 - 1, True)

        sp.wait_ge(h_kept, 2 + PAIRS)
        sp.dma_start(d["out_state"], last_state[:, :, :, :]).then_inc(small_stored, 16)
        sp.wait_ge(conv_last, 2 * NB + 2)
        sp.dma_start(d["out_conv"], last_conv[:, :, :, :]).then_inc(small_stored, 16)
        for n in range(KX):
            sp.wait_ge(out_ready, n + 1)
            sp.dma_start(d["outT"][n], o_st[n % 2][:, :]).then_inc(out_stored[n % 2], 16)
        sp.wait_ge(small_stored, 32)
        for s in range(2):
            sp.wait_ge(out_stored[s], 16 * KX // 2)

    @blk.tensor
    def _(pe):
        def half(h, slot, par, mh, ml, k0, first, last, mid=None, per_block=None):
            pe.wait_ge(lo_ready, h + 1)
            s = slot % 2
            for k in range(KH):
                if k == KH // 2 and mid is not None:
                    mid()
                if per_block is not None:
                    per_block(k0 + k)
                wh = w_hi[s][:, k * P:(k + 1) * P]
                wl = w_lo[s][:, k * P:(k + 1) * P]
                for n, (w, m) in enumerate(((wh, mh), (wh, ml), (wl, mh))):
                    for t in range(2):
                        ins = pe.matmul(acc[:, par, t, 0:TH], w, m[:, k0 + k, t * TH:(t + 1) * TH],
                                        start=first and k == 0 and n == 0,
                                        stop=last and k == KH - 1 and n == 2)
            ins.then_inc(half_done, 1)

        def fresh(par, n):
            if isinstance(n, int) and n == 0:
                return
            pe.wait_ge(acc_free[par], n)

        def x_there(k):
            pe.wait_ge(xl_ready, k + 1)

        def phase_u(i, head):
            for l in range(4):
                par = l // 2
                if l % 2 == 0 and not head:
                    fresh(par, i)
                half(i * 4 + (H_U + l), l, par, xh, xl, (l % 2) * KH, l % 2 == 0, l % 2 == 1,
                     per_block=x_there if head and par == 0 else None)
        phase_u(0, True)
        with pe.Fori(1, NB // 2) as i:
            phase_u(i, False)

        def bu_part(p, j, c):
            if c == 0:
                pe.wait_ge(b_pad_ready, p + 1)
            pe.wait_ge(bu_evac, p * 2 + (c + 1))
            for t in range(2):
                ins = pe.matmul(bu_ps[:, t, 0:TH], b_pad[j % 2][:, c, :], u_blk[:, t * TH:(t + 1) * TH],
                                start=True, stop=True)
            ins.then_inc(bu_done, 1)

        def c_part(p, b, j):
            if j == 0:
                pe.wait_ge(c_ready, b + 1)
                pe.wait_ge(y_read, b + 1)
            pe.wait_ge(h_ready, p * 2 + 5)
            for t in range(2):
                for c in range(2):
                    ins = pe.matmul(y_ps[32 * j:32 * j + 32, t, 0:TH],
                                    host_blk[:, (2 * j + c) * 32:(2 * j + c) * 32 + 32],
                                    hst[j % 2][:, c, t * TH:(t + 1) * TH], start=c == 0, stop=c == 1)
            ins.then_inc(h_used, 1)

        with pe.Fori(0, 4) as b:
            for l in range(16):
                if l in (1, 4, 7, 10):
                    j = (1, 4, 7, 10).index(l)
                    bu_part(b * 4 + j, j, 0)
                    mid = lambda j=j: bu_part(b * 4 + j, j, 1)
                else:
                    mid = None
                if l in (5, 8, 11, 14):
                    j = (5, 8, 11, 14).index(l)
                    c_part(b * 4 + j, b, j)
                par = (l // 2) % 2
                if l % 2 == 0:
                    fresh(par, b * 4 + (S_CONV // 2 + l // 4))
                half(b * 16 + (H_CONV + l), l, par, xh, xl, (l % 2) * KH, l % 2 == 0, l % 2 == 1, mid)

        with pe.Fori(0, 4) as i:
            for l in range(12):
                m, part = l // 3, l % 3
                if l in (1, 3, 5, 7):
                    j = (1, 3, 5, 7).index(l)
                    bu_part(i * 4 + (16 + j), j, 0)
                    mid = lambda j=j: bu_part(i * 4 + (16 + j), j, 1)
                else:
                    mid = None
                if l in (5, 7, 9, 11):
                    j = (5, 7, 9, 11).index(l)
                    c_part(i * 4 + (16 + j), i + 4, j)
                if part != 1:
                    fresh(part // 2, i * 4 + (S_OUTC // 2 + m))
                if part < 2:
                    half(i * 12 + (H_OUTC + l), l, 0, xh, xl, part * KH, part == 0, part == 1, mid)
                else:
                    if m == 0:
                        pe.wait_ge(gl_ready, NB)
                    half(i * 12 + (H_OUTC + l), l, 1, gated_h, gated_l, 0, True, True, mid)

        with pe.Fori(0, 2) as i:
            for l in range(12):
                n, part = l // 3, l % 3
                if part != 1:
                    fresh(part // 2, i * 4 + (S_GLU // 2 + n))
                if part < 2:
                    half(i * 12 + (H_GLU + l), l, 0, xh, xl, part * KH, part == 0, part == 1)
                else:
                    if n == 0:
                        pe.wait_ge(yl_ready, NB)
                    half(i * 12 + (H_GLU + l), l, 1, yh, yl, 0, True, True)

        with pe.Fori(0, 4) as i:
            for l in range(12):
                m, part = l // 3, l % 3
                if part != 1:
                    fresh(part // 2, i * 4 + (S_OUTA // 2 + m))
                if part < 2:
                    half(i * 12 + (H_OUTA + l), l, 0, xh, xl, part * KH, part == 0, part == 1)
                else:
                    if m == 0:
                        pe.wait_ge(gl_ready, 2 * NB)
                    half(i * 12 + (H_OUTA + l), l, 1, gated_h, gated_l, 0, True, True)

        def merged_there(k):
            pe.wait_ge(xl_ready, KX + k + 1)

        def sum_r(n, first, last):
            pe.wait_ge(r_ready, n + 1)
            for t in range(2):
                ins = pe.matmul(bu_ps[:, t, 0:TH], ones[:, :], r_all[:, n, t * TH:(t + 1) * TH],
                                start=first, stop=last)
            return ins

        def phase_o(i, head):
            for l in range(4):
                par = l // 2
                if l % 2 == 0:
                    fresh(par, i + S_O // 2)
                half(i * 4 + (H_O + l), l, par, xh, xl, (l % 2) * KH, l % 2 == 0, l % 2 == 1,
                     per_block=merged_there if head and par == 0 else None)
                if l % 2:
                    if head and par == 0:
                        pe.wait_ge(ones_ready, 1)
                    elif par == 0:
                        sum_r(i * 2 - 1, False, False)
                    else:
                        sum_r(i * 2, head, False)
        phase_o(0, True)
        with pe.Fori(1, KX // 2) as i:
            phase_o(i, False)
        sum_r(KX - 1, False, True).then_inc(sum_done, 1)
        for n in range(KX):
            pe.wait_ge(sq_ready, n + 1)
            for t in range(2):
                ins = pe.matmul(y_ps[:, t, 0:TH], ones[:, :], sq[n % 2][:, t * TH:(t + 1) * TH],
                                start=n == 0, stop=n == KX - 1)
            ins.then_inc(sq_used, 1)

    @blk.scalar
    def _(act):
        act.sem_inc(bu_evac, 1)
        act.sem_inc(h_kept, 2)

        def split(h, slot, n, first=False):
            if first:
                act.wait_ge(raw_loaded[slot], 16)
            else:
                act.wait_ge(raw_loaded[slot], n * 16)
            if not (isinstance(h, int) and h < 2):
                act.wait_ge(half_done, h - 1)
            act.activation(w_hi[slot % 2][:, :], w_raw[:, slot, :], ACT.Copy).then_inc(hi_ready, 1)

        def split_next(i, per, h0, l):
            n = h0 + l + 1
            split(i * per + n, n % 4, i * (per // 4) + (n // 4 + 1))

        def evac_sig(dst, h, par, ready, free=True):
            act.wait_ge(half_done, h + 1)
            ins = act.activation(two(dst), halves_of(acc[:, par]), ACT.Sigmoid)
            ins.then_inc(ready, 1)

        split(0, 0, 1, True)
        for k in range(KX):
            act.wait_ge(x_loaded[k if k < 4 else 3 + k // 4], 16)
            act.activation(xh[:, k, :], x_raw[:, k, :], ACT.Copy).then_inc(xh_ready, 1)

        def phase_u(i, head):
            for l in range(4):
                split_next(i, 4, H_U, l)
                if head and l == 2:
                    act.wait_ge(sin_in, 1)
                    act.activation(s_s[:, :], s_x[:, :], ACT.Sin).then_inc(sin_out, 1)
                    act.activation(s_c[:, :], s_x[:, :], ACT.Sin, scale=0.5).then_inc(sin_out, 1)
                if l % 2:
                    s = l // 2
                    act.wait_ge(half_done, i * 4 + (l + 1))
                    if not head:
                        act.wait_ge(u_stored[s], i * 16)
                    act.activation(two(u_stage_setup[s][:, :]), halves_of(acc[:, s]), ACT.Copy)\
                       .then_inc(u_evac, 1)
                    act.wait_ge(u_evac, i * 2 + (s + 1))
                    act.sem_inc(acc_free[s], 1)
        phase_u(0, True)
        with act.Fori(1, NB // 2) as i:
            phase_u(i, False)
        act.wait_ge(chip_stored, 16)
        for s in range(2):
            act.wait_ge(u_stored[s], 16 * NB // 2)
        act.wait_ge(const_loaded, 64)

        def decay(p, j, b):
            act.wait_ge(table_free, p + 1)
            act.activation(rmask[j % 2][:, :], scan_mask[:, :], ACT.Copy,
                           scale=chip_blk[:, MAG0 + j:MAG0 + j + 1]).then_inc(rmask_ready, 1)

        def evac_bu(p, j, c):
            act.wait_ge(bu_done, p * 2 + (c + 1))
            if c == 0:
                act.wait_ge(h_ready, p * 2 + 1)
            act.activation(two(bu[j % 2][:, c, :]), halves_of(bu_ps), ACT.Copy).then_inc(bu_evac, 1)

        def keep_states(p, j):
            act.wait_ge(h_ready, p * 2 + 5)
            act.activation(last_state[:, p, :, 0:1], hst[j % 2][:, :, SEQ - 1:SEQ], ACT.Copy)
            act.activation(last_state[:, p, :, 1:], hst[j % 2][:, :, SEQ + DEC_T - 1:TOK:DEC_T], ACT.Copy)\
               .then_inc(h_kept, 1)

        def keep_conv(cb):
            act.wait_ge(q_read, cb + 2)
            act.activation(last_conv[:, cb, 0, :], q_pad[:, SEQ:SEQ + 2], ACT.Copy).then_inc(conv_last, 1)
            qs = q_pad[:, SEQ + 2:QPAD].rearrange("p (b t) -> p b t", b=DEC_B)
            act.activation(last_conv[:, cb, 1:, :], qs[:, :, DEC_T:], ACT.Copy).then_inc(conv_last, 1)

        def gelu_act(b):
            act.wait_ge(y_read, b + 2)
            act.activation(y_tmp[:, :], y_pre[:, :], ACT.Square).then_inc(y_sq, 1)
            act.wait_ge(y_arg, b + 1)
            act.activation(y_tmp[:, :], y_tmp[:, :], ACT.Sigmoid, scale=GELU_S).then_inc(y_sig, 1)

        with act.Fori(0, 4) as b:
            for l in range(16):
                split_next(b, 16, H_CONV, l)
                if l in (0, 3, 6, 9):
                    j = (0, 3, 6, 9).index(l)
                    if j == 0:
                        act.wait_ge(blk_loaded, b * 48 + 48)
                    decay(b * 4 + j, j, b)
                if l in (1, 4, 7, 10):
                    j = (1, 4, 7, 10).index(l)
                    for c_ in range(2):
                        evac_bu(b * 4 + j, j, c_)
                if l in (5, 8, 11, 14):
                    j = (5, 8, 11, 14).index(l)
                    keep_states(b * 4 + j, j)
                if l % 8 == 1:
                    act.wait_ge(half_done, b * 16 + (H_CONV + l + 1))
                    act.wait_ge(q_read, b * 2 + (l // 8 + 1))
                    act.activation(two(conv_c[:, :]), halves_of(acc[:, 0]), ACT.Copy).then_inc(cc_ready, 1)
                    act.wait_ge(cc_ready, b * 2 + (l // 8 + 1))
                    act.sem_inc(acc_free[0], 1)
                if l % 8 == 5:
                    keep_conv(b * 2 + l // 8)
                if l % 8 == 7:
                    q = l // 8
                    act.wait_ge(half_done, b * 16 + (H_CONV + l + 1))
                    act.activation(two(gate_t[:, :]), halves_of(acc[:, 1]), ACT.Sigmoid).then_inc(z_sig, 1)
                    act.wait_ge(yc_ready, b * 2 + (q + 1))
                    act.activation(gated_h[:, b * 2 + q, :], conv_t[:, :], ACT.Copy).then_inc(gh_ready, 1)
            gelu_act(b)

        with act.Fori(0, 4) as i:
            for l in range(12):
                m = l // 3
                split_next(i, 12, H_OUTC, l)
                if l in (0, 2, 4, 6):
                    j = (0, 2, 4, 6).index(l)
                    if j == 0:
                        act.wait_ge(blk_loaded, i * 48 + 48 * 5)
                    decay(i * 4 + (16 + j), j, i)
                if l in (1, 3, 5, 7):
                    j = (1, 3, 5, 7).index(l)
                    for c_ in range(2):
                        evac_bu(i * 4 + (16 + j), j, c_)
                if l in (5, 7, 9, 11):
                    j = (5, 7, 9, 11).index(l)
                    keep_states(i * 4 + (16 + j), j)
                if l % 3 == 1:
                    act.wait_ge(half_done, i * 12 + (H_OUTC + l + 1))
                    act.wait_ge(part_made, i * 4 + m) if m else act.wait_ge(gl_ready, NB)
                    if m == 0:
                        act.wait_ge(acc_free[1], i * 4 + S_OUTC // 2)
                    act.activation(two(gate_t[:, :]), halves_of(acc[:, 0]), ACT.Sigmoid).then_inc(g_sig, 1)
                    act.wait_ge(g_sig, i * 4 + (m + 1))
                    act.sem_inc(acc_free[0], 1)
            gelu_act(i + 4)

        for k in range(NB):
            act.wait_ge(y_loaded[k % 2], 16 * (k // 2 + 1))
            act.activation(yh[:, k, :], y_in[k % 2][:, :], ACT.Copy).then_inc(yh_ready, 1)
        with act.Fori(0, 2) as i:
            for l in range(12):
                n = l // 3
                split_next(i, 12, H_GLU, l)
                if l % 3 == 1:
                    act.wait_ge(half_done, i * 12 + (H_GLU + l + 1))
                    act.wait_ge(gl_ready, i * 4 + (NB + n))
                    act.activation(two(silu_z[:, :]), halves_of(acc[:, 0]), ACT.Sigmoid).then_inc(za_sig, 1)
                if l % 3 == 2:
                    act.wait_ge(half_done, i * 12 + (H_GLU + l + 1))
                    act.activation(two(sig_a[:, :]), halves_of(acc[:, 1]), ACT.Sigmoid).then_inc(glu_sig, 1)
                    act.wait_ge(glu_sig, i * 4 + (n + 1))
                    act.sem_inc(acc_free[1], 1)
                    act.wait_ge(ya_ready, i * 4 + (n + 1))
                    act.activation(gated_h[:, i * 4 + n, :], y_f[:, :], ACT.Copy).then_inc(gh_ready, 1)
        act.wait_ge(gl_ready, 2 * NB)
        with act.Fori(0, 4) as i:
            for l in range(12):
                m = l // 3
                split_next(i, 12, H_OUTA, l)
                if l % 3 == 1:
                    act.wait_ge(half_done, i * 12 + (H_OUTA + l + 1))
                    if m:
                        act.wait_ge(merged_ready, i * 4 + m)
                    else:
                        act.wait_ge(acc_free[1], i * 4 + S_OUTA // 2)
                        act.wait_ge(gl_ready, 2 * NB)
                    act.activation(two(sig_m[:, :]), halves_of(acc[:, 0]), ACT.Sigmoid).then_inc(ga_sig, 1)
                    act.wait_ge(ga_sig, i * 4 + (m + 1))
                    act.sem_inc(acc_free[0], 1)
        for k in range(KX):
            act.wait_ge(merged_ready, k + 1)
            act.activation(xh[:, k, :], merged[:, k, :], ACT.Copy).then_inc(xh_ready, 1)
        with act.Fori(0, KX // 2 - 1) as i:
            for l in range(4):
                split_next(i, 4, H_O, l)
        for l in range(3):
            split_next(KX // 2 - 1, 4, H_O, l)

        act.wait_ge(sum_done, 1)
        act.activation(two(mean[:, :]), halves_of(bu_ps), ACT.Copy, scale=1.0 / D_MODEL).then_inc(mean_ready, 1)
        for n in range(KX):
            act.wait_ge(rc_ready, n + 1)
            if n >= 2:
                act.wait_ge(sq_used, n - 1)
            act.activation(sq[n % 2][:, :], r_all[:, n, :], ACT.Square).then_inc(sq_ready, 1)
        act.wait_ge(var_ready, 1)
        act.activation(rstd[:, :], rstd[:, :], ACT.Sqrt).then_inc(std_ready, 1)
        for n in range(KX):
            act.wait_ge(norm_ready, n + 1)
            if n >= 2:
                act.wait_ge(out_stored[n % 2], 16 * (n // 2))
            act.activation(o_st[n % 2][:, :], r_all[:, n, :], ACT.Identity, scale=ln_par[:, n, 0:1],
                           bias=ln_par[:, n, 1:2]).then_inc(out_ready, 1)

    @blk.vector
    def _(dve):
        own = Steps(dve_step)

        def link(ins):
            own.mark(ins)
            dve.wait_ge(dve_step, own.value())

        def mark(ins):
            own.mark(ins)

        def split(h, slot):
            dve.wait_ge(hi_ready, h + 1)
            dve.tensor_tensor(w_lo[slot % 2][:, :], w_raw[:, slot, :], w_hi[slot % 2][:, :].bitcast(F32),
                              ALU.subtract).then_inc(lo_ready, 1)

        def split_next(i, per, h0, l):
            n = h0 + l + 1
            split(i * per + n, n % 4)

        dve.sem_inc(y_read, 1)
        dve.sem_inc(table_free, 2)
        dve.sem_inc(q_read, 1)
        dve.sem_inc(y_stored, 16)
        dve.sem_inc(conv_last, 2)
        for s in range(2):
            dve.sem_inc(part_stored[s], 16)
        split(0, 0)
        for k in range(KX):
            dve.wait_ge(xh_ready, k + 1)
            dve.tensor_tensor(xl[:, k, :], x_raw[:, k, :], xh[:, k, :].bitcast(F32), ALU.subtract)\
               .then_inc(xl_ready, 1)

        A_RE, A_IM, LOG_DT = par3[:, 0, :], par3[:, 1, :], par3[:, 2, :]

        def exp_reduce(x):
            link(dve.tensor_scalar(s_k[:, :], x, LOG2E, None, ALU.mult))
            link(dve.tensor_scalar(s_k[:, :], s_k[:, :], MAGIC, None, ALU.add))
            link(dve.tensor_scalar(s_k[:, :], s_k[:, :], MAGIC, None, ALU.subtract))
            link(dve.scalar_tensor_tensor(s_f[:, :], s_k[:, :], -LN2_HI, x, ALU.mult, ALU.add))
            link(dve.scalar_tensor_tensor(s_f[:, :], s_k[:, :], -LN2_LO, s_f[:, :], ALU.mult, ALU.add))

        def exp_series():
            link(dve.tensor_scalar(s_p[:, :], s_f[:, :], 1.0 / 5040, None, ALU.mult))
            for n in (720, 120, 24, 6, 2, 1):
                link(dve.scalar_tensor_tensor(s_p[:, :], s_p[:, :], 1.0 / n, s_f[:, :], ALU.add, ALU.mult))

        def exp_scale(out):
            link(dve.tensor_scalar(s_k[:, :], s_k[:, :], 127.0, None, ALU.add))
            link(dve.tensor_scalar(s_k[:, :], s_k[:, :], 0.0, 255.0, ALU.max, ALU.min))
            link(dve.tensor_copy(s_i[:, :], s_k[:, :]))
            link(dve.tensor_scalar(s_i[:, :], s_i[:, :], 23, None, ALU.logical_shift_left))
            link(dve.scalar_tensor_tensor(out, s_p[:, :], 1.0, s_i[:, :].bitcast(F32), ALU.add, ALU.mult))

        def angles():
            link(dve.tensor_tensor(s_x[:, :], A_IM, s_dt[:, :], ALU.mult))
            link(dve.tensor_scalar(s_k[:, :], s_x[:, :], 1.0 / TWO_PI, None, ALU.mult))
            link(dve.tensor_scalar(s_k[:, :], s_k[:, :], MAGIC, None, ALU.add))
            link(dve.tensor_scalar(s_k[:, :], s_k[:, :], MAGIC, None, ALU.subtract))
            for part in (PI_A, PI_B, PI_C):
                link(dve.scalar_tensor_tensor(s_x[:, :], s_k[:, :], -part, s_x[:, :], ALU.mult, ALU.add))
            dve.tensor_scalar(s_x[:, :], s_x[:, :], -PI_LESS, PI_LESS, ALU.max, ALU.min).then_inc(sin_in, 1)

        def phase_and_lam():
            dve.wait_ge(sin_out, 2)
            link(dve.tensor_tensor(s_c[:, :], s_c[:, :], s_c[:, :], ALU.mult))
            link(dve.tensor_scalar(s_c[:, :], s_c[:, :], -2.0, 1.0, ALU.mult, ALU.add))
            st = slice(0, PAIRS)
            link(dve.tensor_tensor(s_f[:, st], s_c[:, st], s_c[:, st], ALU.mult))
            link(dve.tensor_tensor(s_p[:, st], s_s[:, st], s_s[:, st], ALU.mult))
            link(dve.tensor_tensor(s_f[:, st], s_f[:, st], s_p[:, st], ALU.add))
            link(dve.tensor_scalar(s_f[:, st], s_f[:, st], -0.5, 1.5, ALU.mult, ALU.add))
            link(dve.tensor_tensor(fine(0, 0, 1), s_c[:, st].rearrange("p (b j) -> p b j", j=4).unsqueeze(3),
                                   s_f[:, st].rearrange("p (b j) -> p b j", j=4).unsqueeze(3), ALU.mult))
            link(dve.tensor_tensor(fine(1, 0, 1), s_s[:, st].rearrange("p (b j) -> p b j", j=4).unsqueeze(3),
                                   s_f[:, st].rearrange("p (b j) -> p b j", j=4).unsqueeze(3), ALU.mult))
            link(dve.tensor_copy(chip[:, :, MAG0:MAG0 + 4],
                                 s_mag[:, st].rearrange("p (b j) -> p b j", j=4)))

        rot = chip[:, :, 0:ROT].rearrange("p b (j w) -> p b j w", j=4)

        def fine(c, a, b):
            return rot[:, :, :, c * FINE + a:c * FINE + b]

        def coarse(c, a, b):
            return rot[:, :, :, 2 * FINE + c * COARSE + a:2 * FINE + c * COARSE + b]

        def tmp(t, n):
            return t[:, 0:PAIRS * n].rearrange("p (b j n) -> p b j n", j=4, n=n)

        def turn(out, a, by, n):
            e = lambda x: x.to_broadcast([P, NB, 4, n])
            link(dve.tensor_tensor(tmp(s_f, n), a[0], e(by[0]), ALU.mult))
            link(dve.tensor_tensor(tmp(s_p, n), a[1], e(by[1]), ALU.mult))
            link(dve.tensor_tensor(tmp(s_x, n), a[0], e(by[1]), ALU.mult))
            link(dve.tensor_tensor(tmp(s_k, n), a[1], e(by[0]), ALU.mult))
            link(dve.tensor_tensor(out[0], tmp(s_f, n), tmp(s_p, n), ALU.subtract))
            link(dve.tensor_tensor(out[1], tmp(s_x, n), tmp(s_k, n), ALU.add))

        def fine_table(n):
            turn([fine(c, n, 2 * n) for c in (0, 1)], [fine(c, 0, n) for c in (0, 1)],
                 [fine(c, n - 1, n) for c in (0, 1)], n)

        def coarse_start():
            link(dve.memset(coarse(0, 0, 1), 1.0))
            link(dve.memset(coarse(1, 0, 1), 0.0))
            for c in range(2):
                link(dve.tensor_copy(coarse(c, 1, 2), fine(c, FINE - 1, FINE)))

        def coarse_table(n):
            turn([coarse(c, n, n + 1) for c in (0, 1)], [coarse(c, n - 1, n) for c in (0, 1)],
                 [coarse(c, 1, 2) for c in (0, 1)], 1)
            turn([coarse(c, n + 1, 2 * n) for c in (0, 1)], [coarse(c, 1, n) for c in (0, 1)],
                 [coarse(c, n, n + 1) for c in (0, 1)], n - 1)

        ch = slice(PAIRS, SETUP)
        a_re, a_im = A_RE[:, ch], A_IM[:, ch]
        q_re, q_im, w0, w1 = s_s[:, ch], s_c[:, ch], s_mag[:, ch], s_dt[:, ch]

        def zoh_q():
            link(dve.tensor_tensor(w1, s_mag[:, ch], s_s[:, ch], ALU.mult))
            link(dve.tensor_tensor(w0, s_mag[:, ch], s_c[:, ch], ALU.mult))
            link(dve.tensor_scalar(w0, w0, 1.0, None, ALU.subtract))
            link(dve.tensor_tensor(s_f[:, ch], a_re, a_re, ALU.mult))
            link(dve.tensor_tensor(s_p[:, ch], a_im, a_im, ALU.mult))
            link(dve.tensor_tensor(s_f[:, ch], s_f[:, ch], s_p[:, ch], ALU.add))
            link(dve.reciprocal(s_f[:, ch], s_f[:, ch]))
            link(dve.tensor_tensor(q_re, w0, a_re, ALU.mult))
            link(dve.tensor_tensor(s_p[:, ch], w1, a_im, ALU.mult))
            link(dve.tensor_tensor(q_re, q_re, s_p[:, ch], ALU.add))
            link(dve.tensor_tensor(q_re, q_re, s_f[:, ch], ALU.mult))
            link(dve.tensor_tensor(q_im, w1, a_re, ALU.mult))
            link(dve.tensor_tensor(s_p[:, ch], w0, a_im, ALU.mult))
            link(dve.tensor_tensor(q_im, q_im, s_p[:, ch], ALU.subtract))
            link(dve.tensor_tensor(q_im, q_im, s_f[:, ch], ALU.mult))

        def zoh_b():
            blocks = lambda x: x.rearrange("p (b s) -> p b s", b=NB)
            for c, (qa, qb, op) in enumerate(((q_re, q_im, ALU.subtract), (q_im, q_re, ALU.add))):
                link(dve.tensor_tensor(w0, qa, b_par[:, 0, :], ALU.mult))
                link(dve.tensor_tensor(w1, qb, b_par[:, 1, :], ALU.mult))
                link(dve.tensor_tensor(chip[:, :, BB0 + c * STATE:BB0 + (c + 1) * STATE],
                                       blocks(w0), blocks(w1), op))

        for h in range(2 * NB):
            split(h + 1, (h + 1) % 4)
            if h == 0:
                dve.wait_ge(par_loaded, 32)
                exp_reduce(LOG_DT)
                exp_series()
                exp_scale(s_dt[:, :])
            if h == 1:
                angles()
            if h == 3:
                dve.wait_ge(sin_out, 2)
                link(dve.tensor_tensor(s_dt[:, :], A_RE, s_dt[:, :], ALU.mult))
                exp_reduce(s_dt[:, :])
            if h == 4:
                exp_series()
                exp_scale(s_mag[:, :])
            if h == 5:
                phase_and_lam()
            if h == 6:
                for n in (1, 2, 4):
                    fine_table(n)
            if h == 7:
                fine_table(8)
                coarse_start()
                turn([coarse(c, 2, 3) for c in (0, 1)], [coarse(c, 1, 2) for c in (0, 1)],
                     [coarse(c, 1, 2) for c in (0, 1)], 1)
                turn([coarse(c, 3, 4) for c in (0, 1)], [coarse(c, 1, 2) for c in (0, 1)],
                     [coarse(c, 2, 3) for c in (0, 1)], 1)
            if h == 8:
                coarse_table(4)
                coarse_table(8)
            if h == 9:
                coarse_table(16)
            if h == 10:
                zoh_q()
            if h == 11:
                zoh_b()
                dve.memset(ones[:, :], 1.0).then_inc(ones_ready, 1)
                dve.sem_inc(chip_ready, 1)
        dve.wait_ge(chip_stored, 16)
        for s in range(2):
            dve.wait_ge(u_stored[s], 16 * NB // 2)
        dve.wait_ge(const_loaded, 64)
        link(dve.memset(q_pad[:, 0:2], 0.0))

        q_prompt = q_pad[:, 0:SEQ + 2]
        q_sample = q_pad[:, SEQ + 2:QPAD].rearrange("p (b t) -> p b t", b=DEC_B)

        def pad_b(p, j):
            if j >= 2:
                dve.wait_ge(bu_done, (p - 1) * 2)
            src = chip_blk[:, BB0:BB0 + 2 * STATE].rearrange("p (c s) -> p c s", c=2)
            for g in range(2):
                ins = dve.tensor_scalar(b_pad[j % 2][:, :, g * STATE:(g + 1) * STATE], src,
                                        mask8[:, 2 * j + g:2 * j + g + 1], None, ALU.mult)
                if g == 0:
                    mark(ins)
            dve.wait_ge(dve_step, own.value())
            ins.then_inc(b_pad_ready, 1)

        def spread(t, n):
            return t.unsqueeze(1).to_broadcast([P, 2, n])

        def to_frame(p, j):
            dve.wait_ge(table_ready, p + 1)
            dve.wait_ge(bu_evac, p * 2 + 3)
            dve.wait_ge(h_ready, p * 2 + 3)
            s = j % 2
            dve.tensor_tensor(m1[:, :, :], bu[s][:, :, :], spread(table[s][:, 0, :], TOK), ALU.mult)\
               .then_inc(prod1_ready, 1)
            dve.tensor_tensor(m2[:, :, :], bu[s][:, :, :], spread(table[s][:, 1, :], TOK), ALU.mult)\
               .then_inc(prod1_ready, 1)

        def scans(p, j):
            s = j % 2
            first = bu[s][:, :, SEQ:TOK:DEC_T]
            h0 = host_blk[:, C0 + j * 2 * DEC_B:C0 + (j + 1) * 2 * DEC_B].rearrange("p (c b) -> p c b", c=2)
            dve.wait_ge(v_ready, p * 2 + 2)
            link(dve.scalar_tensor_tensor(first, h0, chip_blk[:, MAG0 + j:MAG0 + j + 1], first,
                                          ALU.mult, ALU.add))
            dve.wait_ge(rmask_ready, p + 1)
            for c in range(2):
                ins = dve.tensor_tensor_scan(m1[:, c, :], rmask[s][:, :], bu[s][:, c, :], 0.0,
                                             ALU.mult, ALU.add)
                mark(ins)
            dve.wait_ge(dve_step, own.value())
            dve.tensor_tensor(bu[s][:, :, :], m1[:, :, :], spread(table[s][:, 0, :], TOK), ALU.mult)\
               .then_inc(prod2_ready, 1)
            ins = dve.tensor_tensor(m2[:, :, :], m1[:, :, :], spread(table[s][:, 1, :], TOK), ALU.mult)
            ins.then_inc(prod2_ready, 1)
            dve.wait_ge(prod2_ready, p * 2 + 2)
            dve.sem_inc(table_free, 1)

        def negate_c():
            v = host_blk[:, 0:C0].rearrange("p (j c n) -> p j c n", j=4, c=2)[:, :, 1, :]
            return dve.tensor_scalar(v, v, -1.0, None, ALU.mult)

        def read_y(b):
            dve.wait_ge(h_used, b * 4 + 6)
            dve.wait_ge(y_stored, b * 16 + 16)
            own.mark(dve.scalar_tensor_tensor(two(y_pre[:, :]), two(u_blk[:, :]),
                                              host_blk[:, C0 + H0:C0 + H0 + 1], halves_of(y_ps),
                                              ALU.mult, ALU.add))
            dve.wait_ge(dve_step, own.value())
            dve.sem_inc(y_read, 1)

        def gelu(b):
            dve.wait_ge(y_sq, b + 1)
            link(dve.tensor_scalar(y_tmp[:, :], y_tmp[:, :], GELU_C, 1.0, ALU.mult, ALU.add))
            dve.tensor_tensor(y_tmp[:, :], y_tmp[:, :], y_pre[:, :], ALU.mult).then_inc(y_arg, 1)
            dve.wait_ge(y_sig, b + 1)
            dve.tensor_tensor(y_pre[:, :], y_pre[:, :], y_tmp[:, :], ALU.mult).then_inc(y_made, 1)

        def free(par):
            dve.sem_inc(acc_free[par], 1)

        def conv_h(b, q, h):
            dve.wait_ge(conv_last, b * 4 + 2 * q + 2)
            cb = b * 2 + q
            link(dve.tensor_copy(cw[:, :], conv_par[:, cb, 0:3]))
            link(dve.tensor_copy(q_sample[:, :, 0:2],
                                 conv_par[:, cb, 3:3 + 2 * DEC_B].rearrange("p (s t) -> p s t", t=2)))
            dve.wait_ge(cc_ready, b * 2 + (q + 1))
            dve.wait_ge(half_done, h + 1)
            own.mark(dve.tensor_tensor(q_prompt[:, 2:2 + TH], conv_c[:, 0:TH], acc[:, 1, 0, 0:TH], ALU.mult))
            own.mark(dve.tensor_tensor(q_prompt[:, 2 + TH:2 + SEQ], conv_c[:, TH:SEQ],
                                       acc[:, 1, 1, 0:SEQ - TH], ALU.mult))
            own.mark(dve.tensor_tensor(q_sample[:, :, 2:], conv_c[:, SEQ:].rearrange("p (s t) -> p s t", s=DEC_B),
                                       acc[:, 1, 1, SEQ - TH:TH].rearrange("p (s t) -> p s t", s=DEC_B),
                                       ALU.mult))
            dve.wait_ge(dve_step, own.value())
            dve.sem_inc(q_read, 1)
            free(1)
            c_s = conv_t[:, SEQ:].rearrange("p (s t) -> p s t", s=DEC_B)
            for k in range(3):
                pr, sa = q_prompt[:, k:k + SEQ], q_sample[:, :, k:k + DEC_T]
                w = cw[:, k:k + 1]
                if k == 0:
                    own.mark(dve.tensor_scalar(conv_t[:, 0:SEQ], pr, w, None, ALU.mult))
                    link(dve.tensor_scalar(c_s, sa, w, None, ALU.mult))
                else:
                    own.mark(dve.scalar_tensor_tensor(conv_t[:, 0:SEQ], pr, w, conv_t[:, 0:SEQ],
                                                      ALU.mult, ALU.add))
                    link(dve.scalar_tensor_tensor(c_s, sa, w, c_s, ALU.mult, ALU.add))

        def conv_b(h):
            dve.wait_ge(half_done, h + 1)
            link(dve.tensor_tensor(two(conv_t[:, :]), two(conv_t[:, :]), halves_of(acc[:, 0]), ALU.mult))
            free(0)

        def conv_z(b, q, h):
            dve.wait_ge(half_done, h + 1)
            dve.wait_ge(z_sig, b * 2 + (q + 1))
            link(dve.tensor_tensor(two(gate_t[:, :]), two(gate_t[:, :]), halves_of(acc[:, 1]), ALU.mult))
            free(1)
            dve.tensor_tensor(conv_t[:, :], conv_t[:, :], gate_t[:, :], ALU.mult).then_inc(yc_ready, 1)
            dve.wait_ge(gh_ready, b * 2 + (q + 1))
            hi = gated_h[:, b * 2 + q, :]
            lo = gated_l[:, b * 2 + q, :]
            dve.tensor_tensor(lo, conv_t[:, :], hi.bitcast(F32), ALU.subtract).then_inc(gl_ready, 1)

        STEPS_CONV = own.value()
        count = {}

        def conv_body(b):
            for l in range(16):
                split_next(b, 16, H_CONV, l)
                if l == 0:
                    dve.wait_ge(blk_loaded, b * 48 + 48)
                    pad_b(b * 4, 0)
                    negate_c().then_inc(c_ready, 1)
                if l in (3, 6, 9):
                    pad_b(b * 4 + l // 3, l // 3)
                if l in (2, 5, 8, 11):
                    j = (l - 2) // 3
                    to_frame(b * 4 + j, j)
                if l in (3, 6, 9, 12):
                    j = (l - 3) // 3
                    scans(b * 4 + j, j)
                h = b * 16 + (H_CONV + l)
                if l % 8 == 3:
                    conv_h(b, l // 8, h)
                if l % 8 == 5:
                    conv_b(h)
                if l % 8 == 7:
                    conv_z(b, l // 8, h)
            read_y(b)
            gelu(b)

        CONV_STEPS = 44
        with dve.Fori(0, 4) as b:
            own.at(b * CONV_STEPS + STEPS_CONV)
            conv_body(b)
            assert own.k == CONV_STEPS, own.k
        STEPS_OUTC = STEPS_CONV + 4 * CONV_STEPS

        OUTC_STEPS = 18
        with dve.Fori(0, 4) as i:
            own.at(i * OUTC_STEPS + STEPS_OUTC)
            for l in range(12):
                m = l // 3
                split_next(i, 12, H_OUTC, l)
                if l == 0:
                    dve.wait_ge(blk_loaded, i * 48 + 48 * 5)
                    pad_b(i * 4 + 16, 0)
                    negate_c().then_inc(c_ready, 1)
                if l in (2, 4, 6):
                    pad_b(i * 4 + (16 + l // 2), l // 2)
                if l in (2, 4, 6, 8):
                    j = (l - 2) // 2
                    to_frame(i * 4 + (16 + j), j)
                if l in (3, 5, 7, 9):
                    j = (l - 3) // 2
                    scans(i * 4 + (16 + j), j)
                if l % 3 == 2:
                    dve.wait_ge(half_done, i * 12 + (H_OUTC + l + 1))
                    dve.wait_ge(g_sig, i * 4 + (m + 1))
                    dve.wait_ge(part_stored[m % 2], i * 32 + 16 * (m // 2 + 1))
                    dve.tensor_tensor(two(part_st[m % 2][:, :]), two(gate_t[:, :]), halves_of(acc[:, 1]),
                                      ALU.mult).then_inc(part_made, 1)
                    dve.wait_ge(part_made, i * 4 + (m + 1))
                    free(1)
            read_y(i + 4)
            gelu(i + 4)
            assert own.k == OUTC_STEPS, own.k
        own.at(STEPS_OUTC + 4 * OUTC_STEPS)

        for k in range(NB):
            dve.wait_ge(yh_ready, k + 1)
            dve.tensor_tensor(yl[:, k, :], y_in[k % 2][:, :], yh[:, k, :].bitcast(F32), ALU.subtract)\
               .then_inc(yl_ready, 1)
        STEPS_GLU = own.value()
        GLU_STEPS = 12
        with dve.Fori(0, 2) as i:
            own.at(i * GLU_STEPS + STEPS_GLU)
            for l in range(12):
                n = l // 3
                split_next(i, 12, H_GLU, l)
                if l % 3 == 1:
                    dve.wait_ge(za_sig, i * 4 + (n + 1))
                    link(dve.tensor_tensor(two(silu_z[:, :]), two(silu_z[:, :]), halves_of(acc[:, 0]), ALU.mult))
                    free(0)
                    yv = yh[:, i * 4 + n, :].bitcast(F32)
                    lv = yl[:, i * 4 + n, :].bitcast(F32)
                    link(dve.tensor_tensor(y_f[:, :], yv, lv, ALU.add))
                if l % 3 == 2:
                    dve.wait_ge(glu_sig, i * 4 + (n + 1))
                    link(dve.tensor_tensor(y_f[:, :], y_f[:, :], sig_a[:, :], ALU.mult))
                    dve.tensor_tensor(y_f[:, :], y_f[:, :], silu_z[:, :], ALU.mult).then_inc(ya_ready, 1)
                    dve.wait_ge(gh_ready, i * 4 + (NB + n + 1))
                    hi = gated_h[:, i * 4 + n, :].bitcast(F32)
                    dve.tensor_tensor(gated_l[:, i * 4 + n, :], y_f[:, :], hi, ALU.subtract).then_inc(gl_ready, 1)
            assert own.k == GLU_STEPS, own.k

        with dve.Fori(0, 4) as i:
            for l in range(12):
                m = l // 3
                split_next(i, 12, H_OUTA, l)
                if l % 3 == 2:
                    dve.wait_ge(half_done, i * 12 + (H_OUTA + l + 1))
                    dve.wait_ge(ga_sig, i * 4 + (m + 1))
                    own.at(i * 4 + (STEPS_GLU + 2 * GLU_STEPS + m))
                    link(dve.tensor_tensor(two(sig_m[:, :]), two(sig_m[:, :]), halves_of(acc[:, 1]), ALU.mult))
                    free(1)
                    dve.wait_ge(part_loaded[m % 2], i * 32 + 16 * (m // 2 + 1))
                    dve.tensor_tensor(merged[:, i * 4 + m, :], sig_m[:, :], part_in[m % 2][:, :], ALU.add)\
                       .then_inc(merged_ready, 1)
        own.at(STEPS_GLU + 2 * GLU_STEPS + KX)

        for k in range(KX):
            dve.wait_ge(xh_ready, KX + k + 1)
            dve.tensor_tensor(xl[:, k, :], merged[:, k, :], xh[:, k, :].bitcast(F32), ALU.subtract)\
               .then_inc(xl_ready, 1)

        def phase_o(i, last):
            for l in range(4):
                if not (last and l == 3):
                    split_next(i, 4, H_O, l)
                if l % 2:
                    s = l // 2
                    dve.wait_ge(half_done, i * 4 + (H_O + l + 1))
                    dve.wait_ge(xin_loaded[s], i * 16 + 16)
                    dve.scalar_tensor_tensor(two(r_all[:, i * 2 + s, :]), two(x_in[s][:, :]), ALPHA,
                                             halves_of(acc[:, s]), ALU.mult, ALU.add).then_inc(r_ready, 1)
                    dve.wait_ge(r_ready, i * 2 + (s + 1))
                    free(s)
        with dve.Fori(0, KX // 2 - 1) as i:
            phase_o(i, False)
        phase_o(KX // 2 - 1, True)

        dve.wait_ge(mean_ready, 1)
        for n in range(KX):
            dve.tensor_tensor(r_all[:, n, :], r_all[:, n, :], mean[:, :], ALU.subtract).then_inc(rc_ready, 1)
        dve.wait_ge(sq_used, KX)
        link(dve.tensor_scalar(two(rstd[:, :]), halves_of(y_ps), 1.0 / D_MODEL, LN_EPS, ALU.mult, ALU.add))
        dve.sem_inc(var_ready, 1)
        dve.wait_ge(std_ready, 1)
        link(dve.reciprocal(rstd[:, :], rstd[:, :]))
        for n in range(KX):
            dve.tensor_tensor(r_all[:, n, :], r_all[:, n, :], rstd[:, :], ALU.mult).then_inc(norm_ready, 1)

    @blk.gpsimd
    def _(pool):
        pool.sem_inc(h_ready, 3)
        pool.sem_inc(h_used, 2)

        def make_table(p, j):
            pool.wait_ge(table_free, p + 1)
            s = j % 2
            w = 2 * FINE + 2 * COARSE
            f = lambda c: chip_blk[:, j * w + c * FINE:j * w + (c + 1) * FINE]\
                .unsqueeze(1).to_broadcast([P, COARSE, FINE])
            g = lambda c: chip_blk[:, j * w + 2 * FINE + c * COARSE:j * w + 2 * FINE + (c + 1) * COARSE]\
                .unsqueeze(2).to_broadcast([P, COARSE, FINE])
            grid = lambda x: x.rearrange("p (a b) -> p a b", b=FINE)
            for c, (ga, gb, op) in enumerate(((0, 1, ALU.subtract), (1, 0, ALU.add))):
                out = grid(table[s][:, c, 0:SEQ])
                sample = chip_blk[:, j * w + c * FINE:j * w + c * FINE + DEC_T].unsqueeze(1)\
                    .to_broadcast([P, DEC_B, DEC_T])
                pool_step.mark(pool.tensor_tensor(out, g(ga), f(0), ALU.mult))
                pool_step.mark(pool.tensor_tensor(grid(t_tmp[:, :]), g(gb), f(1), ALU.mult))
                pool_step.mark(pool.tensor_copy(
                    table[s][:, c, SEQ:].rearrange("p (b t) -> p b t", b=DEC_B), sample))
                pool.wait_ge(pool_step.sem, pool_step.value())
                ins = pool.tensor_tensor(out, out, grid(t_tmp[:, :]), op)
                if c == 0:
                    pool_step.mark(ins)
                    pool.wait_ge(pool_step.sem, pool_step.value())
            ins.then_inc(table_ready, 1)

        pool_step = Steps(sem("pool_step"))

        def add_frame(p, j):
            s = j % 2
            pool.wait_ge(prod1_ready, p * 2 + 2)
            pool.tensor_tensor(bu[s][:, 0, :], m1[:, 0, :], m2[:, 1, :], ALU.add).then_inc(v_ready, 1)
            pool.tensor_tensor(bu[s][:, 1, :], m1[:, 1, :], m2[:, 0, :], ALU.subtract).then_inc(v_ready, 1)

        def add_back(p, j):
            s = j % 2
            pool.wait_ge(prod2_ready, p * 2 + 2)
            pool.wait_ge(h_used, p + 1)
            pool.wait_ge(h_kept, p + 1)
            pool.tensor_tensor(hst[s][:, 0, :], bu[s][:, 0, :], m2[:, 1, :], ALU.subtract).then_inc(h_ready, 1)
            pool.tensor_tensor(hst[s][:, 1, :], bu[s][:, 1, :], m2[:, 0, :], ALU.add).then_inc(h_ready, 1)

        pool.wait_ge(chip_stored, 16)
        for s in range(2):
            pool.wait_ge(u_stored[s], 16 * NB // 2)

        def block(p0, k0):
            pool_step.at(k0)
            pool.wait_ge(blk_loaded, p0 * 12 + 48)
            make_table(p0, 0)
            for j in range(4):
                add_frame(p0 + j, j)
                if j < 3:
                    make_table(p0 + (j + 1), j + 1)
                add_back(p0 + j, j)
        with pool.Fori(0, 4) as b:
            block(b * 4, b * 28)
        with pool.Fori(0, 4) as b:
            block(b * 4 + 16, b * 28 + 28 * 4)

    block.__exit__(None, None, None)


def kernel(x_prompt, x_sample, state_ssm_re, state_ssm_im, state_conv, w_in, ssm_a_re, ssm_a_im,
           ssm_log_dt, ssm_b_re, ssm_b_im, ssm_c_re, ssm_c_im, ssm_d, w_glu, w_out_a, conv_w, w_out_c,
           w_o, ln_g, ln_b):
    import concourse.bacc as bacc
    from concourse.bass_utils import run_bass_kernel_spmd

    f = lambda a: np.asarray(a)
    tokens = np.concatenate([f(x_prompt)[0], f(x_sample).reshape(DEC_B * DEC_T, D_MODEL)], 0)
    xT = np.ascontiguousarray(tokens.T).reshape(KX, P, TOK)

    def halves(w):
        k, n = w.shape
        v = w.reshape(k // (KH * P), KH, P, n // P, P).transpose(3, 0, 2, 1, 4)
        return v.reshape(n // P, k // (KH * P), P, KH * P)
    wi = halves(f(w_in)[0])
    bounds = np.cumsum([0, NB, NB, NB, NB, NB, NB, KX, KX])
    u_w, z_a, b_c, c_c, h_c, z_c, g_a, g_c = (wi[bounds[i]:bounds[i + 1]] for i in range(8))
    glu, out_a, out_c, w_out = (halves(f(w)[0]) for w in (w_glu, w_out_a, w_out_c, w_o))
    order = [u_w[n] for n in range(NB)]
    for n in range(NB):
        order += [c_c[n], h_c[n], b_c[n], z_c[n]]
    for n in range(KX):
        order += [g_c[n], out_c[n]]
    for n in range(NB):
        order += [z_a[n], glu[n]]
    for n in range(KX):
        order += [g_a[n], out_a[n]]
    order += [w_out[n] for n in range(KX)]
    w = np.concatenate(order, 0)

    def two_layouts(a):
        states = a.reshape(PAIRS, 2 * STATE).T
        channels = np.broadcast_to(a.reshape(NB, 8, 1, STATE), (NB, 8, GC, STATE))
        channels = channels.transpose(1, 2, 0, 3).reshape(P, NB * STATE)
        return np.concatenate([states, channels], 1)
    log_dt = np.broadcast_to(f(ssm_log_dt)[0][:, None], (2 * PAIRS, STATE))
    par3 = np.stack([two_layouts(a) for a in (f(ssm_a_re)[0], f(ssm_a_im)[0], log_dt)], 1)

    def channel_rows(a):
        return a.reshape(NB, 8, STATE, GC).transpose(1, 3, 0, 2).reshape(P, NB * STATE)
    b_par = np.stack([channel_rows(f(ssm_b_re)[0]), channel_rows(f(ssm_b_im)[0])], 1)

    host_blk = np.zeros((NB, P, HOST_W), np.float32)
    cv = host_blk[:, :, 0:C0].reshape(NB, 2, STATE, 4, 2, 2, GC)
    cv = np.zeros((NB, 2, STATE, 4, 2, 2, GC), np.float32)
    for part, src in enumerate((ssm_c_re, ssm_c_im)):
        s = f(src)[0].reshape(NB, 4, 2, GC, STATE)
        for g in range(2):
            cv[:, g, :, :, part, g, :] = s[:, :, g].transpose(0, 3, 1, 2)
    host_blk[:, :, 0:C0] = cv.reshape(NB, P, C0)
    h0 = np.stack([f(state_ssm_re)[0], f(state_ssm_im)[0]], 0)
    h0 = h0.reshape(2, DEC_B, NB, 4, 2, STATE).transpose(2, 4, 5, 3, 0, 1)
    host_blk[:, :, C0:C0 + H0] = h0.reshape(NB, P, H0)
    host_blk[:, :, C0 + H0] = f(ssm_d)[0].reshape(NB, P)

    conv_par = np.concatenate([
        f(conv_w)[0].reshape(3, NB, P).transpose(2, 1, 0),
        f(state_conv)[0].reshape(DEC_B, 2, NB, P).transpose(3, 2, 0, 1).reshape(P, NB, 2 * DEC_B)], 2)
    ln_par = np.stack([f(ln_g)[0].reshape(KX, P).T, f(ln_b)[0].reshape(KX, P).T], 2)
    mask8 = (np.arange(P)[:, None] // GC == np.arange(8)[None]).astype(np.float32)
    starts = np.ones(TOK, np.float32)
    starts[0] = 0
    starts[SEQ::DEC_T] = 0
    scan_mask = np.broadcast_to(starts, (P, TOK))

    arrays = {"w": w, "xT": xT, "par3": par3, "b_par": b_par, "host_blk": host_blk,
              "conv_par": conv_par, "ln_par": ln_par, "mask8": mask8, "scan_mask": scan_mask}
    nc = bacc.Bacc("TRN2", target_bir_lowering=False, num_devices=1, dynamic_dma_scratch_size=1024)
    d, feed = {}, {}
    for name, a in arrays.items():
        a = np.ascontiguousarray(a)
        feed[f"in_{name}"] = a
        d[name] = nc.dram_tensor(f"in_{name}", a.shape, F32, kind="ExternalInput").ap()
    for name, shape in (("outT", [KX, P, TOK]), ("out_state", [P, PAIRS, 2, SCAN_ENDS]),
                        ("out_conv", [P, NB, SCAN_ENDS, 2])):
        d[name] = nc.dram_tensor(name, shape, F32, kind="ExternalOutput").ap()
    build(nc, d)
    res = run_bass_kernel_spmd(nc, [feed], core_ids=[0]).results[0]

    y = np.asarray(res["outT"]).reshape(D_MODEL, TOK).T
    st = np.asarray(res["out_state"]).reshape(2, STATE, PAIRS, 2, SCAN_ENDS)
    st = st.transpose(3, 4, 2, 0, 1).reshape(2, SCAN_ENDS, 2 * PAIRS, STATE)
    cv = np.asarray(res["out_conv"]).transpose(2, 3, 1, 0).reshape(SCAN_ENDS, 2, D_CONV)
    c = np.ascontiguousarray
    return (c(y[:SEQ])[None], c(y[SEQ:]).reshape(DEC_B, DEC_T, D_MODEL),
            c(st[0, :1])[None], c(st[1, :1])[None], c(cv[:1])[None],
            c(st[0, 1:])[None], c(st[1, 1:])[None], c(cv[1:])[None])
```

```python
import numpy as np
import concourse.bass as bass
import concourse.mybir as mybir
from concourse.alu_op_type import AluOpType as ALU

F32 = mybir.dt.float32
F32R = mybir.dt.float32r
I32 = mybir.dt.int32
ACT = mybir.ActivationFunctionType

P = 128
D_MODEL = 2048
D_SSM = 1024
D_CONV = 1024
SEQ = 512
DEC_B = 8
DEC_T = 8
TOK = SEQ + DEC_B * DEC_T
TH = TOK // 2
KH = 8
KX = D_MODEL // P
NB = D_SSM // P
PAIRS = 32
STATE = 64
GC = 16
FINE = 16
COARSE = SEQ // FINE
SCAN_ENDS = 1 + DEC_B
ALPHA = float(2.0 ** 0.25)
LN_EPS = 1e-5
GELU_C = 0.044715
GELU_S = 2.0 * float(np.sqrt(2.0 / np.pi))

ROT_P = 2 * FINE + 2 * COARSE
C0 = 4 * 2 * 32
H0 = 4 * 2 * DEC_B
HOST_W = C0 + H0 + 1
CONV_W = 3 + 2 * DEC_B
QPAD = SEQ + 2 + DEC_B * (DEC_T + 2)
SETUP = PAIRS + NB * STATE

H_U = 0
H_CONV = H_U + 2 * NB
H_OUTC = H_CONV + 8 * NB
H_GLU = H_OUTC + 3 * KX
H_OUTA = H_GLU + 3 * NB
H_O = H_OUTA + 3 * KX
HALVES = H_O + 2 * KX
S_CONV = NB
S_OUTC = S_CONV + 4 * NB
S_GLU = S_OUTC + 2 * KX
S_OUTA = S_GLU + 2 * NB
S_O = S_OUTA + 2 * KX

POOL_BLOCKS = list(range(2, KX - 1, 3))
DVE_BLOCKS = [n for n in range(KX) if n not in POOL_BLOCKS]

MAGIC = 12582912.0
LOG2E = 1.4426950408889634
LN2_HI = 0.693359375
LN2_LO = -2.12194440e-4
TWO_PI = 2.0 * np.pi
PI_A = 6.28125
PI_B = float(np.float32(np.round((TWO_PI - PI_A) * 2.0 ** 20) / 2.0 ** 20))
PI_C = float(TWO_PI - PI_A - PI_B)
PI_LESS = 3.1415925


CONV_BU, CONV_C = (2, 5, 8, 11), (9, 15)
OUTC_BU, OUTC_C = (2, 4, 6, 8), (8, 11)
CONV_KEEP = (5, 8, 11, 14)
OUTC_KEEP = (5, 7, 9, 11)


class Steps:

    def __init__(self, sem, start=0):
        self.sem, self.base, self.k = sem, start, 0

    def at(self, base):
        self.base, self.k = base, 0

    def mark(self, ins):
        ins.then_inc(self.sem, 1)
        self.k += 1

    def value(self):
        return self.base + self.k


def build(nc, d):
    sb = lambda name, shape, dt=F32: nc.alloc_sbuf_tensor(name, shape, dt)
    sem = nc.alloc_semaphore

    xh = sb("xh", [P, KX, TOK], F32R)
    xl = sb("xl", [P, KX, TOK], F32R)
    w_raw = sb("w_raw", [P, 4, KH * P])
    w_hi = [sb(f"w_hi{i}", [P, KH * P], F32R) for i in range(2)]
    w_lo = [sb(f"w_lo{i}", [P, KH * P], F32R) for i in range(2)]
    conv_par = sb("conv_par", [P, NB, CONV_W])
    mask8 = sb("mask8", [P, 8])
    scan_mask = sb("scan_mask", [P, TOK])
    ones = sb("ones", [P, P])
    ln_par = sb("ln_par", [P, KX, 2])
    last_state = sb("last_state", [P, PAIRS, 2, SCAN_ENDS])
    last_conv = sb("last_conv", [P, NB, SCAN_ENDS, 2])

    base = nc.sbuf_base + (-nc.sbuf_base) % 32
    end = nc.sbuf_usable_end

    class Region:

        def __init__(self, at):
            self.at = at

        def __call__(self, name, shape, dt=F32):
            t = nc.alloc_sbuf_tensor_at(name, shape, dt, offset=self.at)
            self.at += -(-4 * int(np.prod(shape[1:])) // 32) * 32
            assert self.at <= end, (name, self.at, end)
            return t

    c0 = base
    c = Region(c0)
    gated_h = c("gated_h", [P, NB, TOK], F32R)
    gated_l = c("gated_l", [P, NB, TOK], F32R)
    d0 = c.at
    x_raw = Region(c0)("x_raw", [P, KX, TOK])
    r_all = Region(c0)("r_all", [P, KX, TOK])

    r = Region(d0)
    rot_all = r("rot_all", [P, PAIRS * ROT_P])
    mag_all = r("mag_all", [P, PAIRS])
    bb_all = r("bb_all", [P, NB, 2 * STATE])
    after_setup = r.at

    par3 = r("par3", [P, 3, SETUP])
    b_par = r("b_par", [P, 2, NB * STATE])
    s_dt, s_mag, s_x, s_k, s_f, s_p, s_c, s_s = (r(f"set{i}", [P, SETUP]) for i in range(8))
    s_i = r("s_i", [P, SETUP], I32)
    u_stage = [r(f"u_stage{i}", [P, TOK]) for i in range(2)]
    setup_end = r.at

    r = Region(after_setup)
    table1 = r("table1", [P, 2, TOK])
    bu = [r(f"bu{i}", [P, 2, TOK]) for i in range(2)]
    m1 = r("m1", [P, 2, TOK])
    m2 = r("m2", [P, 2, TOK])
    hst = [r(f"h{i}", [P, 2, TOK]) for i in range(2)]
    rmask = [r(f"rmask{i}", [P, TOK]) for i in range(2)]
    y_tmp = rmask[1]
    b_pad = [r(f"b_pad{i}", [P, 2, P]) for i in range(2)]
    y_pre = r("y_pre", [P, TOK])
    mag_blk = r("mag_blk", [P, 4])
    cw = r("cw", [P, 3])
    gate_t = r("gate_t", [P, TOK])
    conv_c = gate_t
    part0 = r.at
    conv_t = r("conv_t", [P, TOK])
    q_pad = r("q_pad", [P, QPAD])
    assert r.at >= setup_end
    table = [r("table0", [P, 2, TOK]), table1]
    t_tmp = r("t_tmp", [P, 2, SEQ])
    u_blk = r("u_blk", [P, TOK])
    host_blk = r("host_blk", [P, HOST_W])
    r = Region(part0)
    part_st = [r(f"part_st{i}", [P, TOK]) for i in range(2)]

    r = Region(d0)
    yh = r("yh", [P, NB, TOK], F32R)
    yl = r("yl", [P, NB, TOK], F32R)
    y_in = [r(f"y_in{i}", [P, TOK]) for i in range(2)]
    silu_z = [r(f"silu_z{i}", [P, TOK]) for i in range(4)]
    sig_a = r("sig_a", [P, TOK])
    y_f = r("y_f", [P, TOK])

    r = Region(d0)
    merged = r("merged", [P, KX, TOK])
    part_in = [r(f"part_in{i}", [P, TOK]) for i in range(2)]
    sig_m = r("sig_m", [P, TOK])
    x_in = [r(f"x_in{i}", [P, TOK]) for i in range(2)]
    pivot = r("pivot", [P, TOK])
    acc_d = r("acc_d", [P, TOK])
    acc_q = r("acc_q", [P, TOK])
    sq = [r(f"sq{i}", [P, TOK]) for i in range(2)]
    r = Region(d0)
    mean = r("mean", [P, TOK])
    rstd = r("rstd", [P, TOK])
    mean_r = r("mean_r", [P, TOK])
    o_st = [r(f"o_st{i}", [P, TOK]) for i in range(4)]

    acc = nc.alloc_psum_tensor("acc", [P, 2, 2, 512], F32)
    bu_ps = nc.alloc_psum_tensor("bu_ps", [P, 2, 512], F32)
    y_ps = nc.alloc_psum_tensor("y_ps", [P, 2, 512], F32)

    def halves_of(ps):
        return ps[:, :, 0:TH]

    def two(ap):
        return ap.rearrange("p (t n) -> p t n", t=2)

    u_dram = nc.dram_tensor("u_dram", [NB, P, TOK], F32, kind="Internal").ap()
    y_dram = nc.dram_tensor("y_dram", [NB, P, TOK], F32, kind="Internal").ap()
    part_dram = nc.dram_tensor("part_dram", [KX, P, TOK], F32, kind="Internal").ap()

    raw_loaded = [sem(f"raw_loaded{i}") for i in range(4)]
    hi_ready = sem("hi_ready")
    lo_ready = sem("lo_ready")
    half_done = sem("half_done")
    acc_free = [sem(f"acc_free{i}") for i in range(2)]
    x_loaded = [sem(f"x_loaded{i}") for i in range(7)]
    xh_ready = sem("xh_ready")
    xl_ready = sem("xl_ready")
    par_loaded = sem("par_loaded")
    const_loaded = sem("const_loaded")
    dve_step = sem("dve_step")
    sin_in = sem("sin_in")
    sin_out = sem("sin_out")
    rot_ready = sem("rot_ready")
    u_evac = sem("u_evac")
    u_stored = [sem(f"u_stored{i}") for i in range(2)]
    mag_ready = sem("mag_ready")
    blk_loaded = sem("blk_loaded")
    y_read = sem("y_read")
    table_ready = sem("table_ready")
    table_free = sem("table_free")
    rmask_ready = sem("rmask_ready")
    b_pad_ready = sem("b_pad_ready")
    c_ready = sem("c_ready")
    bu_done = sem("bu_done")
    bu_evac = sem("bu_evac")
    prod1_ready = sem("prod1_ready")
    v_ready = sem("v_ready")
    prod2_ready = sem("prod2_ready")
    h_ready = sem("h_ready")
    h_used = sem("h_used")
    h_kept = sem("h_kept")
    y_part = sem("y_part")
    y_sq = sem("y_sq")
    y_arg = sem("y_arg")
    y_sig = sem("y_sig")
    y_made = sem("y_made")
    y_stored = sem("y_stored")
    cc_ready = sem("cc_ready")
    q_read = sem("q_read")
    z_sig = sem("z_sig")
    yc_ready = sem("yc_ready")
    gh_ready = sem("gh_ready")
    gl_ready = sem("gl_ready")
    g_sig = sem("g_sig")
    part_made = sem("part_made")
    part_stored = [sem(f"part_stored{i}") for i in range(2)]
    y_loaded = [sem(f"y_loaded{i}") for i in range(2)]
    yh_ready = sem("yh_ready")
    yl_ready = sem("yl_ready")
    za_sig = sem("za_sig")
    glu_sig = sem("glu_sig")
    ya_ready = sem("ya_ready")
    part_loaded = [sem(f"part_loaded{i}") for i in range(2)]
    merged_ready = sem("merged_ready")
    ga_sig = sem("ga_sig")
    xin_loaded = [sem(f"xin_loaded{i}") for i in range(2)]
    r_ready = sem("r_ready")
    pivot_sum = sem("pivot_sum")
    pivot_ready = sem("pivot_ready")
    d_ready = sem("d_ready")
    sq_ready = sem("sq_ready")
    sums_ready = sem("sums_ready")
    sums_done = sem("sums_done")
    mean_ready = sem("mean_ready")
    var_ready = sem("var_ready")
    std_ready = sem("std_ready")
    rstd_ready = sem("rstd_ready")
    norm_dve = sem("norm_dve")
    norm_pool = sem("norm_pool")
    out_ready = sem("out_ready")
    out_stored = [sem(f"out_stored{i}") for i in range(4)]
    small_stored = sem("small_stored")
    ones_ready = sem("ones_ready")
    conv_last = sem("conv_last")

    def load_half(sp, h, slot, first=False):
        src = d["w"][h]
        if not first:
            v = sp.snap(h - 3) if not isinstance(h, int) else h - 3
            sp.wait_ge(lo_ready, v)
        sp.dma_start(w_raw[:, slot, :], src).then_inc(raw_loaded[slot], 16)

    block = nc.Block()
    blk = block.__enter__()

    @blk.sync
    def _(sp):
        for k in range(4):
            sp.dma_start(x_raw[:, k, :], d["xT"][k]).then_inc(x_loaded[k], 16)
            if k == 0:
                load_half(sp, 0, 0, True)
        for k in range(1, 4):
            sp.dma_start(x_raw[:, 4 * k:4 * k + 4, :],
                         d["xT"][4 * k:4 * k + 4].rearrange("k p n -> p k n")).then_inc(x_loaded[3 + k], 16)
            load_half(sp, k, k, True)
        sp.dma_start(par3[:, :, :], d["par3"]).then_inc(par_loaded, 16)
        sp.dma_start(b_par[:, :, :], d["b_par"]).then_inc(par_loaded, 16)
        sp.dma_start(conv_par[:, :, :], d["conv_par"]).then_inc(const_loaded, 16)
        sp.dma_start(mask8[:, :], d["mask8"]).then_inc(const_loaded, 16)
        sp.dma_start(scan_mask[:, :], d["scan_mask"]).then_inc(const_loaded, 16)
        sp.dma_start(ln_par[:, :, :], d["ln_par"]).then_inc(const_loaded, 16)

        def phase_u(i, last):
            for l in range(4):
                load_half(sp, i * 4 + (H_U + l + 4), l)
                if l >= 2:
                    s = l - 2
                    dst = u_dram[i * 2 + s]
                    v = sp.snap(i * 2 + (s + 1)) if not last else i * 2 + s + 1
                    sp.wait_ge(u_evac, v)
                    sp.dma_start(dst, u_stage[s][:, :]).then_inc(u_stored[s], 16)
        with sp.Fori(0, NB // 2 - 1) as i:
            phase_u(i, False)

        def load_block(b):
            a = (d["host_blk"][b], u_dram[b])
            v = sp.snap(b + 1) if not isinstance(b, int) else b + 1
            sp.wait_ge(y_read, v)
            for dst, src in zip((host_blk[:, :], u_blk[:, :]), a):
                sp.dma_start(dst, src).then_inc(blk_loaded, 16)

        def store_y(b):
            dst = y_dram[b]
            v = sp.snap(b + 1) if not isinstance(b, int) else b + 1
            sp.wait_ge(y_made, v)
            sp.dma_start(dst, y_pre[:, :]).then_inc(y_stored, 16)

        sp.wait_ge(u_stored[0], 16)
        load_block(0)
        phase_u(NB // 2 - 1, True)
        sp.wait_ge(const_loaded, 64)
        for s in range(2):
            sp.wait_ge(u_stored[s], 16 * NB // 2)
        with sp.Fori(0, 4) as i:
            for l in range(16):
                load_half(sp, i * 16 + (H_CONV + l + 4), l % 4)
            load_block(i + 1)
            store_y(i)

        def phase_outc(i, last):
            for l in range(12):
                load_half(sp, i * 12 + (H_OUTC + l + 4), l % 4)
                if l == 11 and not last:
                    load_block(i + 5)
                if l % 3 == 2:
                    m = l // 3
                    dst = part_dram[i * 4 + m]
                    v = sp.snap(i * 4 + (m + 1)) if not last else i * 4 + m + 1
                    sp.wait_ge(part_made, v)
                    sp.dma_start(dst, part_st[m % 2][:, :]).then_inc(part_stored[m % 2], 16)
            store_y(i + 4)
        with sp.Fori(0, 3) as i:
            phase_outc(i, False)
        phase_outc(3, True)
        sp.wait_ge(y_stored, 16 * NB + 16)
        for s in range(2):
            sp.wait_ge(part_stored[s], 16 * KX // 2 + 16)

        for s in range(2):
            sp.dma_start(y_in[s][:, :], y_dram[s]).then_inc(y_loaded[s], 16)
        for i in range(2):
            for l in range(12):
                load_half(sp, i * 12 + (H_GLU + l + 4), l % 4)
                if i == 0 and l < NB - 2:
                    sp.wait_ge(yl_ready, l + 1)
                    sp.dma_start(y_in[l % 2][:, :], y_dram[l + 2]).then_inc(y_loaded[l % 2], 16)

        sp.wait_ge(gl_ready, 2 * NB)
        for s in range(2):
            sp.dma_start(part_in[s][:, :], part_dram[s]).then_inc(part_loaded[s], 16)

        def phase_outa(i, last):
            for l in range(12):
                load_half(sp, i * 12 + (H_OUTA + l + 4), l % 4)
                if l % 3 == 2:
                    m = l // 3
                    if last and m >= 2:
                        continue
                    src = part_dram[i * 4 + (m + 2)]
                    v = sp.snap(i * 4 + (m + 1)) if not last else i * 4 + m + 1
                    sp.wait_ge(merged_ready, v)
                    sp.dma_start(part_in[m % 2][:, :], src).then_inc(part_loaded[m % 2], 16)
        with sp.Fori(0, 3) as i:
            phase_outa(i, False)
        phase_outa(3, True)

        for s in range(2):
            sp.dma_start(x_in[s][:, :], d["xT"][s]).then_inc(xin_loaded[s], 16)

        def phase_o(i, last):
            for l in range(4):
                if not last:
                    load_half(sp, i * 4 + (H_O + l + 4), l)
                if l >= 2 and not last:
                    s = l - 2
                    src = d["xT"][i * 2 + (s + 2)]
                    v = sp.snap(i * 2 + (s + 1))
                    sp.wait_ge(r_ready, v)
                    sp.dma_start(x_in[s][:, :], src).then_inc(xin_loaded[s], 16)
        with sp.Fori(0, KX // 2 - 1) as i:
            phase_o(i, False)
        phase_o(KX // 2 - 1, True)

        sp.wait_ge(h_kept, 2 + PAIRS)
        sp.dma_start(d["out_state"], last_state[:, :, :, :]).then_inc(small_stored, 16)
        sp.wait_ge(conv_last, 2 * NB + 2)
        sp.dma_start(d["out_conv"], last_conv[:, :, :, :]).then_inc(small_stored, 16)
        for n in range(KX):
            sp.wait_ge(out_ready, n + 1)
            sp.dma_start(d["outT"][n], o_st[n % 4][:, :]).then_inc(out_stored[n % 4], 16)
        sp.wait_ge(small_stored, 32)
        for s in range(4):
            sp.wait_ge(out_stored[s], 16 * KX // 4)

    @blk.tensor
    def _(pe):
        def half(h, slot, par, mh, ml, k0, first, last, mid=None, per_block=None):
            pe.wait_ge(lo_ready, h + 1)
            s = slot % 2
            for k in range(KH):
                if k == KH // 2 and mid is not None:
                    mid()
                if per_block is not None:
                    per_block(k0 + k)
                wh = w_hi[s][:, k * P:(k + 1) * P]
                wl = w_lo[s][:, k * P:(k + 1) * P]
                for n, (w, m) in enumerate(((wh, mh), (wh, ml), (wl, mh))):
                    for t in range(2):
                        ins = pe.matmul(acc[:, par, t, 0:TH], w, m[:, k0 + k, t * TH:(t + 1) * TH],
                                        start=first and k == 0 and n == 0,
                                        stop=last and k == KH - 1 and n == 2)
            ins.then_inc(half_done, 1)

        def fresh(par, n):
            if isinstance(n, int) and n == 0:
                return
            pe.wait_ge(acc_free[par], n)

        def x_there(k):
            pe.wait_ge(xl_ready, k + 1)

        def phase_u(i, head):
            for l in range(4):
                if l < 2 and not head:
                    fresh(l, i)
                half(i * 4 + (H_U + l), l, l % 2, xh, xl, (l // 2) * KH, l < 2, l >= 2,
                     per_block=x_there if head and l % 2 == 0 else None)
        phase_u(0, True)
        with pe.Fori(1, NB // 2) as i:
            phase_u(i, False)

        def bu_part(p, j, c):
            if c == 0:
                pe.wait_ge(b_pad_ready, p + 1)
            pe.wait_ge(bu_evac, p * 2 + (c + 1))
            for t in range(2):
                ins = pe.matmul(bu_ps[:, t, 0:TH], b_pad[j % 2][:, c, :], u_blk[:, t * TH:(t + 1) * TH],
                                start=True, stop=True)
            ins.then_inc(bu_done, 1)

        def c_part(p, b, j):
            if j == 0:
                pe.wait_ge(c_ready, b + 1)
                pe.wait_ge(y_read, b + 1)
            pe.wait_ge(h_ready, p * 2 + 7)
            for t in range(2):
                for c in range(2):
                    for jj in (j, j + 1):
                        ins = pe.matmul(y_ps[32 * jj:32 * jj + 32, t, 0:TH],
                                        host_blk[:, (2 * jj + c) * 32:(2 * jj + c) * 32 + 32],
                                        hst[jj % 2][:, c, t * TH:(t + 1) * TH], start=c == 0, stop=c == 1)
                        if t == 1 and c == 1:
                            ins.then_inc(h_used, 1)

        with pe.Fori(0, 4) as b:
            for l in range(16):
                if l in CONV_BU:
                    j = CONV_BU.index(l)
                    bu_part(b * 4 + j, j, 0)
                    mid = lambda j=j: bu_part(b * 4 + j, j, 1)
                else:
                    mid = None
                if l in CONV_C:
                    j = 2 * CONV_C.index(l)
                    c_part(b * 4 + j, b, j)
                par = (l // 2) % 2
                if l % 2 == 0:
                    fresh(par, b * 4 + (S_CONV // 2 + l // 4))
                half(b * 16 + (H_CONV + l), l, par, xh, xl, (l % 2) * KH, l % 2 == 0, l % 2 == 1, mid)

        with pe.Fori(0, 4) as i:
            for l in range(12):
                m, part = l // 3, l % 3
                if l in OUTC_BU:
                    j = OUTC_BU.index(l)
                    bu_part(i * 4 + (16 + j), j, 0)
                    mid = lambda j=j: bu_part(i * 4 + (16 + j), j, 1)
                else:
                    mid = None
                if l in OUTC_C:
                    j = 2 * OUTC_C.index(l)
                    c_part(i * 4 + (16 + j), i + 4, j)
                if part != 1:
                    fresh(part // 2, i * 4 + (S_OUTC // 2 + m))
                if part < 2:
                    half(i * 12 + (H_OUTC + l), l, 0, xh, xl, part * KH, part == 0, part == 1, mid)
                else:
                    if m == 0:
                        pe.wait_ge(gl_ready, NB)
                    half(i * 12 + (H_OUTC + l), l, 1, gated_h, gated_l, 0, True, True, mid)

        with pe.Fori(0, 2) as i:
            for l in range(12):
                h = i * 12 + (H_GLU + l)
                if l < 8:
                    n = l // 2
                    if l % 2 == 0:
                        fresh(n % 2, i * 4 + (S_GLU // 2 + n // 2))
                    half(h, l, n % 2, xh, xl, (l % 2) * KH, l % 2 == 0, l % 2 == 1)
                else:
                    n = l - 8
                    fresh(n % 2, i * 4 + (S_GLU // 2 + 2 + n // 2))
                    if n == 0:
                        pe.wait_ge(yl_ready, NB)
                    half(h, l, n % 2, yh, yl, 0, True, True)

        with pe.Fori(0, 4) as i:
            for l in range(12):
                m, part = l // 3, l % 3
                if part != 1:
                    fresh(part // 2, i * 4 + (S_OUTA // 2 + m))
                if part < 2:
                    half(i * 12 + (H_OUTA + l), l, 0, xh, xl, part * KH, part == 0, part == 1)
                else:
                    if m == 0:
                        pe.wait_ge(gl_ready, 2 * NB)
                    half(i * 12 + (H_OUTA + l), l, 1, gated_h, gated_l, 0, True, True)

        def merged_there(k):
            pe.wait_ge(xl_ready, KX + k + 1)

        def sum_features(ps, src):
            for t in range(2):
                ins = pe.matmul(ps[:, t, 0:TH], ones[:, :], src[:, t * TH:(t + 1) * TH], start=True, stop=True)
            return ins

        def sum_pivot():
            pe.wait_ge(ones_ready, 1)
            pe.wait_ge(r_ready, 1)
            sum_features(bu_ps, r_all[:, 0, :]).then_inc(pivot_sum, 1)

        def phase_o(i, head):
            for l in range(4):
                if l < 2:
                    fresh(l, i + S_O // 2)
                half(i * 4 + (H_O + l), l, l % 2, xh, xl, (l // 2) * KH, l < 2, l >= 2,
                     mid=sum_pivot if head and l == 3 else None,
                     per_block=merged_there if head and l % 2 == 0 else None)
        phase_o(0, True)
        with pe.Fori(1, KX // 2) as i:
            phase_o(i, False)
        pe.wait_ge(sums_ready, 2)
        pe.wait_ge(pivot_ready, 1)
        sum_features(bu_ps, acc_d).then_inc(sums_done, 1)
        sum_features(y_ps, acc_q).then_inc(sums_done, 1)

    @blk.scalar
    def _(act):
        act.sem_inc(bu_evac, 1)
        act.sem_inc(h_kept, 2)

        def split(h, slot, n, first=False):
            if first:
                act.wait_ge(raw_loaded[slot], 16)
            else:
                act.wait_ge(raw_loaded[slot], n * 16)
            if not (isinstance(h, int) and h < 2):
                act.wait_ge(half_done, h - 1)
            act.activation(w_hi[slot % 2][:, :], w_raw[:, slot, :], ACT.Copy).then_inc(hi_ready, 1)

        def split_next(i, per, h0, l):
            n = h0 + l + 1
            split(i * per + n, n % 4, i * (per // 4) + (n // 4 + 1))

        def evac_sig(dst, h, par, ready, free=True):
            act.wait_ge(half_done, h + 1)
            ins = act.activation(two(dst), halves_of(acc[:, par]), ACT.Sigmoid)
            ins.then_inc(ready, 1)

        def x_high(k):
            act.wait_ge(x_loaded[k if k < 4 else 3 + k // 4], 16)
            act.activation(xh[:, k, :], x_raw[:, k, :], ACT.Copy).then_inc(xh_ready, 1)
        x_high(0)
        split(0, 0, 1, True)
        for k in range(1, KH):
            x_high(k)

        def phase_u(i, head, sines=False):
            for l in range(4):
                split_next(i, 4, H_U, l)
                if head and l < 2:
                    for k in range(4):
                        x_high(KH + 4 * l + k)
                if sines and l == 1:
                    act.wait_ge(sin_in, 1)
                    act.activation(s_s[:, :], s_x[:, :], ACT.Sin).then_inc(sin_out, 1)
                    act.activation(s_c[:, :], s_x[:, :], ACT.Sin, scale=0.5).then_inc(sin_out, 1)
                if l >= 2:
                    s = l - 2
                    act.wait_ge(half_done, i * 4 + (l + 1))
                    if not head:
                        act.wait_ge(u_stored[s], i * 16)
                    act.activation(two(u_stage[s][:, :]), halves_of(acc[:, s]), ACT.Copy)\
                       .then_inc(u_evac, 1)
                    act.wait_ge(u_evac, i * 2 + (s + 1))
                    act.sem_inc(acc_free[s], 1)
        phase_u(0, True)
        phase_u(1, False, True)
        with act.Fori(2, NB // 2) as i:
            phase_u(i, False)
        def decay(p, j, b):
            act.wait_ge(table_free, p + 1)
            act.activation(rmask[j % 2][:, :], scan_mask[:, :], ACT.Copy,
                           scale=mag_blk[:, j:j + 1]).then_inc(rmask_ready, 1)

        def evac_bu(p, j, c):
            act.wait_ge(bu_done, p * 2 + (c + 1))
            if c == 0:
                act.wait_ge(h_ready, p * 2 + 1)
            act.activation(two(bu[j % 2][:, c, :]), halves_of(bu_ps), ACT.Copy).then_inc(bu_evac, 1)

        def keep_states(p, j):
            act.wait_ge(h_ready, p * 2 + 5)
            act.activation(last_state[:, p, :, 0:1], hst[j % 2][:, :, SEQ - 1:SEQ], ACT.Copy)
            act.activation(last_state[:, p, :, 1:], hst[j % 2][:, :, SEQ + DEC_T - 1:TOK:DEC_T], ACT.Copy)\
               .then_inc(h_kept, 1)

        def keep_conv(cb):
            act.wait_ge(q_read, cb + 2)
            act.activation(last_conv[:, cb, 0, :], q_pad[:, SEQ:SEQ + 2], ACT.Copy).then_inc(conv_last, 1)
            qs = q_pad[:, SEQ + 2:QPAD].rearrange("p (b t) -> p b t", b=DEC_B)
            act.activation(last_conv[:, cb, 1:, :], qs[:, :, DEC_T:], ACT.Copy).then_inc(conv_last, 1)

        def gelu_act(b):
            act.wait_ge(y_read, b + 2)
            act.activation(y_tmp[:, :], y_pre[:, :], ACT.Square).then_inc(y_sq, 1)
            act.wait_ge(y_arg, b + 1)
            act.activation(y_tmp[:, :], y_tmp[:, :], ACT.Sigmoid, scale=GELU_S).then_inc(y_sig, 1)

        with act.Fori(0, 4) as b:
            for l in range(16):
                split_next(b, 16, H_CONV, l)
                if l + 1 in CONV_BU:
                    j = CONV_BU.index(l + 1)
                    if j == 0:
                        act.wait_ge(mag_ready, b + 1)
                        act.wait_ge(const_loaded, 64)
                        for s in range(2):
                            act.wait_ge(u_stored[s], 16 * NB // 2)
                    decay(b * 4 + j, j, b)
                if l in CONV_BU:
                    j = CONV_BU.index(l)
                    for c_ in range(2):
                        evac_bu(b * 4 + j, j, c_)
                if l in CONV_KEEP:
                    j = CONV_KEEP.index(l)
                    keep_states(b * 4 + j, j)
                if l % 8 == 1:
                    act.wait_ge(half_done, b * 16 + (H_CONV + l + 1))
                    act.wait_ge(q_read, b * 2 + (l // 8 + 1))
                    act.activation(two(conv_c[:, :]), halves_of(acc[:, 0]), ACT.Copy).then_inc(cc_ready, 1)
                    act.wait_ge(cc_ready, b * 2 + (l // 8 + 1))
                    act.sem_inc(acc_free[0], 1)
                if l % 8 == 5:
                    keep_conv(b * 2 + l // 8)
                if l == 15:
                    gelu_act(b)
                if l % 8 == 7:
                    q = l // 8
                    act.wait_ge(half_done, b * 16 + (H_CONV + l + 1))
                    act.activation(two(gate_t[:, :]), halves_of(acc[:, 1]), ACT.Sigmoid).then_inc(z_sig, 1)
                    act.wait_ge(yc_ready, b * 2 + (q + 1))
                    act.activation(gated_h[:, b * 2 + q, :], conv_t[:, :], ACT.Copy).then_inc(gh_ready, 1)

        with act.Fori(0, 4) as i:
            for l in range(12):
                m = l // 3
                split_next(i, 12, H_OUTC, l)
                if l + 1 in OUTC_BU:
                    j = OUTC_BU.index(l + 1)
                    if j == 0:
                        act.wait_ge(mag_ready, i + 5)
                    decay(i * 4 + (16 + j), j, i)
                if l in OUTC_BU:
                    j = OUTC_BU.index(l)
                    for c_ in range(2):
                        evac_bu(i * 4 + (16 + j), j, c_)
                if l in OUTC_KEEP:
                    j = OUTC_KEEP.index(l)
                    keep_states(i * 4 + (16 + j), j)
                if l % 3 == 1:
                    act.wait_ge(half_done, i * 12 + (H_OUTC + l + 1))
                    act.wait_ge(part_made, i * 4 + m) if m else act.wait_ge(gl_ready, NB)
                    if m == 0:
                        act.wait_ge(acc_free[1], i * 4 + S_OUTC // 2)
                    act.activation(two(gate_t[:, :]), halves_of(acc[:, 0]), ACT.Sigmoid).then_inc(g_sig, 1)
                    act.wait_ge(g_sig, i * 4 + (m + 1))
                    act.sem_inc(acc_free[0], 1)
                if l == 11:
                    gelu_act(i + 4)

        for i in range(2):
            for l in range(12):
                split_next(i, 12, H_GLU, l)
                if i == 0 and l < NB:
                    act.wait_ge(y_loaded[l % 2], 16 * (l // 2 + 1))
                    act.activation(yh[:, l, :], y_in[l % 2][:, :], ACT.Copy).then_inc(yh_ready, 1)
                if l < 8 and l % 2:
                    n = l // 2
                    act.wait_ge(half_done, i * 12 + (H_GLU + l + 1))
                    if i:
                        act.wait_ge(gl_ready, NB + n + 1)
                    act.activation(two(silu_z[n][:, :]), halves_of(acc[:, n % 2]), ACT.Sigmoid)\
                       .then_inc(za_sig, 1)
                if l >= 8:
                    n = l - 8
                    act.wait_ge(half_done, i * 12 + (H_GLU + l + 1))
                    act.activation(two(sig_a[:, :]), halves_of(acc[:, n % 2]), ACT.Sigmoid)\
                       .then_inc(glu_sig, 1)
                    act.wait_ge(glu_sig, i * 4 + (n + 1))
                    act.sem_inc(acc_free[n % 2], 1)
                    act.wait_ge(ya_ready, i * 4 + (n + 1))
                    act.activation(gated_h[:, i * 4 + n, :], y_f[:, :], ACT.Copy).then_inc(gh_ready, 1)
        act.wait_ge(gl_ready, 2 * NB)
        def merged_high(k):
            act.wait_ge(merged_ready, k + 1)
            act.activation(xh[:, k, :], merged[:, k, :], ACT.Copy).then_inc(xh_ready, 1)

        def phase_outa(i, last):
            for l in range(12):
                m = l // 3
                split_next(i, 12, H_OUTA, l)
                if l % 3 == 1:
                    act.wait_ge(half_done, i * 12 + (H_OUTA + l + 1))
                    if m:
                        act.wait_ge(merged_ready, i * 4 + m)
                    else:
                        act.wait_ge(acc_free[1], i * 4 + S_OUTA // 2)
                    act.activation(two(sig_m[:, :]), halves_of(acc[:, 0]), ACT.Sigmoid).then_inc(ga_sig, 1)
                    act.wait_ge(ga_sig, i * 4 + (m + 1))
                    act.sem_inc(acc_free[0], 1)
            if last:
                act.wait_ge(half_done, H_OUTA + 3 * KX - 1)
                for k in range(6):
                    merged_high(k)
        with act.Fori(0, 3) as i:
            phase_outa(i, False)
        phase_outa(3, True)

        def square(n, s):
            act.wait_ge(d_ready, n + 1)
            act.activation(sq[s][:, :], r_all[:, n, :], ACT.Square).then_inc(sq_ready, 1)

        def phase_o(i, head, last):
            for l in range(4):
                if not (last and l == 3):
                    split_next(i, 4, H_O, l)
                if head and l < 3:
                    for k in range(6 + 4 * l, min(10 + 4 * l, KX)):
                        merged_high(k)
                if head and l == 3:
                    act.wait_ge(pivot_sum, 1)
                    act.activation(two(pivot[:, :]), halves_of(bu_ps), ACT.Copy, scale=1.0 / P)\
                       .then_inc(pivot_ready, 1)
                    square(0, 0)
                if l == 3 or (l == 2 and not head):
                    square(i * 2 + (l - 2), l - 2)
        phase_o(0, True, False)
        with act.Fori(1, KX // 2 - 1) as i:
            phase_o(i, False, False)
        phase_o(KX // 2 - 1, False, True)

        act.wait_ge(sums_done, 1)
        act.activation(two(mean[:, :]), halves_of(bu_ps), ACT.Copy, scale=1.0 / D_MODEL).then_inc(mean_ready, 1)
        act.wait_ge(var_ready, 1)
        act.activation(rstd[:, :], rstd[:, :], ACT.Sqrt).then_inc(std_ready, 1)
        for n in range(KX):
            if n in POOL_BLOCKS:
                act.wait_ge(norm_pool, POOL_BLOCKS.index(n) + 1)
            else:
                act.wait_ge(norm_dve, DVE_BLOCKS.index(n) + 1)
            if n >= 4:
                act.wait_ge(out_stored[n % 4], 16 * (n // 4))
            act.activation(o_st[n % 4][:, :], r_all[:, n, :], ACT.Identity, scale=ln_par[:, n, 0:1],
                           bias=ln_par[:, n, 1:2]).then_inc(out_ready, 1)

    @blk.vector
    def _(dve):
        own = Steps(dve_step)

        def link(ins):
            own.mark(ins)
            dve.wait_ge(dve_step, own.value())

        def mark(ins):
            own.mark(ins)

        def split(h, slot):
            dve.wait_ge(hi_ready, h + 1)
            dve.tensor_tensor(w_lo[slot % 2][:, :], w_raw[:, slot, :], w_hi[slot % 2][:, :].bitcast(F32),
                              ALU.subtract).then_inc(lo_ready, 1)

        def split_next(i, per, h0, l):
            n = h0 + l + 1
            split(i * per + n, n % 4)

        dve.sem_inc(y_read, 1)
        dve.sem_inc(table_free, 2)
        dve.sem_inc(q_read, 1)
        dve.sem_inc(y_stored, 16)
        dve.sem_inc(conv_last, 2)
        for s in range(2):
            dve.sem_inc(part_stored[s], 16)

        def x_low(k):
            dve.wait_ge(xh_ready, k + 1)
            dve.tensor_tensor(xl[:, k, :], x_raw[:, k, :], xh[:, k, :].bitcast(F32), ALU.subtract)\
               .then_inc(xl_ready, 1)
        x_low(0)
        split(0, 0)
        for k in range(1, KH):
            x_low(k)

        A_RE, A_IM, LOG_DT = par3[:, 0, :], par3[:, 1, :], par3[:, 2, :]

        def exp_reduce(x):
            link(dve.tensor_scalar(s_k[:, :], x, LOG2E, None, ALU.mult))
            link(dve.tensor_scalar(s_k[:, :], s_k[:, :], MAGIC, None, ALU.add))
            link(dve.tensor_scalar(s_k[:, :], s_k[:, :], MAGIC, None, ALU.subtract))
            link(dve.scalar_tensor_tensor(s_f[:, :], s_k[:, :], -LN2_HI, x, ALU.mult, ALU.add))
            link(dve.scalar_tensor_tensor(s_f[:, :], s_k[:, :], -LN2_LO, s_f[:, :], ALU.mult, ALU.add))

        def exp_series():
            link(dve.tensor_scalar(s_p[:, :], s_f[:, :], 1.0 / 5040, None, ALU.mult))
            for n in (720, 120, 24, 6, 2, 1):
                link(dve.scalar_tensor_tensor(s_p[:, :], s_p[:, :], 1.0 / n, s_f[:, :], ALU.add, ALU.mult))

        def exp_scale(out):
            link(dve.tensor_scalar(s_k[:, :], s_k[:, :], 127.0, None, ALU.add))
            link(dve.tensor_scalar(s_k[:, :], s_k[:, :], 0.0, 255.0, ALU.max, ALU.min))
            link(dve.tensor_copy(s_i[:, :], s_k[:, :]))
            link(dve.tensor_scalar(s_i[:, :], s_i[:, :], 23, None, ALU.logical_shift_left))
            link(dve.scalar_tensor_tensor(out, s_p[:, :], 1.0, s_i[:, :].bitcast(F32), ALU.add, ALU.mult))

        def angles():
            link(dve.tensor_tensor(s_x[:, :], A_IM, s_dt[:, :], ALU.mult))
            link(dve.tensor_scalar(s_k[:, :], s_x[:, :], 1.0 / TWO_PI, None, ALU.mult))
            link(dve.tensor_scalar(s_k[:, :], s_k[:, :], MAGIC, None, ALU.add))
            link(dve.tensor_scalar(s_k[:, :], s_k[:, :], MAGIC, None, ALU.subtract))
            for part in (PI_A, PI_B, PI_C):
                link(dve.scalar_tensor_tensor(s_x[:, :], s_k[:, :], -part, s_x[:, :], ALU.mult, ALU.add))
            dve.tensor_scalar(s_x[:, :], s_x[:, :], -PI_LESS, PI_LESS, ALU.max, ALU.min).then_inc(sin_in, 1)

        def phase_and_lam():
            dve.wait_ge(sin_out, 2)
            link(dve.tensor_tensor(s_c[:, :], s_c[:, :], s_c[:, :], ALU.mult))
            link(dve.tensor_scalar(s_c[:, :], s_c[:, :], -2.0, 1.0, ALU.mult, ALU.add))
            st = slice(0, PAIRS)
            link(dve.tensor_tensor(s_f[:, st], s_c[:, st], s_c[:, st], ALU.mult))
            link(dve.tensor_tensor(s_p[:, st], s_s[:, st], s_s[:, st], ALU.mult))
            link(dve.tensor_tensor(s_f[:, st], s_f[:, st], s_p[:, st], ALU.add))
            link(dve.tensor_scalar(s_f[:, st], s_f[:, st], -0.5, 1.5, ALU.mult, ALU.add))
            link(dve.tensor_tensor(fine(0, 0, 1), s_c[:, st].rearrange("p (b j) -> p b j", j=4).unsqueeze(3),
                                   s_f[:, st].rearrange("p (b j) -> p b j", j=4).unsqueeze(3), ALU.mult))
            link(dve.tensor_tensor(fine(1, 0, 1), s_s[:, st].rearrange("p (b j) -> p b j", j=4).unsqueeze(3),
                                   s_f[:, st].rearrange("p (b j) -> p b j", j=4).unsqueeze(3), ALU.mult))
            link(dve.tensor_copy(mag_all[:, :], s_mag[:, st]))

        rot = rot_all[:, :].rearrange("p (b j w) -> p b j w", j=4, w=ROT_P)

        def fine(c, a, b):
            return rot[:, :, :, c * FINE + a:c * FINE + b]

        def coarse(c, a, b):
            return rot[:, :, :, 2 * FINE + c * COARSE + a:2 * FINE + c * COARSE + b]

        def tmp(t, n):
            return t[:, 0:PAIRS * n].rearrange("p (b j n) -> p b j n", j=4, n=n)

        def turn(out, a, by, n):
            e = lambda x: x.to_broadcast([P, NB, 4, n])
            link(dve.tensor_tensor(tmp(s_f, n), a[0], e(by[0]), ALU.mult))
            link(dve.tensor_tensor(tmp(s_p, n), a[1], e(by[1]), ALU.mult))
            link(dve.tensor_tensor(tmp(s_x, n), a[0], e(by[1]), ALU.mult))
            link(dve.tensor_tensor(tmp(s_k, n), a[1], e(by[0]), ALU.mult))
            link(dve.tensor_tensor(out[0], tmp(s_f, n), tmp(s_p, n), ALU.subtract))
            link(dve.tensor_tensor(out[1], tmp(s_x, n), tmp(s_k, n), ALU.add))

        def fine_table(n):
            turn([fine(c, n, 2 * n) for c in (0, 1)], [fine(c, 0, n) for c in (0, 1)],
                 [fine(c, n - 1, n) for c in (0, 1)], n)

        def coarse_start():
            link(dve.memset(coarse(0, 0, 1), 1.0))
            link(dve.memset(coarse(1, 0, 1), 0.0))
            for c in range(2):
                link(dve.tensor_copy(coarse(c, 1, 2), fine(c, FINE - 1, FINE)))

        def coarse_table(n):
            turn([coarse(c, n, n + 1) for c in (0, 1)], [coarse(c, n - 1, n) for c in (0, 1)],
                 [coarse(c, 1, 2) for c in (0, 1)], 1)
            turn([coarse(c, n + 1, 2 * n) for c in (0, 1)], [coarse(c, 1, n) for c in (0, 1)],
                 [coarse(c, n, n + 1) for c in (0, 1)], n - 1)

        ch = slice(PAIRS, SETUP)
        a_re, a_im = A_RE[:, ch], A_IM[:, ch]
        q_re, q_im, w0, w1 = s_s[:, ch], s_c[:, ch], s_mag[:, ch], s_dt[:, ch]

        def zoh_lam():
            link(dve.tensor_tensor(w1, s_mag[:, ch], s_s[:, ch], ALU.mult))
            link(dve.tensor_tensor(w0, s_mag[:, ch], s_c[:, ch], ALU.mult))
            link(dve.tensor_scalar(w0, w0, 1.0, None, ALU.subtract))
            link(dve.tensor_tensor(s_f[:, ch], a_re, a_re, ALU.mult))
            link(dve.tensor_tensor(s_p[:, ch], a_im, a_im, ALU.mult))
            link(dve.tensor_tensor(s_f[:, ch], s_f[:, ch], s_p[:, ch], ALU.add))
            link(dve.reciprocal(s_f[:, ch], s_f[:, ch]))

        def zoh_q():
            link(dve.tensor_tensor(q_re, w0, a_re, ALU.mult))
            link(dve.tensor_tensor(s_p[:, ch], w1, a_im, ALU.mult))
            link(dve.tensor_tensor(q_re, q_re, s_p[:, ch], ALU.add))
            link(dve.tensor_tensor(q_re, q_re, s_f[:, ch], ALU.mult))
            link(dve.tensor_tensor(q_im, w1, a_re, ALU.mult))
            link(dve.tensor_tensor(s_p[:, ch], w0, a_im, ALU.mult))
            link(dve.tensor_tensor(q_im, q_im, s_p[:, ch], ALU.subtract))
            link(dve.tensor_tensor(q_im, q_im, s_f[:, ch], ALU.mult))

        def zoh_b():
            blocks = lambda x: x.rearrange("p (b s) -> p b s", b=NB)
            for c, (qa, qb, op) in enumerate(((q_re, q_im, ALU.subtract), (q_im, q_re, ALU.add))):
                link(dve.tensor_tensor(w0, qa, b_par[:, 0, :], ALU.mult))
                link(dve.tensor_tensor(w1, qb, b_par[:, 1, :], ALU.mult))
                link(dve.tensor_tensor(bb_all[:, :, c * STATE:(c + 1) * STATE],
                                       blocks(w0), blocks(w1), op))

        for h in range(2 * NB):
            split(h + 1, (h + 1) % 4)
            if h < 2:
                for k in range(4):
                    x_low(KH + 4 * h + k)
            if h == 2:
                dve.wait_ge(par_loaded, 32)
                exp_reduce(LOG_DT)
            if h == 3:
                exp_series()
                exp_scale(s_dt[:, :])
            if h == 4:
                angles()
                link(dve.tensor_tensor(s_dt[:, :], A_RE, s_dt[:, :], ALU.mult))
            if h == 5:
                exp_reduce(s_dt[:, :])
                exp_series()
            if h == 6:
                exp_scale(s_mag[:, :])
                phase_and_lam()
            if h == 7:
                for n in (1, 2, 4):
                    fine_table(n)
            if h == 8:
                fine_table(8)
                coarse_start()
                for n in (2, 3):
                    turn([coarse(c, n, n + 1) for c in (0, 1)], [coarse(c, n - 1, n) for c in (0, 1)],
                         [coarse(c, 1, 2) for c in (0, 1)], 1)
            if h == 9:
                coarse_table(4)
                coarse_table(8)
            if h == 10:
                coarse_table(16)
                dve.sem_inc(rot_ready, 1)
            if h == 11:
                zoh_lam()
            if h == 12:
                zoh_q()
            if h == 13:
                zoh_b()
                dve.memset(ones[:, :], 1.0).then_inc(ones_ready, 1)

        q_prompt = q_pad[:, 0:SEQ + 2]
        q_sample = q_pad[:, SEQ + 2:QPAD].rearrange("p (b t) -> p b t", b=DEC_B)

        def pad_b(p, b, j):
            if j >= 2:
                dve.wait_ge(bu_done, (p - 1) * 2)
            src = bb_all[:, b, :].rearrange("p (c s) -> p c s", c=2)
            for g in range(2):
                ins = dve.tensor_scalar(b_pad[j % 2][:, :, g * STATE:(g + 1) * STATE], src,
                                        mask8[:, 2 * j + g:2 * j + g + 1], None, ALU.mult)
                if g == 0:
                    mark(ins)
            dve.wait_ge(dve_step, own.value())
            ins.then_inc(b_pad_ready, 1)

        def spread(t, n):
            return t.unsqueeze(1).to_broadcast([P, 2, n])

        def to_frame(p, j):
            dve.wait_ge(table_ready, p * 2 + 2)
            dve.wait_ge(bu_evac, p * 2 + 3)
            dve.wait_ge(h_ready, p * 2 + 3)
            s = j % 2
            dve.tensor_tensor(m1[:, :, :], bu[s][:, :, :], spread(table[s][:, 0, :], TOK), ALU.mult)\
               .then_inc(prod1_ready, 1)
            dve.tensor_tensor(m2[:, :, :], bu[s][:, :, :], spread(table[s][:, 1, :], TOK), ALU.mult)\
               .then_inc(prod1_ready, 1)

        def scans(p, j):
            s = j % 2
            first = bu[s][:, :, SEQ:TOK:DEC_T]
            h0 = host_blk[:, C0 + j * 2 * DEC_B:C0 + (j + 1) * 2 * DEC_B].rearrange("p (c b) -> p c b", c=2)
            dve.wait_ge(v_ready, p * 2 + 2)
            link(dve.scalar_tensor_tensor(first, h0, mag_blk[:, j:j + 1], first,
                                          ALU.mult, ALU.add))
            dve.wait_ge(rmask_ready, p + 1)
            for c in range(2):
                ins = dve.tensor_tensor_scan(m1[:, c, :], rmask[s][:, :], bu[s][:, c, :], 0.0,
                                             ALU.mult, ALU.add)
                mark(ins)
            dve.wait_ge(dve_step, own.value())
            dve.tensor_tensor(bu[s][:, :, :], m1[:, :, :], spread(table[s][:, 0, :], TOK), ALU.mult)\
               .then_inc(prod2_ready, 1)
            ins = dve.tensor_tensor(m2[:, :, :], m1[:, :, :], spread(table[s][:, 1, :], TOK), ALU.mult)
            ins.then_inc(prod2_ready, 1)
            dve.wait_ge(prod2_ready, p * 2 + 2)
            dve.sem_inc(table_free, 1)

        def new_block(b, loaded):
            dve.wait_ge(blk_loaded, loaded)
            for s in range(2):
                dve.wait_ge(u_stored[s], 16 * NB // 2)
            dve.wait_ge(const_loaded, 64)
            dve.tensor_copy(mag_blk[:, :], mag_all[:, bass.ds(b * 4, 4)]).then_inc(mag_ready, 1)

        def negate_c():
            v = host_blk[:, 0:C0].rearrange("p (j c n) -> p j c n", j=4, c=2)[:, :, 1, :]
            return dve.tensor_scalar(v, v, -1.0, None, ALU.mult)

        def read_y(b):
            dve.wait_ge(h_used, b * 4 + 6)
            dve.wait_ge(y_stored, b * 16 + 16)
            own.mark(dve.scalar_tensor_tensor(two(y_pre[:, :]), two(u_blk[:, :]),
                                              host_blk[:, C0 + H0:C0 + H0 + 1], halves_of(y_ps),
                                              ALU.mult, ALU.add))
            dve.wait_ge(dve_step, own.value())
            dve.sem_inc(y_read, 1)

        def gelu(b):
            dve.wait_ge(y_sq, b + 1)
            link(dve.tensor_scalar(y_tmp[:, :], y_tmp[:, :], GELU_C, 1.0, ALU.mult, ALU.add))
            dve.tensor_tensor(y_tmp[:, :], y_tmp[:, :], y_pre[:, :], ALU.mult).then_inc(y_arg, 1)
            dve.wait_ge(y_sig, b + 1)
            dve.tensor_tensor(y_pre[:, :], y_pre[:, :], y_tmp[:, :], ALU.mult).then_inc(y_made, 1)

        def free(par):
            dve.sem_inc(acc_free[par], 1)

        def conv_h(b, q, h):
            dve.wait_ge(conv_last, b * 4 + 2 * q + 2)
            cb = b * 2 + q
            link(dve.tensor_copy(cw[:, :], conv_par[:, cb, 0:3]))
            link(dve.tensor_copy(q_sample[:, :, 0:2],
                                 conv_par[:, cb, 3:3 + 2 * DEC_B].rearrange("p (s t) -> p s t", t=2)))
            dve.wait_ge(cc_ready, b * 2 + (q + 1))
            dve.wait_ge(half_done, h + 1)
            own.mark(dve.tensor_tensor(q_prompt[:, 2:2 + TH], conv_c[:, 0:TH], acc[:, 1, 0, 0:TH], ALU.mult))
            own.mark(dve.tensor_tensor(q_prompt[:, 2 + TH:2 + SEQ], conv_c[:, TH:SEQ],
                                       acc[:, 1, 1, 0:SEQ - TH], ALU.mult))
            own.mark(dve.tensor_tensor(q_sample[:, :, 2:], conv_c[:, SEQ:].rearrange("p (s t) -> p s t", s=DEC_B),
                                       acc[:, 1, 1, SEQ - TH:TH].rearrange("p (s t) -> p s t", s=DEC_B),
                                       ALU.mult))
            dve.wait_ge(dve_step, own.value())
            dve.sem_inc(q_read, 1)
            free(1)
            c_s = conv_t[:, SEQ:].rearrange("p (s t) -> p s t", s=DEC_B)
            for k in range(3):
                pr, sa = q_prompt[:, k:k + SEQ], q_sample[:, :, k:k + DEC_T]
                w = cw[:, k:k + 1]
                if k == 0:
                    own.mark(dve.tensor_scalar(conv_t[:, 0:SEQ], pr, w, None, ALU.mult))
                    link(dve.tensor_scalar(c_s, sa, w, None, ALU.mult))
                else:
                    own.mark(dve.scalar_tensor_tensor(conv_t[:, 0:SEQ], pr, w, conv_t[:, 0:SEQ],
                                                      ALU.mult, ALU.add))
                    link(dve.scalar_tensor_tensor(c_s, sa, w, c_s, ALU.mult, ALU.add))

        def conv_b(h):
            dve.wait_ge(half_done, h + 1)
            link(dve.tensor_tensor(two(conv_t[:, :]), two(conv_t[:, :]), halves_of(acc[:, 0]), ALU.mult))
            free(0)

        def conv_z(b, q, h):
            dve.wait_ge(half_done, h + 1)
            dve.wait_ge(z_sig, b * 2 + (q + 1))
            link(dve.tensor_tensor(two(gate_t[:, :]), two(gate_t[:, :]), halves_of(acc[:, 1]), ALU.mult))
            free(1)
            dve.tensor_tensor(conv_t[:, :], conv_t[:, :], gate_t[:, :], ALU.mult).then_inc(yc_ready, 1)
            dve.wait_ge(gh_ready, b * 2 + (q + 1))
            hi = gated_h[:, b * 2 + q, :]
            lo = gated_l[:, b * 2 + q, :]
            dve.tensor_tensor(lo, conv_t[:, :], hi.bitcast(F32), ALU.subtract).then_inc(gl_ready, 1)

        STEPS_CONV = own.value()
        count = {}

        def conv_body(b):
            for l in range(16):
                split_next(b, 16, H_CONV, l)
                if l == 1:
                    new_block(b, b * 32 + 32)
                    link(dve.memset(q_pad[:, 0:2], 0.0))
                    negate_c().then_inc(c_ready, 1)
                if l + 1 in CONV_BU:
                    j = CONV_BU.index(l + 1)
                    pad_b(b * 4 + j, b, j)
                if l - 1 in CONV_BU:
                    j = CONV_BU.index(l - 1)
                    scans(b * 4 + j, j)
                if l in CONV_BU:
                    j = CONV_BU.index(l)
                    to_frame(b * 4 + j, j)
                h = b * 16 + (H_CONV + l)
                if l == 15:
                    read_y(b)
                    gelu(b)
                if l % 8 == 3:
                    conv_h(b, l // 8, h)
                if l % 8 == 5:
                    conv_b(h)
                if l % 8 == 7:
                    conv_z(b, l // 8, h)

        CONV_STEPS = 45
        with dve.Fori(0, 4) as b:
            own.at(b * CONV_STEPS + STEPS_CONV)
            conv_body(b)
            assert own.k == CONV_STEPS, own.k
        STEPS_OUTC = STEPS_CONV + 4 * CONV_STEPS

        OUTC_STEPS = 18
        with dve.Fori(0, 4) as i:
            own.at(i * OUTC_STEPS + STEPS_OUTC)
            for l in range(12):
                m = l // 3
                split_next(i, 12, H_OUTC, l)
                if l == 1:
                    new_block(i + 4, i * 32 + 32 * 5)
                    negate_c().then_inc(c_ready, 1)
                if l + 1 in OUTC_BU:
                    j = OUTC_BU.index(l + 1)
                    pad_b(i * 4 + (16 + j), i + 4, j)
                if l - 1 in OUTC_BU:
                    j = OUTC_BU.index(l - 1)
                    scans(i * 4 + (16 + j), j)
                if l in OUTC_BU:
                    j = OUTC_BU.index(l)
                    to_frame(i * 4 + (16 + j), j)
                if l == 11:
                    read_y(i + 4)
                    gelu(i + 4)
                if l % 3 == 2:
                    dve.wait_ge(half_done, i * 12 + (H_OUTC + l + 1))
                    dve.wait_ge(g_sig, i * 4 + (m + 1))
                    dve.wait_ge(part_stored[m % 2], i * 32 + 16 * (m // 2 + 1))
                    dve.tensor_tensor(two(part_st[m % 2][:, :]), two(gate_t[:, :]), halves_of(acc[:, 1]),
                                      ALU.mult).then_inc(part_made, 1)
                    dve.wait_ge(part_made, i * 4 + (m + 1))
                    free(1)
            assert own.k == OUTC_STEPS, own.k
        own.at(STEPS_OUTC + 4 * OUTC_STEPS)

        STEPS_GLU = own.value()
        for i in range(2):
            for l in range(12):
                split_next(i, 12, H_GLU, l)
                if i == 0 and l < NB:
                    dve.wait_ge(yh_ready, l + 1)
                    dve.tensor_tensor(yl[:, l, :], y_in[l % 2][:, :], yh[:, l, :].bitcast(F32), ALU.subtract)\
                       .then_inc(yl_ready, 1)
                if l < 8 and l % 2:
                    n = l // 2
                    dve.wait_ge(za_sig, i * 4 + (n + 1))
                    link(dve.tensor_tensor(two(silu_z[n][:, :]), two(silu_z[n][:, :]),
                                           halves_of(acc[:, n % 2]), ALU.mult))
                    free(n % 2)
                if l >= 8:
                    n = l - 8
                    if l == 8:
                        dve.wait_ge(yl_ready, NB)
                    if i or n:
                        dve.wait_ge(gl_ready, i * 4 + NB + n)
                    yv, lv = (y[:, i * 4 + n, :].bitcast(F32) for y in (yh, yl))
                    link(dve.tensor_tensor(y_f[:, :], yv, lv, ALU.add))
                    link(dve.tensor_tensor(y_f[:, :], y_f[:, :], silu_z[n][:, :], ALU.mult))
                    dve.wait_ge(glu_sig, i * 4 + (n + 1))
                    dve.tensor_tensor(y_f[:, :], y_f[:, :], sig_a[:, :], ALU.mult).then_inc(ya_ready, 1)
                    dve.wait_ge(gh_ready, i * 4 + (NB + n + 1))
                    hi = gated_h[:, i * 4 + n, :].bitcast(F32)
                    dve.tensor_tensor(gated_l[:, i * 4 + n, :], y_f[:, :], hi, ALU.subtract).then_inc(gl_ready, 1)
        STEPS_OUTA = own.value()

        def merged_low(k):
            dve.wait_ge(xh_ready, KX + k + 1)
            dve.tensor_tensor(xl[:, k, :], merged[:, k, :], xh[:, k, :].bitcast(F32), ALU.subtract)\
               .then_inc(xl_ready, 1)

        def phase_outa(i, last):
            for l in range(12):
                m = l // 3
                split_next(i, 12, H_OUTA, l)
                if last and l == 11:
                    for k in range(4):
                        merged_low(k)
                if l % 3 == 2:
                    dve.wait_ge(half_done, i * 12 + (H_OUTA + l + 1))
                    dve.wait_ge(ga_sig, i * 4 + (m + 1))
                    own.at(i * 4 + (STEPS_OUTA + m))
                    link(dve.tensor_tensor(two(sig_m[:, :]), two(sig_m[:, :]), halves_of(acc[:, 1]), ALU.mult))
                    free(1)
                    dve.wait_ge(part_loaded[m % 2], i * 32 + 16 * (m // 2 + 1))
                    dve.tensor_tensor(merged[:, i * 4 + m, :], sig_m[:, :], part_in[m % 2][:, :], ALU.add)\
                       .then_inc(merged_ready, 1)
        with dve.Fori(0, 3) as i:
            phase_outa(i, False)
        phase_outa(3, True)
        for k in (4, 5):
            merged_low(k)
        STEPS_O = STEPS_OUTA + KX
        own.at(STEPS_O)

        def take_r(i, s):
            n = i * 2 + s
            dve.wait_ge(half_done, i * 4 + (H_O + s + 3))
            dve.wait_ge(xin_loaded[s], i * 16 + 16)
            dve.scalar_tensor_tensor(two(r_all[:, n, :]), two(x_in[s][:, :]), ALPHA, halves_of(acc[:, s]),
                                     ALU.mult, ALU.add).then_inc(r_ready, 1)
            dve.wait_ge(r_ready, n + 1)
            free(s)

        def take_d(i, s, first=False):
            n = i * 2 + s
            out = r_all[:, n, :]
            dve.tensor_tensor(out, out, pivot[:, :], ALU.subtract).then_inc(d_ready, 1)
            dve.wait_ge(d_ready, n + 1)
            if first:
                link(dve.tensor_copy(acc_d[:, :], out))
            else:
                link(dve.tensor_tensor(acc_d[:, :], acc_d[:, :], out, ALU.add))
            dve.wait_ge(sq_ready, n + 1)
            if first:
                link(dve.tensor_copy(acc_q[:, :], sq[s][:, :]))
            else:
                link(dve.tensor_tensor(acc_q[:, :], acc_q[:, :], sq[s][:, :], ALU.add))

        def phase_o(i, head, last):
            for l in range(4):
                if not (last and l == 3):
                    split_next(i, 4, H_O, l)
                if head and l < 3:
                    for k in range(6 + 4 * l, min(10 + 4 * l, KX)):
                        merged_low(k)
                if head and l == 3:
                    dve.wait_ge(pivot_ready, 1)
                    take_d(0, 0, True)
                if l >= 2:
                    take_r(i, l - 2)
                    if not (head and l == 2):
                        take_d(i, l - 2)
        phase_o(0, True, False)
        assert own.k == 4
        with dve.Fori(1, KX // 2 - 1) as i:
            own.at(i * 4 + STEPS_O)
            phase_o(i, False, False)
            assert own.k == 4
        own.at((KX // 2 - 1) * 4 + STEPS_O)
        phase_o(KX // 2 - 1, False, True)
        dve.sem_inc(sums_ready, 2)

        dve.wait_ge(sums_done, 2)
        link(dve.tensor_scalar(two(rstd[:, :]), halves_of(y_ps), 1.0 / D_MODEL, LN_EPS, ALU.mult, ALU.add))
        dve.wait_ge(mean_ready, 1)
        link(dve.tensor_tensor(mean_r[:, :], mean[:, :], mean[:, :], ALU.mult))
        dve.tensor_tensor(rstd[:, :], rstd[:, :], mean_r[:, :], ALU.subtract).then_inc(var_ready, 1)
        dve.wait_ge(std_ready, 1)
        link(dve.reciprocal(rstd[:, :], rstd[:, :]))
        dve.tensor_tensor(mean_r[:, :], mean[:, :], rstd[:, :], ALU.mult).then_inc(rstd_ready, 1)
        dve.wait_ge(rstd_ready, 1)
        for n in DVE_BLOCKS:
            link(dve.tensor_tensor(r_all[:, n, :], r_all[:, n, :], rstd[:, :], ALU.mult))
            dve.tensor_tensor(r_all[:, n, :], r_all[:, n, :], mean_r[:, :], ALU.subtract).then_inc(norm_dve, 1)

    @blk.gpsimd
    def _(pool):
        pool.sem_inc(h_ready, 3)
        pool.sem_inc(h_used, 2)

        def make_table(p, s):
            pool.wait_ge(table_free, p + 1)
            at = p * ROT_P
            f = lambda c: rot_all[:, bass.ds(at + c * FINE, FINE)].unsqueeze(1).to_broadcast([P, COARSE, FINE])
            g = lambda c: rot_all[:, bass.ds(at + (2 * FINE + c * COARSE), COARSE)]\
                .unsqueeze(2).to_broadcast([P, COARSE, FINE])
            grid = lambda x: x.rearrange("p (a b) -> p a b", b=FINE)
            for c, (ga, gb) in enumerate(((0, 1), (1, 0))):
                pool_step.mark(pool.tensor_tensor(grid(table[s][:, c, 0:SEQ]), g(ga), f(0), ALU.mult))
                pool_step.mark(pool.tensor_tensor(grid(t_tmp[:, c, :]), g(gb), f(1), ALU.mult))
                sample = rot_all[:, bass.ds(at + c * FINE, DEC_T)].unsqueeze(1).to_broadcast([P, DEC_B, DEC_T])
                pool_step.mark(pool.tensor_copy(
                    table[s][:, c, SEQ:].rearrange("p (b t) -> p b t", b=DEC_B), sample))
            pool.wait_ge(pool_step.sem, pool_step.value())
            for c, op in enumerate((ALU.subtract, ALU.add)):
                out = table[s][:, c, 0:SEQ]
                pool.tensor_tensor(out, out, t_tmp[:, c, :], op).then_inc(table_ready, 1)

        pool_step = Steps(sem("pool_step"))

        def add_frame(p, j):
            s = j % 2
            pool.wait_ge(prod1_ready, p * 2 + 2)
            pool.tensor_tensor(bu[s][:, 0, :], m1[:, 0, :], m2[:, 1, :], ALU.add).then_inc(v_ready, 1)
            pool.tensor_tensor(bu[s][:, 1, :], m1[:, 1, :], m2[:, 0, :], ALU.subtract).then_inc(v_ready, 1)

        def add_back(p, j):
            s = j % 2
            pool.wait_ge(prod2_ready, p * 2 + 2)
            pool.wait_ge(h_used, p + 1)
            pool.wait_ge(h_kept, p + 1)
            pool.tensor_tensor(hst[s][:, 0, :], bu[s][:, 0, :], m2[:, 1, :], ALU.subtract).then_inc(h_ready, 1)
            pool.tensor_tensor(hst[s][:, 1, :], bu[s][:, 1, :], m2[:, 0, :], ALU.add).then_inc(h_ready, 1)

        def block(p0, k0, last):
            pool_step.at(k0)
            for j in range(4):
                add_frame(p0 + j, j)
                if j < 3:
                    make_table(p0 + (j + 1), (j + 1) % 2)
                add_back(p0 + j, j)
            if not last:
                make_table(p0 + 4, 0)
        pool.wait_ge(rot_ready, 1)
        make_table(0, 0)
        per = 6 * 4
        with pool.Fori(0, NB - 1) as b:
            block(b * 4, b * per + 6, False)
            assert pool_step.k == per
        block((NB - 1) * 4, (NB - 1) * per + 6, True)

        pool.wait_ge(rstd_ready, 1)
        pool_step.at((NB - 1) * per + 6 + 18)
        for n in POOL_BLOCKS:
            pool_step.mark(pool.tensor_tensor(r_all[:, n, :], r_all[:, n, :], rstd[:, :], ALU.mult))
            pool.wait_ge(pool_step.sem, pool_step.value())
            pool.tensor_tensor(r_all[:, n, :], r_all[:, n, :], mean_r[:, :], ALU.subtract).then_inc(norm_pool, 1)

    block.__exit__(None, None, None)


def kernel(x_prompt, x_sample, state_ssm_re, state_ssm_im, state_conv, w_in, ssm_a_re, ssm_a_im,
           ssm_log_dt, ssm_b_re, ssm_b_im, ssm_c_re, ssm_c_im, ssm_d, w_glu, w_out_a, conv_w, w_out_c,
           w_o, ln_g, ln_b):
    import concourse.bacc as bacc
    from concourse.bass_utils import run_bass_kernel_spmd

    f = lambda a: np.asarray(a)
    tokens = np.concatenate([f(x_prompt)[0], f(x_sample).reshape(DEC_B * DEC_T, D_MODEL)], 0)
    xT = np.ascontiguousarray(tokens.T).reshape(KX, P, TOK)

    def halves(w):
        k, n = w.shape
        v = w.reshape(k // (KH * P), KH, P, n // P, P).transpose(3, 0, 2, 1, 4)
        return v.reshape(n // P, k // (KH * P), P, KH * P)
    wi = halves(f(w_in)[0])
    bounds = np.cumsum([0, NB, NB, NB, NB, NB, NB, KX, KX])
    u_w, z_a, b_c, c_c, h_c, z_c, g_a, g_c = (wi[bounds[i]:bounds[i + 1]] for i in range(8))
    glu, out_a, out_c, w_out = (halves(f(w)[0]) for w in (w_glu, w_out_a, w_out_c, w_o))
    def side_by_side(v):
        return [v[n + o][k:k + 1] for n in range(0, len(v), 2) for k in range(2) for o in range(2)]
    order = side_by_side(u_w)
    for n in range(NB):
        order += [c_c[n], h_c[n], b_c[n], z_c[n]]
    for n in range(KX):
        order += [g_c[n], out_c[n]]
    for n in range(0, NB, 4):
        order += [*z_a[n:n + 4], *glu[n:n + 4]]
    for n in range(KX):
        order += [g_a[n], out_a[n]]
    order += side_by_side(w_out)
    w = np.concatenate(order, 0)

    def two_layouts(a):
        states = a.reshape(PAIRS, 2 * STATE).T
        channels = np.broadcast_to(a.reshape(NB, 8, 1, STATE), (NB, 8, GC, STATE))
        channels = channels.transpose(1, 2, 0, 3).reshape(P, NB * STATE)
        return np.concatenate([states, channels], 1)
    log_dt = np.broadcast_to(f(ssm_log_dt)[0][:, None], (2 * PAIRS, STATE))
    par3 = np.stack([two_layouts(a) for a in (f(ssm_a_re)[0], f(ssm_a_im)[0], log_dt)], 1)

    def channel_rows(a):
        return a.reshape(NB, 8, STATE, GC).transpose(1, 3, 0, 2).reshape(P, NB * STATE)
    b_par = np.stack([channel_rows(f(ssm_b_re)[0]), channel_rows(f(ssm_b_im)[0])], 1)

    host_blk = np.zeros((NB, P, HOST_W), np.float32)
    cv = host_blk[:, :, 0:C0].reshape(NB, 2, STATE, 4, 2, 2, GC)
    cv = np.zeros((NB, 2, STATE, 4, 2, 2, GC), np.float32)
    for part, src in enumerate((ssm_c_re, ssm_c_im)):
        s = f(src)[0].reshape(NB, 4, 2, GC, STATE)
        for g in range(2):
            cv[:, g, :, :, part, g, :] = s[:, :, g].transpose(0, 3, 1, 2)
    host_blk[:, :, 0:C0] = cv.reshape(NB, P, C0)
    h0 = np.stack([f(state_ssm_re)[0], f(state_ssm_im)[0]], 0)
    h0 = h0.reshape(2, DEC_B, NB, 4, 2, STATE).transpose(2, 4, 5, 3, 0, 1)
    host_blk[:, :, C0:C0 + H0] = h0.reshape(NB, P, H0)
    host_blk[:, :, C0 + H0] = f(ssm_d)[0].reshape(NB, P)

    conv_par = np.concatenate([
        f(conv_w)[0].reshape(3, NB, P).transpose(2, 1, 0),
        f(state_conv)[0].reshape(DEC_B, 2, NB, P).transpose(3, 2, 0, 1).reshape(P, NB, 2 * DEC_B)], 2)
    ln_par = np.stack([f(ln_g)[0].reshape(KX, P).T, f(ln_b)[0].reshape(KX, P).T], 2)
    mask8 = (np.arange(P)[:, None] // GC == np.arange(8)[None]).astype(np.float32)
    starts = np.ones(TOK, np.float32)
    starts[0] = 0
    starts[SEQ::DEC_T] = 0
    scan_mask = np.broadcast_to(starts, (P, TOK))

    arrays = {"w": w, "xT": xT, "par3": par3, "b_par": b_par, "host_blk": host_blk,
              "conv_par": conv_par, "ln_par": ln_par, "mask8": mask8, "scan_mask": scan_mask}
    nc = bacc.Bacc("TRN2", target_bir_lowering=False, num_devices=1, dynamic_dma_scratch_size=1024)
    d, feed = {}, {}
    for name, a in arrays.items():
        a = np.ascontiguousarray(a)
        feed[f"in_{name}"] = a
        d[name] = nc.dram_tensor(f"in_{name}", a.shape, F32, kind="ExternalInput").ap()
    for name, shape in (("outT", [KX, P, TOK]), ("out_state", [P, PAIRS, 2, SCAN_ENDS]),
                        ("out_conv", [P, NB, SCAN_ENDS, 2])):
        d[name] = nc.dram_tensor(name, shape, F32, kind="ExternalOutput").ap()
    build(nc, d)
    res = run_bass_kernel_spmd(nc, [feed], core_ids=[0]).results[0]

    y = np.asarray(res["outT"]).reshape(D_MODEL, TOK).T
    st = np.asarray(res["out_state"]).reshape(2, STATE, PAIRS, 2, SCAN_ENDS)
    st = st.transpose(3, 4, 2, 0, 1).reshape(2, SCAN_ENDS, 2 * PAIRS, STATE)
    cv = np.asarray(res["out_conv"]).transpose(2, 3, 1, 0).reshape(SCAN_ENDS, 2, D_CONV)
    c = np.ascontiguousarray
    return (c(y[:SEQ])[None], c(y[SEQ:]).reshape(DEC_B, DEC_T, D_MODEL),
            c(st[0, :1])[None], c(st[1, :1])[None], c(cv[:1])[None],
            c(st[0, 1:])[None], c(st[1, 1:])[None], c(cv[1:])[None])
```

```python
import numpy as np
import concourse.bass as bass
import concourse.mybir as mybir
from concourse.alu_op_type import AluOpType as ALU

F32 = mybir.dt.float32
F32R = mybir.dt.float32r
I32 = mybir.dt.int32
ACT = mybir.ActivationFunctionType

P = 128
D_MODEL = 2048
D_SSM = 1024
D_CONV = 1024
SEQ = 512
DEC_B = 8
DEC_T = 8
TOK = SEQ + DEC_B * DEC_T
TH = TOK // 2
KH = 8
KX = D_MODEL // P
NB = D_SSM // P
PAIRS = 32
STATE = 64
GC = 16
FINE = 16
COARSE = SEQ // FINE
SCAN_ENDS = 1 + DEC_B
ALPHA = float(2.0 ** 0.25)
LN_EPS = 1e-5
GELU_C = 0.044715
GELU_S = 2.0 * float(np.sqrt(2.0 / np.pi))

ROT_P = 2 * FINE + 2 * COARSE
C0 = 4 * 2 * 32
H0 = 4 * 2 * DEC_B
HOST_W = C0 + H0 + 2
CONV_W = 3 + 2 * DEC_B
QPAD = SEQ + 2 + DEC_B * (DEC_T + 2)
SETUP = PAIRS + NB * STATE

H_U = 0
H_CONV = H_U + 2 * NB
H_OUTC = H_CONV + 8 * NB
H_GLU = H_OUTC + 3 * KX
H_OUTA = H_GLU + 3 * NB
H_O = H_OUTA + 3 * KX
S_CONV = NB
S_OUTC = S_CONV + 4 * NB
S_GLU = S_OUTC + 2 * KX
S_OUTA = S_GLU + 2 * NB
S_O = S_OUTA + 2 * KX

POOL_BLOCKS = list(range(2, KX - 1, 3))
DVE_BLOCKS = [n for n in range(KX) if n not in POOL_BLOCKS]

MAGIC = 12582912.0
LOG2E = 1.4426950408889634
LN2_HI = 0.693359375
LN2_LO = -2.12194440e-4
TWO_PI = 2.0 * np.pi
PI_A = 6.28125
PI_B = float(np.float32(np.round((TWO_PI - PI_A) * 2.0 ** 20) / 2.0 ** 20))
PI_C = float(TWO_PI - PI_A - PI_B)
PI_LESS = 3.1415925


U_STORES = 16 * 3
B_STORES = 16 * 2 * 2

CONV_BU, CONV_C = (2, 5, 8, 11), (8, 14)
OUTC_BU, OUTC_C = (2, 4, 6, 8), (7, 11)
CONV_TAPS = (4, 13)
CONV_KEEP = (4, 7, 10, 13)
OUTC_KEEP = (4, 6, 8, 10)


class Steps:

    def __init__(self, sem, start=0):
        self.sem, self.base, self.k = sem, start, 0

    def at(self, base):
        self.base, self.k = base, 0

    def mark(self, ins):
        ins.then_inc(self.sem, 1)
        self.k += 1

    def value(self):
        return self.base + self.k


def build(nc, d):
    sb = lambda name, shape, dt=F32: nc.alloc_sbuf_tensor(name, shape, dt)
    sem = nc.alloc_semaphore

    xh = sb("xh", [P, KX, TOK], F32R)
    xl = sb("xl", [P, KX, TOK], F32R)
    w_raw = sb("w_raw", [P, 4, KH * P])
    w_hi = [sb(f"w_hi{i}", [P, KH * P], F32R) for i in range(2)]
    w_lo = [sb(f"w_lo{i}", [P, KH * P], F32R) for i in range(2)]
    conv_par = sb("conv_par", [P, NB, CONV_W])
    mask2 = sb("mask2", [P, 2])
    scan_mask = sb("scan_mask", [P, TOK])
    ones = sb("ones", [P, P])
    sig_table = sb("sig_table", [P, 1])
    ln_par = sb("ln_par", [P, KX, 2])
    last_state = sb("last_state", [P, PAIRS, 2, SCAN_ENDS])
    last_conv = sb("last_conv", [P, NB, SCAN_ENDS, 2])

    base = nc.sbuf_base + (-nc.sbuf_base) % 32
    end = nc.sbuf_usable_end

    class Region:

        def __init__(self, at):
            self.at = at

        def __call__(self, name, shape, dt=F32):
            t = nc.alloc_sbuf_tensor_at(name, shape, dt, offset=self.at)
            self.at += -(-4 * int(np.prod(shape[1:])) // 32) * 32
            assert self.at <= end, (name, self.at, end)
            return t

    c0 = base
    c = Region(c0)
    gated_h = c("gated_h", [P, NB, TOK], F32R)
    gated_l = c("gated_l", [P, NB, TOK], F32R)
    d0 = c.at
    x_raw = Region(c0)("x_raw", [P, KX, TOK])
    r = Region(c0)
    u_stage = [r(f"u_stage{i}", [P, TOK]) for i in range(2)]
    u_hi = [r(f"u_hi{i}", [P, TOK], F32R) for i in range(2)]
    u_lo = [r(f"u_lo{i}", [P, TOK], F32R) for i in range(2)]
    bb = r("bb", [P, NB, 2, STATE])
    bb_hi = r("bb_hi", [P, NB, 2, 2, STATE], F32R)
    bb_lo = r("bb_lo", [P, NB, 2, 2, STATE], F32R)
    assert r.at <= d0
    r_all = Region(c0)("r_all", [P, KX, TOK])

    r = Region(d0)
    rot_all = r("rot_all", [P, PAIRS * ROT_P])
    mag_all = r("mag_all", [P, PAIRS])
    after_setup = r.at

    a_par = r("a_par", [P, 2, SETUP])
    log_dt = r("log_dt", [P, PAIRS + NB])
    b_par = r("b_par", [P, 2, NB * STATE])
    s_dt, s_mag, s_x, s_k, s_f, s_p, s_c, s_s = (r(f"set{i}", [P, SETUP]) for i in range(8))
    s_i = r("s_i", [P, SETUP], I32)
    turn_t = [r(f"turn_t{i}", [P, PAIRS * FINE]) for i in range(2)]
    setup_end = r.at

    r = Region(after_setup)
    table1 = r("table1", [P, 2, TOK])
    bu = [r(f"bu{i}", [P, 2, TOK]) for i in range(2)]
    m1 = r("m1", [P, 2, TOK])
    m2 = r("m2", [P, 2, TOK])
    hst = [r(f"h{i}", [P, 2, TOK]) for i in range(2)]
    rmask = [r(f"rmask{i}", [P, TOK]) for i in range(2)]
    y_tmp = rmask[1]
    y_pre = r("y_pre", [P, TOK])
    mag_blk = r("mag_blk", [P, 4])
    cw = r("cw", [P, 3])
    gate_t = r("gate_t", [P, TOK])
    conv_c = gate_t
    part0 = r.at
    conv_t = r("conv_t", [P, TOK])
    q_pad = r("q_pad", [P, QPAD])
    assert r.at >= setup_end
    table = [r("table0", [P, 2, TOK]), table1]
    t_tmp = r("t_tmp", [P, 2, SEQ])
    u_blk = r("u_blk", [P, TOK])
    u_pair = [r(f"u_pair{i}", [P, TOK], F32R) for i in range(2)]
    b_pair = [r(f"b_pair{i}", [P, 2 * P], F32R) for i in range(2)]
    host_blk = r("host_blk", [P, HOST_W])
    r = Region(part0)
    part_st = [r(f"part_st{i}", [P, TOK]) for i in range(2)]

    r = Region(d0)
    yh = r("yh", [P, NB, TOK], F32R)
    yl = r("yl", [P, NB, TOK], F32R)
    y_in = [r(f"y_in{i}", [P, TOK]) for i in range(2)]
    silu_z = [r(f"silu_z{i}", [P, TOK]) for i in range(4)]
    sig_a = r("sig_a", [P, TOK])
    y_f = r("y_f", [P, TOK])

    r = Region(d0)
    merged = r("merged", [P, KX, TOK])
    part_in = [r(f"part_in{i}", [P, TOK]) for i in range(2)]
    sig_m = r("sig_m", [P, TOK])
    x_in = [r(f"x_in{i}", [P, TOK]) for i in range(2)]
    pivot = r("pivot", [P, TOK])
    acc_d = r("acc_d", [P, TOK])
    acc_q = r("acc_q", [P, TOK])
    sq = [r(f"sq{i}", [P, TOK]) for i in range(2)]
    r = Region(d0)
    mean = r("mean", [P, TOK])
    rstd = r("rstd", [P, TOK])
    mean_r = r("mean_r", [P, TOK])
    o_st = [r(f"o_st{i}", [P, TOK]) for i in range(4)]

    acc = nc.alloc_psum_tensor("acc", [P, 2, 2, 512], F32)
    bu_ps = nc.alloc_psum_tensor("bu_ps", [P, 2, 512], F32)
    y_ps = nc.alloc_psum_tensor("y_ps", [P, 2, 512], F32)

    def halves_of(ps):
        return ps[:, :, 0:TH]

    def two(ap):
        return ap.rearrange("p (t n) -> p t n", t=2)

    u_dram = nc.dram_tensor("u_dram", [NB, P, TOK], F32, kind="Internal").ap()
    u_parts = nc.dram_tensor("u_parts", [NB, 4, 2, 32, TOK], F32, kind="Internal").ap()
    b_parts = nc.dram_tensor("b_parts", [2, NB, P, 2 * P], F32, kind="Internal").ap()
    y_dram = nc.dram_tensor("y_dram", [NB, P, TOK], F32, kind="Internal").ap()
    part_dram = nc.dram_tensor("part_dram", [KX, P, TOK], F32, kind="Internal").ap()

    rot = rot_all[:, :].rearrange("p (b j w) -> p b j w", j=4, w=ROT_P)

    def fine(c, a, b):
        return rot[:, :, :, c * FINE + a:c * FINE + b]

    def coarse(c, a, b):
        return rot[:, :, :, 2 * FINE + c * COARSE + a:2 * FINE + c * COARSE + b]

    raw_loaded = [sem(f"raw_loaded{i}") for i in range(4)]
    hi_ready = sem("hi_ready")
    lo_ready = sem("lo_ready")
    half_done = sem("half_done")
    acc_free = [sem(f"acc_free{i}") for i in range(2)]
    x_loaded = [sem(f"x_loaded{i}") for i in range(7)]
    xh_ready = sem("xh_ready")
    xl_ready = sem("xl_ready")
    par_loaded = sem("par_loaded")
    const_loaded = sem("const_loaded")
    dve_step = sem("dve_step")
    sin_in = sem("sin_in")
    sin_out = sem("sin_out")
    phase_ready = sem("phase_ready")
    u_evac = sem("u_evac")
    u_hi_ready = sem("u_hi_ready")
    u_lo_ready = sem("u_lo_ready")
    bb_ready = sem("bb_ready")
    bb_hi_ready = sem("bb_hi_ready")
    bb_lo_ready = sem("bb_lo_ready")
    b_stored = sem("b_stored")
    pair_loaded = [sem(f"pair_loaded{i}") for i in range(2)]
    u_stored = [sem(f"u_stored{i}") for i in range(2)]
    mag_ready = sem("mag_ready")
    blk_loaded = sem("blk_loaded")
    y_read = sem("y_read")
    table_ready = sem("table_ready")
    table_free = sem("table_free")
    rmask_ready = sem("rmask_ready")
    c_ready = sem("c_ready")
    bu_done = sem("bu_done")
    bu_evac = sem("bu_evac")
    prod1_ready = sem("prod1_ready")
    v_ready = sem("v_ready")
    prod2_ready = sem("prod2_ready")
    h_ready = sem("h_ready")
    h_used = sem("h_used")
    h_kept = sem("h_kept")
    y_arg = sem("y_arg")
    y_sig = sem("y_sig")
    y_made = sem("y_made")
    y_stored = sem("y_stored")
    cc_ready = sem("cc_ready")
    q_read = sem("q_read")
    z_sig = sem("z_sig")
    yc_ready = sem("yc_ready")
    gh_ready = sem("gh_ready")
    gl_ready = sem("gl_ready")
    g_sig = sem("g_sig")
    part_made = sem("part_made")
    part_stored = [sem(f"part_stored{i}") for i in range(2)]
    y_loaded = [sem(f"y_loaded{i}") for i in range(2)]
    yh_ready = sem("yh_ready")
    yl_ready = sem("yl_ready")
    za_sig = sem("za_sig")
    glu_sig = sem("glu_sig")
    ya_ready = sem("ya_ready")
    part_loaded = [sem(f"part_loaded{i}") for i in range(2)]
    merged_ready = sem("merged_ready")
    ga_sig = sem("ga_sig")
    xin_loaded = [sem(f"xin_loaded{i}") for i in range(2)]
    r_ready = sem("r_ready")
    pivot_sum = sem("pivot_sum")
    pivot_ready = sem("pivot_ready")
    d_ready = sem("d_ready")
    sq_ready = sem("sq_ready")
    sums_ready = sem("sums_ready")
    sums_done = sem("sums_done")
    mean_ready = sem("mean_ready")
    var_ready = sem("var_ready")
    std_ready = sem("std_ready")
    rstd_ready = sem("rstd_ready")
    norm_dve = sem("norm_dve")
    norm_pool = sem("norm_pool")
    out_ready = sem("out_ready")
    out_stored = [sem(f"out_stored{i}") for i in range(4)]
    small_stored = sem("small_stored")
    ones_ready = sem("ones_ready")
    conv_last = sem("conv_last")

    def load_half(sp, h, slot, first=False):
        src = d["w"][h]
        if not first:
            v = sp.snap(h - 3) if not isinstance(h, int) else h - 3
            sp.wait_ge(lo_ready, v)
        sp.dma_start(w_raw[:, slot, :], src).then_inc(raw_loaded[slot], 16)

    block = nc.Block()
    blk = block.__enter__()

    @blk.sync
    def _(sp):
        for k in range(4):
            sp.dma_start(x_raw[:, k, :], d["xT"][k]).then_inc(x_loaded[k], 16)
            if k == 0:
                load_half(sp, 0, 0, True)
        for k in range(1, 4):
            sp.dma_start(x_raw[:, 4 * k:4 * k + 4, :],
                         d["xT"][4 * k:4 * k + 4].rearrange("k p n -> p k n")).then_inc(x_loaded[3 + k], 16)
            load_half(sp, k, k, True)
        sp.dma_start(log_dt[:, :], d["log_dt"]).then_inc(par_loaded, 16)
        sp.dma_start(a_par[:, :, :], d["a_par"]).then_inc(par_loaded, 16)
        sp.dma_start(b_par[:, :, :], d["b_par"]).then_inc(par_loaded, 16)
        sp.dma_start(conv_par[:, :, :], d["conv_par"]).then_inc(const_loaded, 16)
        sp.dma_start(mask2[:, :], d["mask2"]).then_inc(const_loaded, 16)
        sp.dma_start(scan_mask[:, :], d["scan_mask"]).then_inc(const_loaded, 16)
        sp.dma_start(ln_par[:, :, :], d["ln_par"]).then_inc(const_loaded, 16)

        def phase_u(i, last):
            for l in range(4):
                load_half(sp, i * 4 + (H_U + l + 4), l)
                if l >= 2:
                    s = l - 2
                    dst = u_dram[i * 2 + s]
                    v = sp.snap(i * 2 + (s + 1)) if not last else i * 2 + s + 1
                    sp.wait_ge(u_evac, v)
                    sp.dma_start(dst, u_stage[s][:, :]).then_inc(u_stored[s], 16)
                    parts = [u_parts[i * 2 + s, :, part] for part in range(2)]
                    sp.wait_ge(u_hi_ready, v)
                    sp.dma_start(parts[0], u_hi[s][:, :].bitcast(F32)).then_inc(u_stored[s], 16)
                    sp.wait_ge(u_lo_ready, v)
                    sp.dma_start(parts[1], u_lo[s][:, :].bitcast(F32)).then_inc(u_stored[s], 16)
        with sp.Fori(0, NB // 2 - 1) as i:
            phase_u(i, False)

        def as_y(tile, t):
            return two(tile[64 * t:64 * t + 64, :])

        def of_y(dram, t):
            return dram.rearrange("(q r) n -> r q n", q=2)[:, :, t * TH:(t + 1) * TH]

        def load_block(b):
            a = (d["host_blk"][b], u_dram[b])
            v = sp.snap(b + 1) if not isinstance(b, int) else b + 1
            sp.wait_ge(y_read, v)
            sp.dma_start(host_blk[:, :], a[0]).then_inc(blk_loaded, 16)
            for t in range(2):
                sp.dma_start(as_y(u_blk, t), of_y(a[1], t)).then_inc(blk_loaded, 16)

        def store_y(b):
            dst = y_dram[b]
            v = sp.snap(b + 1) if not isinstance(b, int) else b + 1
            sp.wait_ge(y_made, v)
            for t in range(2):
                sp.dma_start(of_y(dst, t), as_y(y_pre, t)).then_inc(y_stored, 16)

        def load_pair(b, j):
            a = (u_parts[b, j].unsqueeze(0).to_broadcast([2, 2, 32, TOK]),
                 *(b_parts[part, b, 32 * j:32 * j + 32].unsqueeze(0).to_broadcast([2, 32, 2 * P]) for part in range(2)))
            to = (u_pair[j % 2][:, :], *(b_pair[j % 2][64 * part:64 * part + 64, :] for part in range(2)))
            if isinstance(b, int):
                if b * 4 + j >= 2:
                    sp.wait_ge(bu_done, (b * 4 + j) * 2 - 2)
            else:
                sp.wait_ge(bu_done, sp.snap(b * 8 + (2 * j - 2)))
            for dst, src in zip(to, a):
                sp.dma_start(dst.bitcast(F32), src).then_inc(pair_loaded[j % 2], 16)

        sp.wait_ge(u_stored[0], U_STORES)
        load_block(0)
        phase_u(NB // 2 - 1, True)
        sp.wait_ge(const_loaded, 64)
        for part, (src, ready) in enumerate(((bb_hi, bb_hi_ready), (bb_lo, bb_lo_ready))):
            sp.wait_ge(ready, 2)
            sp.dma_start(b_parts[part, 0], src[:, 0].rearrange("p c g n -> p (c g n)").bitcast(F32))\
              .then_inc(b_stored, 16)
        sp.wait_ge(b_stored, 16 * 2)
        load_pair(0, 0)
        load_pair(0, 1)
        for part, src in enumerate((bb_hi, bb_lo)):
            sp.dma_start(b_parts[part, 1:].rearrange("b p n -> p b n"),
                         src[:, 1:].rearrange("p b c g n -> p b (c g n)").bitcast(F32)).then_inc(b_stored, 16)
        for s in range(2):
            sp.wait_ge(u_stored[s], U_STORES * NB // 2)
        with sp.Fori(0, 4) as i:
            for l in range(16):
                load_half(sp, i * 16 + (H_CONV + l + 4), l % 4)
                if l - 1 in CONV_BU:
                    j = CONV_BU.index(l - 1) + 2
                    if j == 4:
                        sp.wait_ge(b_stored, B_STORES)
                    load_pair(i + j // 4, j % 4)
            load_block(i + 1)
            store_y(i)

        def phase_outc(i, last):
            for l in range(12):
                load_half(sp, i * 12 + (H_OUTC + l + 4), l % 4)
                if l - 1 in OUTC_BU:
                    j = OUTC_BU.index(l - 1) + 2
                    if not (last and j >= 4):
                        load_pair(i + (4 + j // 4), j % 4)
                if l == 11 and not last:
                    load_block(i + 5)
                if l % 3 == 2:
                    m = l // 3
                    dst = part_dram[i * 4 + m]
                    v = sp.snap(i * 4 + (m + 1)) if not last else i * 4 + m + 1
                    sp.wait_ge(part_made, v)
                    sp.dma_start(dst, part_st[m % 2][:, :]).then_inc(part_stored[m % 2], 16)
            store_y(i + 4)
        with sp.Fori(0, 3) as i:
            phase_outc(i, False)
        phase_outc(3, True)
        sp.wait_ge(y_stored, 32 * NB + 32)
        for s in range(2):
            sp.wait_ge(part_stored[s], 16 * KX // 2 + 16)

        for s in range(2):
            sp.dma_start(y_in[s][:, :], y_dram[s]).then_inc(y_loaded[s], 16)
        for i in range(2):
            for l in range(12):
                load_half(sp, i * 12 + (H_GLU + l + 4), l % 4)
                if i == 0 and l < NB - 2:
                    sp.wait_ge(yl_ready, l + 1)
                    sp.dma_start(y_in[l % 2][:, :], y_dram[l + 2]).then_inc(y_loaded[l % 2], 16)

        sp.wait_ge(gl_ready, 2 * NB)
        for s in range(2):
            sp.dma_start(part_in[s][:, :], part_dram[s]).then_inc(part_loaded[s], 16)

        def phase_outa(i, last):
            for l in range(12):
                load_half(sp, i * 12 + (H_OUTA + l + 4), l % 4)
                if l % 3 == 2:
                    m = l // 3
                    if last and m >= 2:
                        continue
                    src = part_dram[i * 4 + (m + 2)]
                    v = sp.snap(i * 4 + (m + 1)) if not last else i * 4 + m + 1
                    sp.wait_ge(merged_ready, v)
                    sp.dma_start(part_in[m % 2][:, :], src).then_inc(part_loaded[m % 2], 16)
        with sp.Fori(0, 3) as i:
            phase_outa(i, False)
        phase_outa(3, True)

        for s in range(2):
            sp.dma_start(x_in[s][:, :], d["xT"][s]).then_inc(xin_loaded[s], 16)

        def phase_o(i, last):
            for l in range(4):
                if not last:
                    load_half(sp, i * 4 + (H_O + l + 4), l)
                if l >= 2 and not last:
                    s = l - 2
                    src = d["xT"][i * 2 + (s + 2)]
                    v = sp.snap(i * 2 + (s + 1))
                    sp.wait_ge(r_ready, v)
                    sp.dma_start(x_in[s][:, :], src).then_inc(xin_loaded[s], 16)
        with sp.Fori(0, KX // 2 - 1) as i:
            phase_o(i, False)
        phase_o(KX // 2 - 1, True)

        sp.wait_ge(h_kept, 2 + PAIRS)
        sp.dma_start(d["out_state"], last_state[:, :, :, :]).then_inc(small_stored, 16)
        sp.wait_ge(conv_last, 2 * NB + 2)
        sp.dma_start(d["out_conv"], last_conv[:, :, :, :]).then_inc(small_stored, 16)
        for n in range(KX):
            sp.wait_ge(out_ready, n + 1)
            sp.dma_start(d["outT"][n], o_st[n % 4][:, :]).then_inc(out_stored[n % 4], 16)
        sp.wait_ge(small_stored, 32)
        for s in range(4):
            sp.wait_ge(out_stored[s], 16 * KX // 4)

    @blk.tensor
    def _(pe):
        def half(h, slot, par, mh, ml, k0, first, last, mid=None, per_block=None):
            pe.wait_ge(lo_ready, h + 1)
            s = slot % 2
            for k in range(KH):
                if k == KH // 2 and mid is not None:
                    mid()
                if per_block is not None:
                    per_block(k0 + k)
                wh = w_hi[s][:, k * P:(k + 1) * P]
                wl = w_lo[s][:, k * P:(k + 1) * P]
                for n, (w, m) in enumerate(((wh, mh), (wh, ml), (wl, mh))):
                    for t in range(2):
                        ins = pe.matmul(acc[:, par, t, 0:TH], w, m[:, k0 + k, t * TH:(t + 1) * TH],
                                        start=first and k == 0 and n == 0,
                                        stop=last and k == KH - 1 and n == 2)
            ins.then_inc(half_done, 1)

        def fresh(par, n):
            pe.wait_ge(acc_free[par], n)

        def x_there(k):
            pe.wait_ge(xl_ready, k + 1)

        def phase_u(i, head):
            for l in range(4):
                if l < 2 and not head:
                    fresh(l, i)
                half(i * 4 + (H_U + l), l, l % 2, xh, xl, (l // 2) * KH, l < 2, l >= 2,
                     per_block=x_there if head and l % 2 == 0 else None)
        phase_u(0, True)
        with pe.Fori(1, NB // 2) as i:
            phase_u(i, False)

        def bu_part(b, j, c):
            p = b * 4 + j
            if c == 0:
                pe.wait_ge(pair_loaded[j % 2], b * 96 + 48 * (j // 2 + 1))
            pe.wait_ge(bu_evac, p * 2 + (c + 1))
            for t in range(2):
                ins = pe.matmul(bu_ps[:, t, 0:TH], b_pair[j % 2][:, c * P:(c + 1) * P], u_pair[j % 2][:, t * TH:(t + 1) * TH],
                                start=True, stop=True)
            ins.then_inc(bu_done, 1)

        def c_part(p, b, j):
            if j == 0:
                pe.wait_ge(c_ready, b + 1)
                pe.wait_ge(y_read, b + 1)
            pe.wait_ge(h_ready, p * 2 + 7)
            for c in range(2):
                for t in range(2):
                    for jj in (j, j + 1):
                        q = 32 * (2 * t + jj - j)
                        ins = pe.matmul(y_ps[q:q + 32, j // 2, 0:TH],
                                        host_blk[:, (2 * jj + c) * 32:(2 * jj + c) * 32 + 32],
                                        hst[jj % 2][:, c, t * TH:(t + 1) * TH], start=c == 0, stop=c == 1)
                        if t == 1 and c == 1:
                            ins.then_inc(h_used, 1)

        with pe.Fori(0, 4) as b:
            for l in range(16):
                if l in CONV_BU:
                    j = CONV_BU.index(l)
                    bu_part(b, j, 0)
                    mid = lambda j=j: bu_part(b, j, 1)
                else:
                    mid = None
                if l in CONV_C:
                    j = 2 * CONV_C.index(l)
                    c_part(b * 4 + j, b, j)
                par = (l // 2) % 2
                if l % 2 == 0:
                    fresh(par, b * 4 + (S_CONV // 2 + l // 4))
                half(b * 16 + (H_CONV + l), l, par, xh, xl, (l % 2) * KH, l % 2 == 0, l % 2 == 1, mid)

        with pe.Fori(0, 4) as i:
            for l in range(12):
                m, part = l // 3, l % 3
                if l in OUTC_BU:
                    j = OUTC_BU.index(l)
                    bu_part(i + 4, j, 0)
                    mid = lambda j=j: bu_part(i + 4, j, 1)
                else:
                    mid = None
                if l in OUTC_C:
                    j = 2 * OUTC_C.index(l)
                    c_part(i * 4 + (16 + j), i + 4, j)
                if part != 1:
                    fresh(part // 2, i * 4 + (S_OUTC // 2 + m))
                if part < 2:
                    half(i * 12 + (H_OUTC + l), l, 0, xh, xl, part * KH, part == 0, part == 1, mid)
                else:
                    if m == 0:
                        pe.wait_ge(gl_ready, NB)
                    half(i * 12 + (H_OUTC + l), l, 1, gated_h, gated_l, 0, True, True, mid)

        with pe.Fori(0, 2) as i:
            for l in range(12):
                h = i * 12 + (H_GLU + l)
                if l < 8:
                    n = l // 2
                    if l % 2 == 0:
                        fresh(n % 2, i * 4 + (S_GLU // 2 + n // 2))
                    half(h, l, n % 2, xh, xl, (l % 2) * KH, l % 2 == 0, l % 2 == 1)
                else:
                    n = l - 8
                    fresh(n % 2, i * 4 + (S_GLU // 2 + 2 + n // 2))
                    if n == 0:
                        pe.wait_ge(yl_ready, NB)
                    half(h, l, n % 2, yh, yl, 0, True, True)

        with pe.Fori(0, 4) as i:
            for l in range(12):
                m, part = l // 3, l % 3
                if part != 1:
                    fresh(part // 2, i * 4 + (S_OUTA // 2 + m))
                if part < 2:
                    half(i * 12 + (H_OUTA + l), l, 0, xh, xl, part * KH, part == 0, part == 1)
                else:
                    if m == 0:
                        pe.wait_ge(gl_ready, 2 * NB)
                    half(i * 12 + (H_OUTA + l), l, 1, gated_h, gated_l, 0, True, True)

        def merged_there(k):
            pe.wait_ge(xl_ready, KX + k + 1)

        def sum_features(ps, src):
            for t in range(2):
                ins = pe.matmul(ps[:, t, 0:TH], ones[:, :], src[:, t * TH:(t + 1) * TH], start=True, stop=True)
            return ins

        def sum_pivot():
            pe.wait_ge(ones_ready, 1)
            pe.wait_ge(r_ready, 1)
            sum_features(bu_ps, r_all[:, 0, :]).then_inc(pivot_sum, 1)

        def phase_o(i, head):
            for l in range(4):
                if l < 2:
                    fresh(l, i + S_O // 2)
                half(i * 4 + (H_O + l), l, l % 2, xh, xl, (l // 2) * KH, l < 2, l >= 2,
                     mid=sum_pivot if head and l == 3 else None,
                     per_block=merged_there if head and l % 2 == 0 else None)
        phase_o(0, True)
        with pe.Fori(1, KX // 2) as i:
            phase_o(i, False)
        pe.wait_ge(sums_ready, 1)
        pe.wait_ge(pivot_ready, 1)
        sum_features(bu_ps, acc_d).then_inc(sums_done, 1)
        pe.wait_ge(sums_ready, 2)
        sum_features(y_ps, acc_q).then_inc(sums_done, 1)

    @blk.scalar
    def _(act):
        act.sem_inc(bu_evac, 1)
        act.sem_inc(h_kept, 2)

        def split(h, slot, n, first=False):
            if first:
                act.wait_ge(raw_loaded[slot], 16)
            else:
                act.wait_ge(raw_loaded[slot], n * 16)
            if not (isinstance(h, int) and h < 2):
                act.wait_ge(half_done, h - 1)
            act.activation(w_hi[slot % 2][:, :], w_raw[:, slot, :], ACT.Copy).then_inc(hi_ready, 1)

        def split_next(i, per, h0, l):
            n = h0 + l + 1
            split(i * per + n, n % 4, i * (per // 4) + (n // 4 + 1))

        def x_high(k):
            act.wait_ge(x_loaded[k if k < 4 else 3 + k // 4], 16)
            act.activation(xh[:, k, :], x_raw[:, k, :], ACT.Copy).then_inc(xh_ready, 1)
        x_high(0)
        split(0, 0, 1, True)
        for k in range(1, KH):
            x_high(k)

        def phase_u(i, head, sines=False, b_high=False):
            for l in range(4):
                split_next(i, 4, H_U, l)
                if head and l < 2:
                    for k in range(4):
                        x_high(KH + 4 * l + k)
                if sines and l == 1:
                    act.wait_ge(sin_in, 1)
                    act.activation(s_s[:, :], s_x[:, :], ACT.Sin).then_inc(sin_out, 1)
                    act.activation(s_c[:, :], s_x[:, :], ACT.Sin, scale=0.5).then_inc(sin_out, 1)
                if b_high and l == 1:
                    act.wait_ge(const_loaded, 64)
                    act.activation(sig_table[:, :], mask2[:, 0:1], ACT.Sigmoid)
                    act.wait_ge(bb_ready, 2)
                    for g in range(2):
                        act.activation(bb_hi[:, :, :, g, :], bb[:, :, :, :], ACT.Copy,
                                       scale=mask2[:, g:g + 1]).then_inc(bb_hi_ready, 1)
                if l >= 2:
                    s = l - 2
                    act.wait_ge(half_done, i * 4 + (l + 1))
                    if head:
                        act.wait_ge(xl_ready, KX)
                    else:
                        act.wait_ge(u_stored[s], i * U_STORES)
                    act.activation(two(u_stage[s][:, :]), halves_of(acc[:, s]), ACT.Copy)\
                       .then_inc(u_evac, 1)
                    act.wait_ge(u_evac, i * 2 + (s + 1))
                    act.sem_inc(acc_free[s], 1)
                    act.activation(u_hi[s][:, :], u_stage[s][:, :], ACT.Copy).then_inc(u_hi_ready, 1)
        phase_u(0, True)
        phase_u(1, False, True)
        phase_u(2, False)
        phase_u(3, False, b_high=True)

        def decay(p, j):
            act.wait_ge(table_free, p + 1)
            act.activation(rmask[j % 2][:, :], scan_mask[:, :], ACT.Copy,
                           scale=mag_blk[:, j:j + 1]).then_inc(rmask_ready, 1)

        def evac_bu(p, j, c):
            act.wait_ge(bu_done, p * 2 + (c + 1))
            if c == 0:
                act.wait_ge(h_ready, p * 2 + 1)
            act.activation(two(bu[j % 2][:, c, :]), halves_of(bu_ps), ACT.Copy).then_inc(bu_evac, 1)

        def keep_states(p, j):
            act.wait_ge(h_ready, p * 2 + 5)
            act.activation(last_state[:, p, :, 0:1], hst[j % 2][:, :, SEQ - 1:SEQ], ACT.Copy)
            act.activation(last_state[:, p, :, 1:], hst[j % 2][:, :, SEQ + DEC_T - 1:TOK:DEC_T], ACT.Copy)\
               .then_inc(h_kept, 1)

        def keep_conv(cb):
            act.wait_ge(q_read, cb + 2)
            act.activation(last_conv[:, cb, 0, :], q_pad[:, SEQ:SEQ + 2], ACT.Copy).then_inc(conv_last, 1)
            qs = q_pad[:, SEQ + 2:QPAD].rearrange("p (b t) -> p b t", b=DEC_B)
            act.activation(last_conv[:, cb, 1:, :], qs[:, :, DEC_T:], ACT.Copy).then_inc(conv_last, 1)

        def conv_high(b, q):
            if q == 0:
                for s in range(2):
                    act.wait_ge(u_stored[s], U_STORES * NB // 2)
                act.wait_ge(b_stored, B_STORES)
            act.wait_ge(yc_ready, b * 2 + (q + 1))
            act.activation(gated_h[:, b * 2 + q, :], conv_t[:, :], ACT.Copy).then_inc(gh_ready, 1)

        def gelu_act(b):
            act.wait_ge(y_arg, b + 1)
            act.activation(y_tmp[:, :], y_tmp[:, :], ACT.Sigmoid, scale=GELU_S).then_inc(y_sig, 1)

        with act.Fori(0, 4) as b:
            for l in range(16):
                split_next(b, 16, H_CONV, l)
                if l + 1 in CONV_BU:
                    j = CONV_BU.index(l + 1)
                    if j == 0:
                        act.wait_ge(mag_ready, b + 1)
                    decay(b * 4 + j, j)
                if l in CONV_BU:
                    j = CONV_BU.index(l)
                    for c_ in range(2):
                        evac_bu(b * 4 + j, j, c_)
                if l == 8:
                    conv_high(b, 0)
                if l in CONV_KEEP:
                    j = CONV_KEEP.index(l)
                    keep_states(b * 4 + j, j)
                if l % 8 == 1:
                    act.wait_ge(half_done, b * 16 + (H_CONV + l + 1))
                    act.wait_ge(q_read, b * 2 + (l // 8 + 1))
                    act.activation(two(conv_c[:, :]), halves_of(acc[:, 0]), ACT.Copy).then_inc(cc_ready, 1)
                    act.wait_ge(cc_ready, b * 2 + (l // 8 + 1))
                    act.sem_inc(acc_free[0], 1)
                if l % 8 == 5:
                    keep_conv(b * 2 + l // 8)
                if l == CONV_C[1]:
                    gelu_act(b)
                if l % 8 == 7:
                    q = l // 8
                    act.wait_ge(half_done, b * 16 + (H_CONV + l + 1))
                    act.activation(two(gate_t[:, :]), halves_of(acc[:, 1]), ACT.Sigmoid).then_inc(z_sig, 1)
                    if q == 1:
                        conv_high(b, 1)

        with act.Fori(0, 4) as i:
            for l in range(12):
                m = l // 3
                split_next(i, 12, H_OUTC, l)
                if l + 1 in OUTC_BU:
                    j = OUTC_BU.index(l + 1)
                    if j == 0:
                        act.wait_ge(mag_ready, i + 5)
                    decay(i * 4 + (16 + j), j)
                if l in OUTC_BU:
                    j = OUTC_BU.index(l)
                    for c_ in range(2):
                        evac_bu(i * 4 + (16 + j), j, c_)
                if l in OUTC_KEEP:
                    j = OUTC_KEEP.index(l)
                    keep_states(i * 4 + (16 + j), j)
                if l % 3 == 1:
                    act.wait_ge(half_done, i * 12 + (H_OUTC + l + 1))
                    act.wait_ge(part_made, i * 4 + m) if m else act.wait_ge(gl_ready, NB)
                    if m == 0:
                        act.wait_ge(acc_free[1], i * 4 + S_OUTC // 2)
                    act.activation(two(gate_t[:, :]), halves_of(acc[:, 0]), ACT.Sigmoid).then_inc(g_sig, 1)
                    act.wait_ge(g_sig, i * 4 + (m + 1))
                    act.sem_inc(acc_free[0], 1)
                if l == OUTC_C[1]:
                    gelu_act(i + 4)

        for i in range(2):
            for l in range(12):
                split_next(i, 12, H_GLU, l)
                if i == 0 and l < NB:
                    act.wait_ge(y_loaded[l % 2], 16 * (l // 2 + 1))
                    act.activation(yh[:, l, :], y_in[l % 2][:, :], ACT.Copy).then_inc(yh_ready, 1)
                if l < 8 and l % 2:
                    n = l // 2
                    act.wait_ge(half_done, i * 12 + (H_GLU + l + 1))
                    if i:
                        act.wait_ge(gl_ready, NB + n + 1)
                    act.activation(two(silu_z[n][:, :]), halves_of(acc[:, n % 2]), ACT.Sigmoid)\
                       .then_inc(za_sig, 1)
                if l >= 8:
                    n = l - 8
                    act.wait_ge(half_done, i * 12 + (H_GLU + l + 1))
                    act.activation(two(sig_a[:, :]), halves_of(acc[:, n % 2]), ACT.Sigmoid)\
                       .then_inc(glu_sig, 1)
                    act.wait_ge(glu_sig, i * 4 + (n + 1))
                    act.sem_inc(acc_free[n % 2], 1)
                    act.wait_ge(ya_ready, i * 4 + (n + 1))
                    act.activation(gated_h[:, i * 4 + n, :], y_f[:, :], ACT.Copy).then_inc(gh_ready, 1)
        act.wait_ge(gl_ready, 2 * NB)
        def merged_high(k):
            act.wait_ge(merged_ready, k + 1)
            act.activation(xh[:, k, :], merged[:, k, :], ACT.Copy).then_inc(xh_ready, 1)

        def phase_outa(i, last):
            for l in range(12):
                m = l // 3
                split_next(i, 12, H_OUTA, l)
                if l % 3 == 1:
                    act.wait_ge(half_done, i * 12 + (H_OUTA + l + 1))
                    if m:
                        act.wait_ge(merged_ready, i * 4 + m)
                    else:
                        act.wait_ge(acc_free[1], i * 4 + S_OUTA // 2)
                    act.activation(two(sig_m[:, :]), halves_of(acc[:, 0]), ACT.Sigmoid).then_inc(ga_sig, 1)
                    act.wait_ge(ga_sig, i * 4 + (m + 1))
                    act.sem_inc(acc_free[0], 1)
            if last:
                act.wait_ge(half_done, H_OUTA + 3 * KX - 1)
                for k in range(6):
                    merged_high(k)
        with act.Fori(0, 3) as i:
            phase_outa(i, False)
        phase_outa(3, True)

        def square(n, s):
            act.wait_ge(d_ready, n + 1)
            act.activation(sq[s][:, :], r_all[:, n, :], ACT.Square).then_inc(sq_ready, 1)

        def phase_o(i, head, last):
            for l in range(4):
                if not (last and l == 3):
                    split_next(i, 4, H_O, l)
                if head and l < 3:
                    for k in range(6 + 4 * l, min(10 + 4 * l, KX)):
                        merged_high(k)
                if head and l == 3:
                    act.wait_ge(pivot_sum, 1)
                    act.activation(two(pivot[:, :]), halves_of(bu_ps), ACT.Copy, scale=1.0 / P)\
                       .then_inc(pivot_ready, 1)
                    square(0, 0)
                if l == 3 or (l == 2 and not head):
                    square(i * 2 + (l - 2), l - 2)
        phase_o(0, True, False)
        with act.Fori(1, KX // 2 - 1) as i:
            phase_o(i, False, False)
        phase_o(KX // 2 - 1, False, True)

        act.wait_ge(sums_done, 1)
        act.activation(two(mean[:, :]), halves_of(bu_ps), ACT.Copy, scale=1.0 / D_MODEL).then_inc(mean_ready, 1)
        act.wait_ge(var_ready, 1)
        act.activation(rstd[:, :], rstd[:, :], ACT.Sqrt).then_inc(std_ready, 1)
        for n in range(KX):
            if n in POOL_BLOCKS:
                act.wait_ge(norm_pool, POOL_BLOCKS.index(n) + 1)
            else:
                act.wait_ge(norm_dve, DVE_BLOCKS.index(n) + 1)
            if n >= 4:
                act.wait_ge(out_stored[n % 4], 16 * (n // 4))
            act.activation(o_st[n % 4][:, :], r_all[:, n, :], ACT.Identity, scale=ln_par[:, n, 0:1],
                           bias=ln_par[:, n, 1:2]).then_inc(out_ready, 1)

    @blk.vector
    def _(dve):
        own = Steps(dve_step)

        def link(ins):
            own.mark(ins)
            dve.wait_ge(dve_step, own.value())

        def mark(ins):
            own.mark(ins)

        def split(h, slot):
            dve.wait_ge(hi_ready, h + 1)
            dve.tensor_tensor(w_lo[slot % 2][:, :], w_raw[:, slot, :], w_hi[slot % 2][:, :].bitcast(F32),
                              ALU.subtract).then_inc(lo_ready, 1)

        def split_next(i, per, h0, l):
            n = h0 + l + 1
            split(i * per + n, n % 4)

        dve.sem_inc(y_read, 1)
        dve.sem_inc(table_free, 2)
        dve.sem_inc(q_read, 1)
        dve.sem_inc(y_stored, 32)
        dve.sem_inc(conv_last, 2)
        for s in range(2):
            dve.sem_inc(part_stored[s], 16)

        def x_low(k):
            dve.wait_ge(xh_ready, k + 1)
            dve.tensor_tensor(xl[:, k, :], x_raw[:, k, :], xh[:, k, :].bitcast(F32), ALU.subtract)\
               .then_inc(xl_ready, 1)
        x_low(0)
        split(0, 0)
        for k in range(1, KH):
            x_low(k)

        A_RE, A_IM = a_par[:, 0, :], a_par[:, 1, :]

        def exp_reduce(x, n):
            link(dve.tensor_scalar(s_k[:, 0:n], x, LOG2E, None, ALU.mult))
            link(dve.tensor_scalar(s_k[:, 0:n], s_k[:, 0:n], MAGIC, None, ALU.add))
            link(dve.tensor_scalar(s_k[:, 0:n], s_k[:, 0:n], MAGIC, None, ALU.subtract))
            link(dve.scalar_tensor_tensor(s_f[:, 0:n], s_k[:, 0:n], -LN2_HI, x, ALU.mult, ALU.add))
            link(dve.scalar_tensor_tensor(s_f[:, 0:n], s_k[:, 0:n], -LN2_LO, s_f[:, 0:n], ALU.mult, ALU.add))

        def exp_series(n):
            link(dve.tensor_scalar(s_p[:, 0:n], s_f[:, 0:n], 1.0 / 5040, None, ALU.mult))
            for m in (720, 120, 24, 6, 2, 1):
                link(dve.scalar_tensor_tensor(s_p[:, 0:n], s_p[:, 0:n], 1.0 / m, s_f[:, 0:n], ALU.add, ALU.mult))

        def exp_scale(out, n):
            link(dve.tensor_scalar(s_k[:, 0:n], s_k[:, 0:n], 127.0, None, ALU.add))
            link(dve.tensor_scalar(s_k[:, 0:n], s_k[:, 0:n], 0.0, 255.0, ALU.max, ALU.min))
            link(dve.tensor_copy(s_i[:, 0:n], s_k[:, 0:n]))
            link(dve.tensor_scalar(s_i[:, 0:n], s_i[:, 0:n], 23, None, ALU.logical_shift_left))
            link(dve.scalar_tensor_tensor(out, s_p[:, 0:n], 1.0, s_i[:, 0:n].bitcast(F32), ALU.add, ALU.mult))

        def spread_dt():
            link(dve.tensor_copy(s_dt[:, 0:PAIRS], log_dt[:, 0:PAIRS]))
            link(dve.tensor_copy(s_dt[:, PAIRS:].rearrange("p (b s) -> p b s", b=NB),
                                 log_dt[:, PAIRS:].unsqueeze(2).to_broadcast([P, NB, STATE])))

        def angles():
            link(dve.tensor_tensor(s_x[:, :], A_IM, s_dt[:, :], ALU.mult))
            link(dve.tensor_scalar(s_k[:, :], s_x[:, :], 1.0 / TWO_PI, None, ALU.mult))
            link(dve.tensor_scalar(s_k[:, :], s_k[:, :], MAGIC, None, ALU.add))
            link(dve.tensor_scalar(s_k[:, :], s_k[:, :], MAGIC, None, ALU.subtract))
            for part in (PI_A, PI_B, PI_C):
                link(dve.scalar_tensor_tensor(s_x[:, :], s_k[:, :], -part, s_x[:, :], ALU.mult, ALU.add))
            dve.tensor_scalar(s_x[:, :], s_x[:, :], -PI_LESS, PI_LESS, ALU.max, ALU.min).then_inc(sin_in, 1)

        def phase_and_lam():
            dve.wait_ge(sin_out, 2)
            link(dve.tensor_tensor(s_c[:, :], s_c[:, :], s_c[:, :], ALU.mult))
            link(dve.tensor_scalar(s_c[:, :], s_c[:, :], -2.0, 1.0, ALU.mult, ALU.add))
            st = slice(0, PAIRS)
            link(dve.tensor_tensor(s_f[:, st], s_c[:, st], s_c[:, st], ALU.mult))
            link(dve.tensor_tensor(s_p[:, st], s_s[:, st], s_s[:, st], ALU.mult))
            link(dve.tensor_tensor(s_f[:, st], s_f[:, st], s_p[:, st], ALU.add))
            link(dve.tensor_scalar(s_f[:, st], s_f[:, st], -0.5, 1.5, ALU.mult, ALU.add))
            link(dve.tensor_tensor(fine(0, 0, 1), s_c[:, st].rearrange("p (b j) -> p b j", j=4).unsqueeze(3),
                                   s_f[:, st].rearrange("p (b j) -> p b j", j=4).unsqueeze(3), ALU.mult))
            link(dve.tensor_tensor(fine(1, 0, 1), s_s[:, st].rearrange("p (b j) -> p b j", j=4).unsqueeze(3),
                                   s_f[:, st].rearrange("p (b j) -> p b j", j=4).unsqueeze(3), ALU.mult))
            dve.sem_inc(phase_ready, 1)
            link(dve.tensor_copy(mag_all[:, :], s_mag[:, st]))

        ch = slice(PAIRS, SETUP)
        a_re, a_im = A_RE[:, ch], A_IM[:, ch]
        q_re, q_im, w0, w1 = s_s[:, ch], s_c[:, ch], s_mag[:, ch], s_dt[:, ch]

        def zoh_lam():
            link(dve.tensor_tensor(w1, s_mag[:, ch], s_s[:, ch], ALU.mult))
            link(dve.tensor_tensor(w0, s_mag[:, ch], s_c[:, ch], ALU.mult))
            link(dve.tensor_scalar(w0, w0, 1.0, None, ALU.subtract))
            link(dve.tensor_tensor(s_f[:, ch], a_re, a_re, ALU.mult))
            link(dve.tensor_tensor(s_p[:, ch], a_im, a_im, ALU.mult))
            link(dve.tensor_tensor(s_f[:, ch], s_f[:, ch], s_p[:, ch], ALU.add))

        def zoh_abs():
            link(dve.reciprocal(s_f[:, ch], s_f[:, ch]))

        def zoh_q(q, x, y, op):
            link(dve.tensor_tensor(q, x, a_re, ALU.mult))
            link(dve.tensor_tensor(s_p[:, ch], y, a_im, ALU.mult))
            link(dve.tensor_tensor(q, q, s_p[:, ch], op))
            link(dve.tensor_tensor(q, q, s_f[:, ch], ALU.mult))

        def zoh_b():
            blocks = lambda x: x.rearrange("p (b s) -> p b s", b=NB)
            for c, (qa, qb, op) in enumerate(((q_re, q_im, ALU.subtract), (q_im, q_re, ALU.add))):
                link(dve.tensor_tensor(w0, qa, b_par[:, 0, :], ALU.mult))
                link(dve.tensor_tensor(w1, qb, b_par[:, 1, :], ALU.mult))
                dve.tensor_tensor(bb[:, :, c, :], blocks(w0), blocks(w1), op).then_inc(bb_ready, 1)
                dve.wait_ge(bb_ready, c + 1)

        def bb_low():
            dve.wait_ge(const_loaded, 64)
            for g in range(2):
                dve.wait_ge(bb_hi_ready, g + 1)
                dve.scalar_tensor_tensor(bb_lo[:, :, :, g, :], bb[:, :, :, :], mask2[:, g:g + 1],
                                         bb_hi[:, :, :, g, :].bitcast(F32), ALU.mult, ALU.subtract)\
                   .then_inc(bb_lo_ready, 1)

        for h in range(2 * NB):
            split(h + 1, (h + 1) % 4)
            if h >= 2 and h % 4 >= 2:
                s, n = h % 2, h // 4 * 2 + h % 2
                dve.wait_ge(u_hi_ready, n + 1)
                if n >= 2:
                    dve.wait_ge(u_stored[s], U_STORES * (n // 2))
                dve.tensor_tensor(u_lo[s][:, :], u_stage[s][:, :], u_hi[s][:, :].bitcast(F32), ALU.subtract)\
                   .then_inc(u_lo_ready, 1)
            if h < 2:
                for k in range(4):
                    x_low(KH + 4 * h + k)
            if h == 2:
                dve.wait_ge(par_loaded, 48)
                n = PAIRS + NB
                exp_reduce(log_dt[:, :], n)
                exp_series(n)
                exp_scale(log_dt[:, :], n)
                spread_dt()
            if h == 3:
                angles()
            if h == 4:
                link(dve.tensor_tensor(s_dt[:, :], A_RE, s_dt[:, :], ALU.mult))
                exp_reduce(s_dt[:, :], SETUP)
            if h == 5:
                exp_series(SETUP)
            if h == 6:
                exp_scale(s_mag[:, :], SETUP)
            if h == 7:
                phase_and_lam()
            if h == 8:
                zoh_lam()
            if h == 9:
                zoh_abs()
            if h == 10:
                zoh_q(q_re, w0, w1, ALU.add)
            if h == 11:
                zoh_q(q_im, w1, w0, ALU.subtract)
            if h == 12:
                zoh_b()
            if h == 13:
                bb_low()
        dve.memset(ones[:, :], 1.0).then_inc(ones_ready, 1)

        q_prompt = q_pad[:, 0:SEQ + 2]
        q_sample = q_pad[:, SEQ + 2:QPAD].rearrange("p (b t) -> p b t", b=DEC_B)

        def spread(t, n):
            return t.unsqueeze(1).to_broadcast([P, 2, n])

        def to_frame(p, j):
            dve.wait_ge(table_ready, p * 2 + 2)
            dve.wait_ge(bu_evac, p * 2 + 3)
            dve.wait_ge(h_ready, p * 2 + 3)
            s = j % 2
            dve.tensor_tensor(m1[:, :, :], bu[s][:, :, :], spread(table[s][:, 0, :], TOK), ALU.mult)\
               .then_inc(prod1_ready, 1)
            dve.tensor_tensor(m2[:, :, :], bu[s][:, :, :], spread(table[s][:, 1, :], TOK), ALU.mult)\
               .then_inc(prod1_ready, 1)

        def scans(p, j):
            s = j % 2
            first = bu[s][:, :, SEQ:TOK:DEC_T]
            h0 = host_blk[:, C0 + j * 2 * DEC_B:C0 + (j + 1) * 2 * DEC_B].rearrange("p (c b) -> p c b", c=2)
            dve.wait_ge(v_ready, p * 2 + 2)
            link(dve.scalar_tensor_tensor(first, h0, mag_blk[:, j:j + 1], first,
                                          ALU.mult, ALU.add))
            dve.wait_ge(rmask_ready, p + 1)
            for c in range(2):
                ins = dve.tensor_tensor_scan(m1[:, c, :], rmask[s][:, :], bu[s][:, c, :], 0.0,
                                             ALU.mult, ALU.add)
                mark(ins)
            dve.wait_ge(dve_step, own.value())
            dve.tensor_tensor(bu[s][:, :, :], m1[:, :, :], spread(table[s][:, 0, :], TOK), ALU.mult)\
               .then_inc(prod2_ready, 1)
            ins = dve.tensor_tensor(m2[:, :, :], m1[:, :, :], spread(table[s][:, 1, :], TOK), ALU.mult)
            ins.then_inc(prod2_ready, 1)
            dve.wait_ge(prod2_ready, p * 2 + 2)
            dve.sem_inc(table_free, 1)
            dve.wait_ge(h_used, p + 1)
            dve.wait_ge(h_kept, p + 1)
            dve.tensor_tensor(hst[s][:, 0, :], bu[s][:, 0, :], m2[:, 1, :], ALU.subtract).then_inc(h_ready, 1)
            dve.tensor_tensor(hst[s][:, 1, :], bu[s][:, 1, :], m2[:, 0, :], ALU.add).then_inc(h_ready, 1)

        def new_block(b, loaded):
            dve.wait_ge(blk_loaded, loaded)
            dve.tensor_copy(mag_blk[:, :], mag_all[:, bass.ds(b * 4, 4)]).then_inc(mag_ready, 1)

        def negate_c():
            v = host_blk[:, 0:C0].rearrange("p (j c n) -> p j c n", j=4, c=2)[:, :, 1, :]
            return dve.tensor_scalar(v, v, -1.0, None, ALU.mult)

        def read_y(b):
            dve.wait_ge(h_used, b * 4 + 6)
            dve.wait_ge(y_stored, b * 32 + 32)
            for q in range(2):
                own.mark(dve.scalar_tensor_tensor(y_pre[:, q * TH:(q + 1) * TH], u_blk[:, q * TH:(q + 1) * TH],
                                                  host_blk[:, C0 + H0 + q:C0 + H0 + q + 1],
                                                  y_ps[:, q, 0:TH], ALU.mult, ALU.add))
            dve.wait_ge(dve_step, own.value())
            dve.sem_inc(y_read, 1)

        def gelu(b):
            link(dve.scalar_tensor_tensor(y_tmp[:, :], y_pre[:, :], GELU_C, y_pre[:, :], ALU.mult, ALU.mult))
            dve.scalar_tensor_tensor(y_tmp[:, :], y_tmp[:, :], 1.0, y_pre[:, :], ALU.add, ALU.mult)\
               .then_inc(y_arg, 1)
            dve.wait_ge(y_sig, b + 1)
            dve.tensor_tensor(y_pre[:, :], y_pre[:, :], y_tmp[:, :], ALU.mult).then_inc(y_made, 1)

        def free(par):
            dve.sem_inc(acc_free[par], 1)

        def conv_h(b, q, h):
            dve.wait_ge(conv_last, b * 4 + 2 * q + 2)
            cb = b * 2 + q
            link(dve.tensor_copy(cw[:, :], conv_par[:, cb, 0:3]))
            link(dve.tensor_copy(q_sample[:, :, 0:2],
                                 conv_par[:, cb, 3:3 + 2 * DEC_B].rearrange("p (s t) -> p s t", t=2)))
            dve.wait_ge(cc_ready, b * 2 + (q + 1))
            dve.wait_ge(half_done, h + 1)
            own.mark(dve.tensor_tensor(q_prompt[:, 2:2 + TH], conv_c[:, 0:TH], acc[:, 1, 0, 0:TH], ALU.mult))
            own.mark(dve.tensor_tensor(q_prompt[:, 2 + TH:2 + SEQ], conv_c[:, TH:SEQ],
                                       acc[:, 1, 1, 0:SEQ - TH], ALU.mult))
            own.mark(dve.tensor_tensor(q_sample[:, :, 2:], conv_c[:, SEQ:].rearrange("p (s t) -> p s t", s=DEC_B),
                                       acc[:, 1, 1, SEQ - TH:TH].rearrange("p (s t) -> p s t", s=DEC_B),
                                       ALU.mult))
            dve.wait_ge(dve_step, own.value())
            dve.sem_inc(q_read, 1)
            free(1)

        def conv_taps():
            c_s = conv_t[:, SEQ:].rearrange("p (s t) -> p s t", s=DEC_B)
            for k in range(3):
                pr, sa = q_prompt[:, k:k + SEQ], q_sample[:, :, k:k + DEC_T]
                w = cw[:, k:k + 1]
                if k == 0:
                    own.mark(dve.tensor_scalar(conv_t[:, 0:SEQ], pr, w, None, ALU.mult))
                    link(dve.tensor_scalar(c_s, sa, w, None, ALU.mult))
                else:
                    own.mark(dve.scalar_tensor_tensor(conv_t[:, 0:SEQ], pr, w, conv_t[:, 0:SEQ],
                                                      ALU.mult, ALU.add))
                    link(dve.scalar_tensor_tensor(c_s, sa, w, c_s, ALU.mult, ALU.add))

        def conv_b(h):
            dve.wait_ge(half_done, h + 1)
            link(dve.tensor_tensor(two(conv_t[:, :]), two(conv_t[:, :]), halves_of(acc[:, 0]), ALU.mult))
            free(0)

        def conv_z(b, q, h):
            dve.wait_ge(half_done, h + 1)
            dve.wait_ge(z_sig, b * 2 + (q + 1))
            link(dve.tensor_tensor(two(gate_t[:, :]), two(gate_t[:, :]), halves_of(acc[:, 1]), ALU.mult))
            free(1)
            dve.tensor_tensor(conv_t[:, :], conv_t[:, :], gate_t[:, :], ALU.mult).then_inc(yc_ready, 1)

        def conv_low(b, q):
            dve.wait_ge(gh_ready, b * 2 + (q + 1))
            hi = gated_h[:, b * 2 + q, :]
            lo = gated_l[:, b * 2 + q, :]
            dve.tensor_tensor(lo, conv_t[:, :], hi.bitcast(F32), ALU.subtract).then_inc(gl_ready, 1)

        STEPS_CONV = own.value()

        def conv_body(b):
            for l in range(16):
                split_next(b, 16, H_CONV, l)
                if l == 1:
                    new_block(b, b * 48 + 48)
                    link(dve.memset(q_pad[:, 0:2], 0.0))
                    negate_c().then_inc(c_ready, 1)
                if l - 1 in CONV_BU:
                    j = CONV_BU.index(l - 1)
                    scans(b * 4 + j, j)
                if l == 8:
                    conv_low(b, 0)
                if l in CONV_BU:
                    j = CONV_BU.index(l)
                    to_frame(b * 4 + j, j)
                h = b * 16 + (H_CONV + l)
                if l == CONV_C[1]:
                    read_y(b)
                    gelu(b)
                if l % 8 == 3:
                    conv_h(b, l // 8, h)
                if l in CONV_TAPS:
                    conv_taps()
                if l % 8 == 5:
                    conv_b(h)
                if l % 8 == 7:
                    conv_z(b, l // 8, h)
                if l == 15:
                    conv_low(b, 1)

        CONV_STEPS = 42
        with dve.Fori(0, 4) as b:
            own.at(b * CONV_STEPS + STEPS_CONV)
            conv_body(b)
            assert own.k == CONV_STEPS, own.k
        STEPS_OUTC = STEPS_CONV + 4 * CONV_STEPS

        OUTC_STEPS = 15
        with dve.Fori(0, 4) as i:
            own.at(i * OUTC_STEPS + STEPS_OUTC)
            for l in range(12):
                m = l // 3
                split_next(i, 12, H_OUTC, l)
                if l == 1:
                    new_block(i + 4, i * 48 + 48 * 5)
                    negate_c().then_inc(c_ready, 1)
                if l - 1 in OUTC_BU:
                    j = OUTC_BU.index(l - 1)
                    scans(i * 4 + (16 + j), j)
                if l in OUTC_BU:
                    j = OUTC_BU.index(l)
                    to_frame(i * 4 + (16 + j), j)
                if l == OUTC_C[1]:
                    read_y(i + 4)
                    gelu(i + 4)
                if l % 3 == 2:
                    dve.wait_ge(half_done, i * 12 + (H_OUTC + l + 1))
                    dve.wait_ge(g_sig, i * 4 + (m + 1))
                    dve.wait_ge(part_stored[m % 2], i * 32 + 16 * (m // 2 + 1))
                    dve.tensor_tensor(two(part_st[m % 2][:, :]), two(gate_t[:, :]), halves_of(acc[:, 1]),
                                      ALU.mult).then_inc(part_made, 1)
                    dve.wait_ge(part_made, i * 4 + (m + 1))
                    free(1)
            assert own.k == OUTC_STEPS, own.k
        own.at(STEPS_OUTC + 4 * OUTC_STEPS)

        for i in range(2):
            for l in range(12):
                split_next(i, 12, H_GLU, l)
                if i == 0 and l < NB:
                    dve.wait_ge(yh_ready, l + 1)
                    dve.tensor_tensor(yl[:, l, :], y_in[l % 2][:, :], yh[:, l, :].bitcast(F32), ALU.subtract)\
                       .then_inc(yl_ready, 1)
                if l < 8 and l % 2:
                    n = l // 2
                    dve.wait_ge(za_sig, i * 4 + (n + 1))
                    link(dve.tensor_tensor(two(silu_z[n][:, :]), two(silu_z[n][:, :]),
                                           halves_of(acc[:, n % 2]), ALU.mult))
                    free(n % 2)
                if l >= 8:
                    n = l - 8
                    if l == 8:
                        dve.wait_ge(yl_ready, NB)
                    if i or n:
                        dve.wait_ge(gl_ready, i * 4 + NB + n)
                    yv, lv = (y[:, i * 4 + n, :].bitcast(F32) for y in (yh, yl))
                    link(dve.tensor_tensor(y_f[:, :], yv, lv, ALU.add))
                    link(dve.tensor_tensor(y_f[:, :], y_f[:, :], silu_z[n][:, :], ALU.mult))
                    dve.wait_ge(glu_sig, i * 4 + (n + 1))
                    dve.tensor_tensor(y_f[:, :], y_f[:, :], sig_a[:, :], ALU.mult).then_inc(ya_ready, 1)
                    dve.wait_ge(gh_ready, i * 4 + (NB + n + 1))
                    hi = gated_h[:, i * 4 + n, :].bitcast(F32)
                    dve.tensor_tensor(gated_l[:, i * 4 + n, :], y_f[:, :], hi, ALU.subtract).then_inc(gl_ready, 1)
        STEPS_OUTA = own.value()

        def merged_low(k):
            dve.wait_ge(xh_ready, KX + k + 1)
            dve.tensor_tensor(xl[:, k, :], merged[:, k, :], xh[:, k, :].bitcast(F32), ALU.subtract)\
               .then_inc(xl_ready, 1)

        def phase_outa(i, last):
            for l in range(12):
                m = l // 3
                split_next(i, 12, H_OUTA, l)
                if last and l == 11:
                    for k in range(4):
                        merged_low(k)
                if l % 3 == 2:
                    dve.wait_ge(half_done, i * 12 + (H_OUTA + l + 1))
                    dve.wait_ge(ga_sig, i * 4 + (m + 1))
                    own.at(i * 4 + (STEPS_OUTA + m))
                    link(dve.tensor_tensor(two(sig_m[:, :]), two(sig_m[:, :]), halves_of(acc[:, 1]), ALU.mult))
                    free(1)
                    dve.wait_ge(part_loaded[m % 2], i * 32 + 16 * (m // 2 + 1))
                    dve.tensor_tensor(merged[:, i * 4 + m, :], sig_m[:, :], part_in[m % 2][:, :], ALU.add)\
                       .then_inc(merged_ready, 1)
        with dve.Fori(0, 3) as i:
            phase_outa(i, False)
        phase_outa(3, True)
        for k in (4, 5):
            merged_low(k)
        STEPS_O = STEPS_OUTA + KX
        own.at(STEPS_O)

        def take_r(i, s):
            n = i * 2 + s
            dve.wait_ge(half_done, i * 4 + (H_O + s + 3))
            dve.wait_ge(xin_loaded[s], i * 16 + 16)
            dve.scalar_tensor_tensor(two(r_all[:, n, :]), two(x_in[s][:, :]), ALPHA, halves_of(acc[:, s]),
                                     ALU.mult, ALU.add).then_inc(r_ready, 1)
            dve.wait_ge(r_ready, n + 1)
            free(s)

        def take_d(i, s, first=False, last=False):
            n = i * 2 + s
            out = r_all[:, n, :]
            dve.tensor_tensor(out, out, pivot[:, :], ALU.subtract).then_inc(d_ready, 1)
            dve.wait_ge(d_ready, n + 1)
            if first:
                link(dve.tensor_copy(acc_d[:, :], out))
            else:
                link(dve.tensor_tensor(acc_d[:, :], acc_d[:, :], out, ALU.add))
            if last:
                dve.sem_inc(sums_ready, 1)
            dve.wait_ge(sq_ready, n + 1)
            if first:
                link(dve.tensor_copy(acc_q[:, :], sq[s][:, :]))
            else:
                link(dve.tensor_tensor(acc_q[:, :], acc_q[:, :], sq[s][:, :], ALU.add))

        def phase_o(i, head, last):
            for l in range(4):
                if not (last and l == 3):
                    split_next(i, 4, H_O, l)
                if head and l < 3:
                    for k in range(6 + 4 * l, min(10 + 4 * l, KX)):
                        merged_low(k)
                if head and l == 3:
                    dve.wait_ge(pivot_ready, 1)
                    take_d(0, 0, True)
                if l >= 2:
                    take_r(i, l - 2)
                    if not (head and l == 2):
                        take_d(i, l - 2, last=last and l == 3)
        phase_o(0, True, False)
        assert own.k == 4
        with dve.Fori(1, KX // 2 - 1) as i:
            own.at(i * 4 + STEPS_O)
            phase_o(i, False, False)
            assert own.k == 4
        own.at((KX // 2 - 1) * 4 + STEPS_O)
        phase_o(KX // 2 - 1, False, True)
        dve.sem_inc(sums_ready, 1)

        dve.wait_ge(sums_done, 2)
        link(dve.tensor_scalar(two(rstd[:, :]), halves_of(y_ps), 1.0 / D_MODEL, LN_EPS, ALU.mult, ALU.add))
        dve.wait_ge(mean_ready, 1)
        link(dve.tensor_tensor(mean_r[:, :], mean[:, :], mean[:, :], ALU.mult))
        dve.tensor_tensor(rstd[:, :], rstd[:, :], mean_r[:, :], ALU.subtract).then_inc(var_ready, 1)
        dve.wait_ge(std_ready, 1)
        link(dve.reciprocal(rstd[:, :], rstd[:, :]))
        dve.tensor_tensor(mean_r[:, :], mean[:, :], rstd[:, :], ALU.mult).then_inc(rstd_ready, 1)
        dve.wait_ge(rstd_ready, 1)
        for n in DVE_BLOCKS:
            link(dve.tensor_tensor(r_all[:, n, :], r_all[:, n, :], rstd[:, :], ALU.mult))
            dve.tensor_tensor(r_all[:, n, :], r_all[:, n, :], mean_r[:, :], ALU.subtract).then_inc(norm_dve, 1)

    @blk.gpsimd
    def _(pool):
        pool.sem_inc(h_ready, 3)
        pool.sem_inc(h_used, 2)

        def make_table(p, s):
            pool.wait_ge(table_free, p + 1)
            at = p * ROT_P
            f = lambda c: rot_all[:, bass.ds(at + c * FINE, FINE)].unsqueeze(1).to_broadcast([P, COARSE, FINE])
            g = lambda c: rot_all[:, bass.ds(at + (2 * FINE + c * COARSE), COARSE)]\
                .unsqueeze(2).to_broadcast([P, COARSE, FINE])
            grid = lambda x: x.rearrange("p (a b) -> p a b", b=FINE)
            for c, (ga, gb) in enumerate(((0, 1), (1, 0))):
                pool_step.mark(pool.tensor_tensor(grid(table[s][:, c, 0:SEQ]), g(ga), f(0), ALU.mult))
                pool_step.mark(pool.tensor_tensor(grid(t_tmp[:, c, :]), g(gb), f(1), ALU.mult))
                sample = rot_all[:, bass.ds(at + c * FINE, DEC_T)].unsqueeze(1).to_broadcast([P, DEC_B, DEC_T])
                pool_step.mark(pool.tensor_copy(
                    table[s][:, c, SEQ:].rearrange("p (b t) -> p b t", b=DEC_B), sample))
            pool.wait_ge(pool_step.sem, pool_step.value())
            for c, op in enumerate((ALU.subtract, ALU.add)):
                out = table[s][:, c, 0:SEQ]
                pool.tensor_tensor(out, out, t_tmp[:, c, :], op).then_inc(table_ready, 1)

        pool_step = Steps(sem("pool_step"))

        def step(ins):
            pool_step.mark(ins)
            pool.wait_ge(pool_step.sem, pool_step.value())

        def tmp(t, n):
            return t[:, 0:PAIRS * n].rearrange("p (b j n) -> p b j n", j=4, n=n)

        def turn(out, a, by, n):
            e = lambda x: x.to_broadcast([P, NB, 4, n])
            step(pool.tensor_tensor(tmp(turn_t[0], n), a[0], e(by[0]), ALU.mult))
            step(pool.tensor_tensor(tmp(turn_t[1], n), a[1], e(by[1]), ALU.mult))
            step(pool.tensor_tensor(tmp(s_x, n), a[0], e(by[1]), ALU.mult))
            step(pool.tensor_tensor(tmp(s_k, n), a[1], e(by[0]), ALU.mult))
            step(pool.tensor_tensor(out[0], tmp(turn_t[0], n), tmp(turn_t[1], n), ALU.subtract))
            step(pool.tensor_tensor(out[1], tmp(s_x, n), tmp(s_k, n), ALU.add))

        def fine_table(n):
            turn([fine(c, n, 2 * n) for c in (0, 1)], [fine(c, 0, n) for c in (0, 1)],
                 [fine(c, n - 1, n) for c in (0, 1)], n)

        def coarse_start():
            step(pool.memset(coarse(0, 0, 1), 1.0))
            step(pool.memset(coarse(1, 0, 1), 0.0))
            for c in range(2):
                step(pool.tensor_copy(coarse(c, 1, 2), fine(c, FINE - 1, FINE)))

        def coarse_table(n):
            turn([coarse(c, n, n + 1) for c in (0, 1)], [coarse(c, n - 1, n) for c in (0, 1)],
                 [coarse(c, 1, 2) for c in (0, 1)], 1)
            turn([coarse(c, n + 1, 2 * n) for c in (0, 1)], [coarse(c, 1, n) for c in (0, 1)],
                 [coarse(c, n, n + 1) for c in (0, 1)], n - 1)

        def add_frame(p, j):
            s = j % 2
            pool.wait_ge(prod1_ready, p * 2 + 2)
            pool.tensor_tensor(bu[s][:, 0, :], m1[:, 0, :], m2[:, 1, :], ALU.add).then_inc(v_ready, 1)
            pool.tensor_tensor(bu[s][:, 1, :], m1[:, 1, :], m2[:, 0, :], ALU.subtract).then_inc(v_ready, 1)

        def block(p0, k0, last):
            pool_step.at(k0)
            for j in range(4):
                add_frame(p0 + j, j)
                if j < 3:
                    make_table(p0 + (j + 1), (j + 1) % 2)
            if not last:
                make_table(p0 + 4, 0)
        pool.wait_ge(phase_ready, 1)
        for n in (1, 2, 4, 8):
            fine_table(n)
        coarse_start()
        for n in (2, 3):
            turn([coarse(c, n, n + 1) for c in (0, 1)], [coarse(c, n - 1, n) for c in (0, 1)],
                 [coarse(c, 1, 2) for c in (0, 1)], 1)
        for n in (4, 8, 16):
            coarse_table(n)
        make_table(0, 0)
        per = 6 * 4
        tables_start = pool_step.value()
        with pool.Fori(0, NB - 1) as b:
            block(b * 4, b * per + tables_start, False)
            assert pool_step.k == per
        block((NB - 1) * 4, (NB - 1) * per + tables_start, True)

        pool.wait_ge(rstd_ready, 1)
        pool_step.at((NB - 1) * per + tables_start + 18)
        for n in POOL_BLOCKS:
            pool_step.mark(pool.tensor_tensor(r_all[:, n, :], r_all[:, n, :], rstd[:, :], ALU.mult))
            pool.wait_ge(pool_step.sem, pool_step.value())
            pool.tensor_tensor(r_all[:, n, :], r_all[:, n, :], mean_r[:, :], ALU.subtract).then_inc(norm_pool, 1)

    block.__exit__(None, None, None)


def kernel(x_prompt, x_sample, state_ssm_re, state_ssm_im, state_conv, w_in, ssm_a_re, ssm_a_im,
           ssm_log_dt, ssm_b_re, ssm_b_im, ssm_c_re, ssm_c_im, ssm_d, w_glu, w_out_a, conv_w, w_out_c,
           w_o, ln_g, ln_b):
    import concourse.bacc as bacc
    from concourse.bass_utils import run_bass_kernel_spmd

    f = lambda a: np.asarray(a)
    tokens = np.concatenate([f(x_prompt)[0], f(x_sample).reshape(DEC_B * DEC_T, D_MODEL)], 0)
    xT = np.ascontiguousarray(tokens.T).reshape(KX, P, TOK)

    def halves(w):
        k, n = w.shape
        v = w.reshape(k // (KH * P), KH, P, n // P, P).transpose(3, 0, 2, 1, 4)
        return v.reshape(n // P, k // (KH * P), P, KH * P)
    wi = halves(f(w_in)[0])
    bounds = np.cumsum([0, NB, NB, NB, NB, NB, NB, KX, KX])
    u_w, z_a, b_c, c_c, h_c, z_c, g_a, g_c = (wi[bounds[i]:bounds[i + 1]] for i in range(8))
    glu, out_a, out_c, w_out = (halves(f(w)[0]) for w in (w_glu, w_out_a, w_out_c, w_o))
    def side_by_side(v):
        return [v[n + o][k:k + 1] for n in range(0, len(v), 2) for k in range(2) for o in range(2)]
    order = side_by_side(u_w)
    for n in range(NB):
        order += [c_c[n], h_c[n], b_c[n], z_c[n]]
    for n in range(KX):
        order += [g_c[n], out_c[n]]
    for n in range(0, NB, 4):
        order += [*z_a[n:n + 4], *glu[n:n + 4]]
    for n in range(KX):
        order += [g_a[n], out_a[n]]
    order += side_by_side(w_out)
    w = np.concatenate(order, 0)

    def two_layouts(a):
        states = a.reshape(PAIRS, 2 * STATE).T
        channels = np.broadcast_to(a.reshape(NB, 8, 1, STATE), (NB, 8, GC, STATE))
        channels = channels.transpose(1, 2, 0, 3).reshape(P, NB * STATE)
        return np.concatenate([states, channels], 1)
    a_par = np.stack([two_layouts(f(a)[0]) for a in (ssm_a_re, ssm_a_im)], 1)
    log_dt = f(ssm_log_dt)[0]
    log_dt = np.concatenate([np.repeat(log_dt.reshape(PAIRS, 2), STATE, 1).T,
                             np.repeat(log_dt.reshape(NB, 8), GC, 1).T], 1)

    def channel_rows(a):
        return a.reshape(NB, 8, STATE, GC).transpose(1, 3, 0, 2).reshape(P, NB * STATE)
    b_par = np.stack([channel_rows(f(ssm_b_re)[0]), channel_rows(f(ssm_b_im)[0])], 1)

    host_blk = np.zeros((NB, P, HOST_W), np.float32)
    cv = np.zeros((NB, 2, STATE, 4, 2, 2, GC), np.float32)
    for part, src in enumerate((ssm_c_re, ssm_c_im)):
        s = f(src)[0].reshape(NB, 4, 2, GC, STATE)
        for g in range(2):
            cv[:, g, :, :, part, g, :] = s[:, :, g].transpose(0, 3, 1, 2)
    host_blk[:, :, 0:C0] = cv.reshape(NB, P, C0)
    h0 = np.stack([f(state_ssm_re)[0], f(state_ssm_im)[0]], 0)
    h0 = h0.reshape(2, DEC_B, NB, 4, 2, STATE).transpose(2, 4, 5, 3, 0, 1)
    host_blk[:, :, C0:C0 + H0] = h0.reshape(NB, P, H0)
    d_y = np.tile(f(ssm_d)[0].reshape(NB, 2, P // 2), (1, 1, 2))
    host_blk[:, :, C0 + H0:] = d_y.transpose(0, 2, 1)

    conv_par = np.concatenate([
        f(conv_w)[0].reshape(3, NB, P).transpose(2, 1, 0),
        f(state_conv)[0].reshape(DEC_B, 2, NB, P).transpose(3, 2, 0, 1).reshape(P, NB, 2 * DEC_B)], 2)
    ln_par = np.stack([f(ln_g)[0].reshape(KX, P).T, f(ln_b)[0].reshape(KX, P).T], 2)
    mask2 = (np.arange(P)[:, None] // GC % 2 == np.arange(2)[None]).astype(np.float32)
    starts = np.ones(TOK, np.float32)
    starts[0] = 0
    starts[SEQ::DEC_T] = 0
    scan_mask = np.broadcast_to(starts, (P, TOK))

    arrays = {"w": w, "xT": xT, "a_par": a_par, "log_dt": log_dt, "b_par": b_par, "host_blk": host_blk,
              "conv_par": conv_par, "ln_par": ln_par, "mask2": mask2, "scan_mask": scan_mask}
    nc = bacc.Bacc("TRN2", target_bir_lowering=False, num_devices=1, dynamic_dma_scratch_size=1024)
    d, feed = {}, {}
    for name, a in arrays.items():
        a = np.ascontiguousarray(a)
        feed[f"in_{name}"] = a
        d[name] = nc.dram_tensor(f"in_{name}", a.shape, F32, kind="ExternalInput").ap()
    for name, shape in (("outT", [KX, P, TOK]), ("out_state", [P, PAIRS, 2, SCAN_ENDS]),
                        ("out_conv", [P, NB, SCAN_ENDS, 2])):
        d[name] = nc.dram_tensor(name, shape, F32, kind="ExternalOutput").ap()
    build(nc, d)
    res = run_bass_kernel_spmd(nc, [feed], core_ids=[0]).results[0]

    y = np.asarray(res["outT"]).reshape(D_MODEL, TOK).T
    st = np.asarray(res["out_state"]).reshape(2, STATE, PAIRS, 2, SCAN_ENDS)
    st = st.transpose(3, 4, 2, 0, 1).reshape(2, SCAN_ENDS, 2 * PAIRS, STATE)
    cv = np.asarray(res["out_conv"]).transpose(2, 3, 1, 0).reshape(SCAN_ENDS, 2, D_CONV)
    c = np.ascontiguousarray
    return (c(y[:SEQ])[None], c(y[SEQ:]).reshape(DEC_B, DEC_T, D_MODEL),
            c(st[0, :1])[None], c(st[1, :1])[None], c(cv[:1])[None],
            c(st[0, 1:])[None], c(st[1, 1:])[None], c(cv[1:])[None])
```
